# Optimizing a Trainium2 kernel written in Bass

```python
import math
import jax, jax.numpy as jnp
from jax import lax
import numpy as np

D_MODEL = 1024
BATCH = 1
SEQ = 256
DEPTH = 1

D_MIX = D_MODEL
HEAD_DIM = 64
SB_HEADS = 8
SB_WIDTH = SB_HEADS * HEAD_DIM
SG_HEADS = 8
SG_WIDTH = SG_HEADS * HEAD_DIM
D_IN = 3 * SB_WIDTH + 2 * SG_WIDTH
CHUNK = 128
Q_BLOCK = 128
N_GROUPS = 4
EXPERTS_PER_GROUP = 8
TOP_K = 2
D_EXPERT = 512
EPS = 1e-6


def rmsnorm(x, g):
    xf = x.astype(jnp.float32)
    y = xf * lax.rsqrt(jnp.mean(xf * xf, axis=-1, keepdims=True) + EPS)
    return (y * g.astype(jnp.float32)).astype(x.dtype)

def stick_breaking_attention(q, k, v):
    B, S, H, Dh = q.shape
    nb = S // Q_BLOCK
    scale = 1.0 / math.sqrt(Dh)
    k = k.transpose(0, 2, 1, 3)
    v = v.transpose(0, 2, 1, 3)
    q_blocks = q.transpose(0, 2, 1, 3).reshape(B, H, nb, Q_BLOCK, Dh).transpose(2, 0, 1, 3, 4)
    key_pos = jnp.arange(S)

    def one_block(args):
        qb, blk = args
        z = jnp.einsum('bhqd,bhkd->bhqk', qb, k).astype(jnp.float32) * scale
        q_pos = blk * Q_BLOCK + jnp.arange(Q_BLOCK)
        mask = key_pos[None, :] < q_pos[:, None]
        log_beta = jax.nn.log_sigmoid(z)
        log_1m_beta = jnp.where(mask, jax.nn.log_sigmoid(-z), 0.0)
        after = lax.cumsum(log_1m_beta, axis=log_1m_beta.ndim - 1, reverse=True) - log_1m_beta
        a = jnp.where(mask, jnp.exp(log_beta + after), 0.0)
        return jnp.einsum('bhqk,bhkd->bhqd', a.astype(v.dtype), v)

    out = lax.map(one_block, (q_blocks, jnp.arange(nb)))
    return out.transpose(1, 0, 3, 2, 4).reshape(B, S, H * Dh)

def chunked_spatial_gating(u, vg, sg_norm_g, w_spatial, b_spatial):
    B, S, _ = u.shape
    nc = S // CHUNK
    u = jax.nn.gelu(u)
    vg = rmsnorm(jax.nn.gelu(vg), sg_norm_g)
    vg = vg.reshape(B, nc, CHUNK, SG_HEADS, HEAD_DIM)
    causal = jnp.tril(jnp.ones((CHUNK, CHUNK), dtype=w_spatial.dtype))
    w_masked = w_spatial * causal[None]
    mixed = jnp.einsum('hts,bcshd->bcthd', w_masked, vg) + b_spatial.T[None, None, :, :, None]
    return u * mixed.reshape(B, S, SG_WIDTH)

def hierarchical_moe(x, w_router_group, b_router_group, w_router_expert, b_router_expert,
                     w_gate, w_up, w_down):
    B, S, D = x.shape
    xt = x.reshape(-1, D)
    n = xt.shape[0]
    g_logits = (xt @ w_router_group).astype(jnp.float32) + b_router_group.astype(jnp.float32)
    g_probs = jax.nn.softmax(g_logits, axis=-1)
    g_idx = jnp.argmax(g_logits, axis=-1)
    g_onehot = jax.nn.one_hot(g_idx, N_GROUPS, dtype=jnp.float32)
    g_weight = jnp.sum(g_probs * g_onehot, axis=-1)
    e_logits_all = jnp.einsum('nd,gde->nge', xt, w_router_expert).astype(jnp.float32) \
        + b_router_expert.astype(jnp.float32)[None]
    e_logits = jnp.sum(e_logits_all * g_onehot[:, :, None], axis=1)
    e_probs = jax.nn.softmax(e_logits, axis=-1)
    top_p, top_i = lax.top_k(e_probs, TOP_K)
    top_p = top_p / jnp.sum(top_p, axis=-1, keepdims=True)
    e_w = jnp.sum(jax.nn.one_hot(top_i, EXPERTS_PER_GROUP, dtype=jnp.float32) * top_p[..., None], axis=1)
    combine = (g_onehot[:, :, None] * (g_weight[:, None] * e_w)[:, None, :]).astype(x.dtype)
    out = jnp.zeros((n, D), dtype=x.dtype)
    for g in range(N_GROUPS):
        h = jax.nn.silu(jnp.einsum('nd,edf->nef', xt, w_gate[g])) * jnp.einsum('nd,edf->nef', xt, w_up[g])
        out = out + jnp.einsum('nef,efd->nd', h * combine[:, g, :, None], w_down[g])
    return out.reshape(B, S, D)

def first_inputs(seed: int = 0) -> dict:
    key = jax.random.key(seed)
    ks = jax.random.split(key, 20)
    f32 = jnp.float32
    nrm = lambda k, shape, s: jax.random.normal(k, shape, f32) * s
    gain = lambda k, shape: 1.0 + 0.02 * jax.random.normal(k, shape, f32)
    L, G, E = DEPTH, N_GROUPS, EXPERTS_PER_GROUP
    return {
        "x": jax.random.normal(ks[0], (BATCH, SEQ, D_MODEL), f32),
        "attn_norm_g": gain(ks[1], (L, D_MODEL)),
        "w_in": nrm(ks[2], (L, D_MODEL, D_IN), D_MODEL ** -0.5),
        "sg_norm_g": gain(ks[3], (L, SG_WIDTH)),
        "w_spatial": nrm(ks[4], (L, SG_HEADS, CHUNK, CHUNK), CHUNK ** -0.5),
        "b_spatial": gain(ks[5], (L, SG_HEADS, CHUNK)),
        "sb_out_norm_g": gain(ks[6], (L, SB_WIDTH)),
        "sg_out_norm_g": gain(ks[7], (L, SG_WIDTH)),
        "w_out": nrm(ks[8], (L, D_MIX, D_MODEL), D_MIX ** -0.5),
        "ffn_norm_g": gain(ks[9], (L, D_MODEL)),
        "w_router_group": nrm(ks[10], (L, D_MODEL, G), D_MODEL ** -0.5),
        "b_router_group": nrm(ks[11], (L, G), 0.01),
        "w_router_expert": nrm(ks[12], (L, G, D_MODEL, E), D_MODEL ** -0.5),
        "b_router_expert": nrm(ks[13], (L, G, E), 0.01),
        "w_gate": nrm(ks[14], (L, G, E, D_MODEL, D_EXPERT), D_MODEL ** -0.5),
        "w_up": nrm(ks[15], (L, G, E, D_MODEL, D_EXPERT), D_MODEL ** -0.5),
        "w_down": nrm(ks[16], (L, G, E, D_EXPERT, D_MODEL), D_EXPERT ** -0.5),
        "final_norm_g": gain(ks[17], (D_MODEL,)),
    }

def first_block(x, attn_norm_g, w_in, sg_norm_g, w_spatial, b_spatial, sb_out_norm_g, sg_out_norm_g,
              w_out, ffn_norm_g, w_router_group, b_router_group, w_router_expert, b_router_expert,
              w_gate, w_up, w_down, final_norm_g):
    B, S, _ = x.shape
    h = x
    for layer in range(DEPTH):
        hn = rmsnorm(h, attn_norm_g[layer])
        proj = hn @ w_in[layer]
        q, k, v, u, vg = jnp.split(proj, [SB_WIDTH, 2 * SB_WIDTH, 3 * SB_WIDTH, 3 * SB_WIDTH + SG_WIDTH], axis=-1)
        shp = (B, S, SB_HEADS, HEAD_DIM)
        sb_out = stick_breaking_attention(q.reshape(shp), k.reshape(shp), v.reshape(shp))
        sg_out = chunked_spatial_gating(u, vg, sg_norm_g[layer], w_spatial[layer], b_spatial[layer])
        mixed = jnp.concatenate([rmsnorm(sb_out, sb_out_norm_g[layer]),
                                 rmsnorm(sg_out, sg_out_norm_g[layer])], axis=-1)
        h = h + mixed @ w_out[layer]
        hn = rmsnorm(h, ffn_norm_g[layer])
        h = h + hierarchical_moe(hn, w_router_group[layer], b_router_group[layer],
                                 w_router_expert[layer], b_router_expert[layer],
                                 w_gate[layer], w_up[layer], w_down[layer])
    return rmsnorm(h, final_norm_g)


DA_HEADS = 4
DA_DIM = 64
NSA_HEADS = 8
NSA_GROUPS = 2
NSA_DIM = 64
NSA_CMP_BLOCK = 32
NSA_SEL_BLOCK = 64
NSA_TOPN = 16
NSA_WINDOW = 512
NSA_CMP_HIDDEN = 256
MEM_LEN = 256
CA_HEADS = 4
CA_DIM = 128
PEER_HEADS = 8
PEER_NKEYS = 128
PEER_EXPERTS = PEER_NKEYS * PEER_NKEYS
PEER_DKEY = 256
PEER_TOPK = 16
PEER_CHUNK = 128

DA_QK = DA_HEADS * 2 * DA_DIM
DA_V = DA_HEADS * 2 * DA_DIM
NSA_Q = NSA_HEADS * NSA_DIM
NSA_KV = 6 * NSA_GROUPS * NSA_DIM
NSA_G = NSA_HEADS * 3
IN_SIZES = (DA_QK, DA_QK, DA_V, NSA_Q, NSA_KV, NSA_G, D_MODEL, D_MODEL)
IN_TOTAL = DA_QK * 2 + DA_V + NSA_Q + NSA_KV + NSA_G + 2 * D_MODEL


def rms_norm(x, g, eps=1e-6):
    xf = x.astype(jnp.float32)
    y = xf * lax.rsqrt(jnp.mean(xf * xf, axis=-1, keepdims=True) + eps)
    return (y * g.astype(jnp.float32)).astype(x.dtype)

def alibi_slopes(n_heads):
    return 2.0 ** (-8.0 * jnp.arange(1, n_heads + 1, dtype=jnp.float32) / n_heads)

def diff_attention(q, k, v, lam_params, subln_g, lambda_init):
    B, S, H, _, d = q.shape
    nqb = S // Q_BLOCK
    lam = (jnp.exp(jnp.sum(lam_params[0] * lam_params[1]).astype(jnp.float32))
           - jnp.exp(jnp.sum(lam_params[2] * lam_params[3]).astype(jnp.float32)) + lambda_init)
    slopes = alibi_slopes(H)
    scale = d ** -0.5
    kpos = jnp.arange(S)
    qb = q.reshape(B, nqb, Q_BLOCK, H, 2, d).transpose(1, 0, 2, 3, 4, 5)

    def block(args):
        qi, i = args
        qpos = i * Q_BLOCK + jnp.arange(Q_BLOCK)
        dist = (qpos[:, None] - kpos[None, :]).astype(jnp.float32)
        s = jnp.einsum('bqhcd,bkhcd->bhcqk', qi, k).astype(jnp.float32) * scale
        s = s - slopes[None, :, None, None, None] * dist
        s = jnp.where(dist >= 0, s, -jnp.inf)
        p = jax.nn.softmax(s, axis=-1)
        a = p[:, :, 0] - lam * p[:, :, 1]
        return jnp.einsum('bhqk,bkhe->bqhe', a.astype(v.dtype), v)

    o = lax.map(block, (qb, jnp.arange(nqb)))
    o = o.transpose(1, 0, 2, 3, 4).reshape(B, S, H, 2 * d)
    o = rms_norm(o, subln_g) * (1.0 - lambda_init)
    return o.reshape(B, S, H * 2 * d)

def nsa_attention(q, kv, gates, cmp_pos, ck_w1, ck_w2, cv_w1, cv_w2):
    B, S, G, R, dh = q.shape
    slopes = alibi_slopes(G * R).reshape(G, R)
    scale = dh ** -0.5
    pos = jnp.arange(S)
    k_c, v_c, k_s, v_s, k_w, v_w = [kv[:, :, j] for j in range(6)]

    nc = S // NSA_CMP_BLOCK

    def compress(t, w1, w2):
        tb = t.reshape(B, nc, NSA_CMP_BLOCK, G, dh) + cmp_pos[None, None, :, None, :]
        tb = tb.transpose(0, 1, 3, 2, 4).reshape(B, nc, G, NSA_CMP_BLOCK * dh)
        return jax.nn.gelu(tb @ w1, approximate=False) @ w2

    kc = compress(k_c, ck_w1, ck_w2)
    vc = compress(v_c, cv_w1, cv_w2)
    cpos = jnp.arange(nc) * NSA_CMP_BLOCK + (NSA_CMP_BLOCK - 1)
    dist_c = (pos[:, None] - cpos[None, :]).astype(jnp.float32)
    valid_c = dist_c >= 0
    s = jnp.einsum('bsgrd,bcgd->bgrsc', q, kc).astype(jnp.float32) * scale
    s = s - slopes[None, :, :, None, None] * dist_c
    s = jnp.where(valid_c, s, -1e30)
    p_cmp = jax.nn.softmax(s, axis=-1) * valid_c
    o_cmp = jnp.einsum('bgrsc,bcgd->bsgrd', p_cmp.astype(vc.dtype), vc)

    nsb = S // NSA_SEL_BLOCK
    ratio = NSA_SEL_BLOCK // NSA_CMP_BLOCK
    p_slc = p_cmp.sum(axis=2).reshape(B, G, S, nsb, ratio).sum(-1)
    blk = jnp.arange(nsb)
    cur = pos // NSA_SEL_BLOCK
    valid_b = blk[None, :] <= cur[:, None]
    forced = (blk[None, :] == 0) | (blk[None, :] == cur[:, None]) | (blk[None, :] == cur[:, None] - 1)
    score = jnp.where(forced, 1e4, jnp.where(valid_b, p_slc, -1e9))
    n_sel = min(NSA_TOPN, nsb)
    _, idx = lax.top_k(score, n_sel)

    nqb = S // Q_BLOCK
    ksb = k_s.reshape(B, nsb, NSA_SEL_BLOCK, G, dh).transpose(0, 3, 1, 2, 4)
    vsb = v_s.reshape(B, nsb, NSA_SEL_BLOCK, G, dh).transpose(0, 3, 1, 2, 4)
    q_blocks = q.reshape(B, nqb, Q_BLOCK, G, R, dh).transpose(1, 0, 2, 3, 4, 5)
    idx_blocks = idx.reshape(B, G, nqb, Q_BLOCK, n_sel).transpose(2, 0, 1, 3, 4)
    b_ix = jnp.arange(B)[:, None, None, None]
    g_ix = jnp.arange(G)[None, :, None, None]
    off = jnp.arange(NSA_SEL_BLOCK)

    def sel_block(args):
        qi, ii, i = args
        kg = ksb[b_ix, g_ix, ii]
        vg = vsb[b_ix, g_ix, ii]
        qpos = i * Q_BLOCK + jnp.arange(Q_BLOCK)
        kpos = ii[..., None] * NSA_SEL_BLOCK + off
        dist = (qpos[None, None, :, None, None] - kpos).astype(jnp.float32)[:, :, None]
        ss = jnp.einsum('bqgrd,bgqnld->bgrqnl', qi, kg).astype(jnp.float32) * scale
        ss = ss - slopes[None, :, :, None, None, None] * dist
        ss = jnp.where(dist >= 0, ss, -jnp.inf)
        pp = jax.nn.softmax(ss.reshape(B, G, R, Q_BLOCK, n_sel * NSA_SEL_BLOCK), axis=-1)
        pp = pp.reshape(B, G, R, Q_BLOCK, n_sel, NSA_SEL_BLOCK).astype(vg.dtype)
        return jnp.einsum('bgrqnl,bgqnld->bqgrd', pp, vg)

    o_slc = lax.map(sel_block, (q_blocks, idx_blocks, jnp.arange(nqb)))
    o_slc = o_slc.transpose(1, 0, 2, 3, 4, 5).reshape(B, S, G, R, dh)

    wb = NSA_WINDOW // Q_BLOCK
    pad = jnp.zeros((B, NSA_WINDOW, G, dh), k_w.dtype)
    kwp = jnp.concatenate([pad, k_w], axis=1).reshape(B, nqb + wb, Q_BLOCK, G, dh)
    vwp = jnp.concatenate([pad, v_w], axis=1).reshape(B, nqb + wb, Q_BLOCK, G, dh)
    kwin = jnp.concatenate([kwp[:, j:j + nqb] for j in range(wb + 1)], axis=2)
    vwin = jnp.concatenate([vwp[:, j:j + nqb] for j in range(wb + 1)], axis=2)
    qblk = q.reshape(B, nqb, Q_BLOCK, G, R, dh)
    qpos = jnp.arange(nqb)[:, None] * Q_BLOCK + jnp.arange(Q_BLOCK)
    kpos = jnp.arange(nqb)[:, None] * Q_BLOCK - NSA_WINDOW + jnp.arange((wb + 1) * Q_BLOCK)
    dist = (qpos[:, :, None] - kpos[:, None, :]).astype(jnp.float32)
    valid = (dist >= 0) & (dist < NSA_WINDOW) & (kpos[:, None, :] >= 0)
    sw = jnp.einsum('bnqgrd,bnkgd->bngrqk', qblk, kwin).astype(jnp.float32) * scale
    sw = sw - slopes[None, None, :, :, None, None] * dist[None, :, None, None]
    sw = jnp.where(valid[None, :, None, None], sw, -jnp.inf)
    pw = jax.nn.softmax(sw, axis=-1).astype(vwin.dtype)
    o_win = jnp.einsum('bngrqk,bnkgd->bnqgrd', pw, vwin).reshape(B, S, G, R, dh)

    o = gates[..., 0:1] * o_cmp + gates[..., 1:2] * o_slc + gates[..., 2:3] * o_win
    return o.reshape(B, S, G * R * dh)

def memory_cross_attention(u, m, wq, wkv, wo):
    B, S, _ = u.shape
    M = m.shape[1]
    q = (u @ wq).reshape(B, S, CA_HEADS, CA_DIM)
    kv = (m @ wkv).reshape(B, M, 2, CA_HEADS, CA_DIM)
    s = jnp.einsum('bshd,bmhd->bhsm', q, kv[:, :, 0]).astype(jnp.float32) * (CA_DIM ** -0.5)
    p = jax.nn.softmax(s, axis=-1).astype(u.dtype)
    o = jnp.einsum('bhsm,bmhd->bshd', p, kv[:, :, 1]).reshape(B, S, CA_HEADS * CA_DIM)
    return o @ wo

def peer_ffn(u, w_q, sub_keys, u_tab, v_tab):
    B, S, D = u.shape
    T = B * S
    K = PEER_TOPK
    H = PEER_HEADS
    xt = u.reshape(T, D)
    q = (xt @ w_q).reshape(T, H, 2, PEER_DKEY // 2)
    s = jnp.einsum('thcd,hcnd->thcn', q, sub_keys).astype(jnp.float32)
    top_s, top_i = lax.top_k(s, K)
    cand = (top_s[:, :, 0, :, None] + top_s[:, :, 1, None, :]).reshape(T, H, K * K)
    cand_i = (top_i[:, :, 0, :, None] * PEER_NKEYS + top_i[:, :, 1, None, :]).reshape(T, H, K * K)
    best_s, best_j = lax.top_k(cand, K)
    expert = jnp.take_along_axis(cand_i, best_j, axis=-1)
    g = jax.nn.softmax(best_s, axis=-1).astype(u.dtype)
    nch = T // PEER_CHUNK

    def chunk(args):
        xc, ec, gc = args
        act = jax.nn.gelu(jnp.einsum('cd,chkd->chk', xc, u_tab[ec]), approximate=False)
        return jnp.einsum('chk,chkd->cd', gc * act, v_tab[ec])

    out = lax.map(chunk, (xt.reshape(nch, PEER_CHUNK, D),
                          expert.reshape(nch, PEER_CHUNK, H, K),
                          g.reshape(nch, PEER_CHUNK, H, K)))
    return out.reshape(B, S, D)

def second_inputs(seed: int = 0) -> dict:
    key = jax.random.key(seed)
    ks = jax.random.split(key, 32)
    L, D = DEPTH, D_MODEL

    def nrm(k, shape, scale):
        return jax.random.normal(k, shape, jnp.float32) * scale

    def gain(k, shape):
        return 1.0 + 0.02 * jax.random.normal(k, shape, jnp.float32)

    return {
        "x": nrm(ks[0], (BATCH, SEQ, D), 1.0),
        "mem": nrm(ks[1], (BATCH, MEM_LEN, D), 1.0),
        "norm_mix": gain(ks[2], (L, D)),
        "w_in": nrm(ks[3], (L, D, IN_TOTAL), D ** -0.5),
        "diff_lambda": nrm(ks[4], (L, 4, DA_DIM), 0.1),
        "diff_subln": gain(ks[5], (L, 2 * DA_DIM)),
        "nsa_cmp_pos": nrm(ks[6], (L, NSA_CMP_BLOCK, NSA_DIM), 0.1),
        "nsa_ck_w1": nrm(ks[7], (L, NSA_CMP_BLOCK * NSA_DIM, NSA_CMP_HIDDEN), (NSA_CMP_BLOCK * NSA_DIM) ** -0.5),
        "nsa_ck_w2": nrm(ks[8], (L, NSA_CMP_HIDDEN, NSA_DIM), NSA_CMP_HIDDEN ** -0.5),
        "nsa_cv_w1": nrm(ks[9], (L, NSA_CMP_BLOCK * NSA_DIM, NSA_CMP_HIDDEN), (NSA_CMP_BLOCK * NSA_DIM) ** -0.5),
        "nsa_cv_w2": nrm(ks[10], (L, NSA_CMP_HIDDEN, NSA_DIM), NSA_CMP_HIDDEN ** -0.5),
        "w_branch_a": nrm(ks[11], (L, DA_V, D), DA_V ** -0.5),
        "w_branch_b": nrm(ks[12], (L, NSA_Q, D), NSA_Q ** -0.5),
        "w_out": nrm(ks[13], (L, D, D), D ** -0.5),
        "norm_cross": gain(ks[14], (L, D)),
        "norm_mem": gain(ks[15], (L, D)),
        "w_cross_q": nrm(ks[16], (L, D, CA_HEADS * CA_DIM), D ** -0.5),
        "w_cross_kv": nrm(ks[17], (L, D, 2 * CA_HEADS * CA_DIM), D ** -0.5),
        "w_cross_o": nrm(ks[18], (L, CA_HEADS * CA_DIM, D), (CA_HEADS * CA_DIM) ** -0.5),
        "norm_ffn": gain(ks[19], (L, D)),
        "peer_wq": nrm(ks[20], (L, D, PEER_HEADS * PEER_DKEY), D ** -0.5),
        "peer_subkeys": nrm(ks[21], (L, PEER_HEADS, 2, PEER_NKEYS, PEER_DKEY // 2), (PEER_DKEY // 2) ** -0.5),
        "peer_u": nrm(ks[22], (L, PEER_EXPERTS, D), D ** -0.5),
        "peer_v": nrm(ks[23], (L, PEER_EXPERTS, D), (PEER_HEADS * PEER_TOPK) ** -0.5),
        "norm_final": gain(ks[24], (D,)),
    }

def second_block(x, mem, norm_mix, w_in, diff_lambda, diff_subln, nsa_cmp_pos, nsa_ck_w1, nsa_ck_w2,
              nsa_cv_w1, nsa_cv_w2, w_branch_a, w_branch_b, w_out, norm_cross, norm_mem,
              w_cross_q, w_cross_kv, w_cross_o, norm_ffn, peer_wq, peer_subkeys, peer_u, peer_v,
              norm_final):
    B, S, D = x.shape
    split_at = np.cumsum(IN_SIZES)[:-1].tolist()
    h = x
    for l in range(DEPTH):
        lambda_init = 0.8 - 0.6 * math.exp(-0.3 * l)
        u = rms_norm(h, norm_mix[l])
        qa, ka, va, qb, kvb, gb, gate_a, gate_b = jnp.split(u @ w_in[l], split_at, axis=-1)
        o_a = diff_attention(qa.reshape(B, S, DA_HEADS, 2, DA_DIM),
                             ka.reshape(B, S, DA_HEADS, 2, DA_DIM),
                             va.reshape(B, S, DA_HEADS, 2 * DA_DIM),
                             diff_lambda[l], diff_subln[l], lambda_init)
        R = NSA_HEADS // NSA_GROUPS
        o_b = nsa_attention(qb.reshape(B, S, NSA_GROUPS, R, NSA_DIM),
                            kvb.reshape(B, S, 6, NSA_GROUPS, NSA_DIM),
                            jax.nn.sigmoid(gb).reshape(B, S, NSA_GROUPS, R, 3),
                            nsa_cmp_pos[l], nsa_ck_w1[l], nsa_ck_w2[l], nsa_cv_w1[l], nsa_cv_w2[l])
        merged = (jax.nn.sigmoid(gate_a) * (o_a @ w_branch_a[l])
                  + jax.nn.sigmoid(gate_b) * (o_b @ w_branch_b[l]))
        h = h + merged @ w_out[l]
        h = h + memory_cross_attention(rms_norm(h, norm_cross[l]), rms_norm(mem, norm_mem[l]),
                                       w_cross_q[l], w_cross_kv[l], w_cross_o[l])
        h = h + peer_ffn(rms_norm(h, norm_ffn[l]), peer_wq[l], peer_subkeys[l], peer_u[l], peer_v[l])
    return rms_norm(h, norm_final)


def setup_inputs(seed=0):
    out = dict(first_inputs(seed))
    for name, value in second_inputs(seed + 1).items():
        if name != "x":
            out[name + "_2"] = value
    return out


def reference(
    x, attn_norm_g, w_in, sg_norm_g, w_spatial, b_spatial, sb_out_norm_g, sg_out_norm_g, w_out,
    ffn_norm_g, w_router_group, b_router_group, w_router_expert, b_router_expert, w_gate, w_up,
    w_down, final_norm_g, mem_2, norm_mix_2, w_in_2, diff_lambda_2, diff_subln_2, nsa_cmp_pos_2,
    nsa_ck_w1_2, nsa_ck_w2_2, nsa_cv_w1_2, nsa_cv_w2_2, w_branch_a_2, w_branch_b_2, w_out_2,
    norm_cross_2, norm_mem_2, w_cross_q_2, w_cross_kv_2, w_cross_o_2, norm_ffn_2, peer_wq_2,
    peer_subkeys_2, peer_u_2, peer_v_2, norm_final_2,
):
    x = first_block(
        x, attn_norm_g, w_in, sg_norm_g, w_spatial, b_spatial, sb_out_norm_g, sg_out_norm_g,
        w_out, ffn_norm_g, w_router_group, b_router_group, w_router_expert, b_router_expert,
        w_gate, w_up, w_down, final_norm_g,
    )
    return second_block(
        x, mem_2, norm_mix_2, w_in_2, diff_lambda_2, diff_subln_2, nsa_cmp_pos_2, nsa_ck_w1_2,
        nsa_ck_w2_2, nsa_cv_w1_2, nsa_cv_w2_2, w_branch_a_2, w_branch_b_2, w_out_2,
        norm_cross_2, norm_mem_2, w_cross_q_2, w_cross_kv_2, w_cross_o_2, norm_ffn_2, peer_wq_2,
        peer_subkeys_2, peer_u_2, peer_v_2, norm_final_2,
    )


_drawn_inputs = setup_inputs


def setup_inputs(seed=0):
    import zlib

    import numpy as np

    out = dict(_drawn_inputs(seed))
    spreads = {}
    factors = {'sg_norm_g': 4.612,
     'b_spatial': 3.265,
     'sb_out_norm_g': 3.105,
     'sg_out_norm_g': 3.976,
     'ffn_norm_g': 2.678,
     'b_router_group': 4.22,
     'b_router_expert': 4.327,
     'norm_mix_2': 4.17,
     'diff_subln_2': 5.756,
     'nsa_cmp_pos_2': 3.514,
     'nsa_ck_w1_2': 2.689,
     'nsa_ck_w2_2': 2.679,
     'norm_cross_2': 8.0,
     'norm_mem_2': 8.0,
     'norm_ffn_2': 45.961,
     'norm_final_2': 8.027}
    for name, (base, spread) in spreads.items():
        noise = np.random.default_rng([zlib.crc32(name.encode()), seed]).standard_normal(out[name].shape)
        drawn = base * np.exp(spread * noise) if base else spread * noise
        out[name] = __import__('jax').numpy.asarray(drawn.astype(out[name].dtype))
    for name, factor in factors.items():
        out[name] = (out[name] * factor).astype(out[name].dtype)
    return out
```

```python
from contextlib import ExitStack

import concourse.bass as bass
from concourse import mybir

F32 = mybir.dt.float32
U32 = mybir.dt.uint32
ALU = mybir.AluOpType
ACT = mybir.ActivationFunctionType
AX = mybir.AxisListType.X

EPS = 1e-6
D = 1024
NC_CONST = dict(ident=128, tri=128, neg=128, m01=128, negu=128, neg1=128, dist=384, cmpb=128, cmpv=16,
                bd=512, esel=64, iota=128)
NC_SMALL = dict(g_attn=8, g_mix=8, g_ffn=8, g_nmix=8, g_sub=1, g_cross=8, g_mem=8, g_peer=8, bsp=8, pos=32,
                lam=256, rb=36)
NC_ROWS = dict(sg=512, fin1=1024, fin2=1024)


class Queue:

    def __init__(self, sem):
        self.sem, self.n, self.items, self.seen = sem, 0, [], {}

    def wait(self, *tokens):
        for t in tokens:
            if t is None:
                continue
            sem, v = t
            if self.seen.get(id(sem), 0) < v:
                self.seen[id(sem)] = v
                self.items.append(lambda e, sem=sem, v=v: e.wait_ge(sem, v))

    def raw(self, f, *tokens):
        self.wait(*tokens)
        self.items.append(f)

    def do(self, f, *tokens):
        self.wait(*tokens)
        self.n += 1
        self.items.append(lambda e: f(e).then_inc(self.sem, 1))
        return (self.sem, self.n)

    def last(self):
        return (self.sem, self.n) if self.n else None


def program(nc, stage, x, const, small, rows, w_in, w_sp, w_out, w_r, w_gate, w_up, w_down, mem, w_in2, ck1, ck2,
            w_a, w_b, w_out2, w_cq, w_ckv, w_co, w_pq, subk, peer_u, peer_v, out):
    ctx = ExitStack()
    with ctx:
        def sb(name, shape, dt=F32):
            return ctx.enter_context(nc.sbuf_tensor(name, shape, dt))

        def sem(name):
            return ctx.enter_context(nc.semaphore(name))

        NR = 6
        AR = sb("AR", [128, 8 * 4096])
        Wk = sb("Wk", [128, 9200])
        Hs = sb("Hs", [128, 2 * D])
        XSs = sb("XSs", [128, 2 * D])
        NTs = sb("NTs", [128, 8 * 256])
        CO = sb("CO", [128, sum(NC_CONST.values())])
        SM = sb("SM", [128, sum(NC_SMALL.values())])
        RW = sb("RW", [128, sum(NC_ROWS.values())])
        ST = sb("ST", [128, 64])
        PSt = ctx.enter_context(nc.psum_tensor("PS", [128, 8 * 512], F32))

        def parts(t, widths):
            at, d = 0, {}
            for k, n in widths.items():
                d[k] = t[:, at:at + n]
                at += n
            return d

        co, sm, rw = parts(CO, NC_CONST), parts(SM, NC_SMALL), parts(RW, NC_ROWS)
        ident = co["ident"]
        H = Hs[:, :].rearrange("p (t d) -> p t d", t=2)
        XS = XSs[:, :].rearrange("p (t d) -> p t d", t=2)
        NT = NTs[:, :].rearrange("p (c t) -> p c t", c=8)

        def P(b, n=1):
            return PSt[:, b * 512:(b + n) * 512]

        pe, act, dve, pool = (Queue(sem(f"s_{n}")) for n in ("pe", "act", "dve", "pool"))
        sp = Queue(sem("s_sp"))
        qs = (pe, act, dve, pool)

        def bar():
            for a in qs:
                for b in qs:
                    a.wait(b.last())

        nload = [0]

        def load(q, dst, src, *tokens):
            nload[0] += 1
            s = sem(f"ld{nload[0]}")
            q.raw(lambda e: e.dma_start(dst, src).then_inc(s, 16), *tokens)
            return (s, 16)

        ring_sem = [sem(f"ring{i}") for i in range(NR)]
        ring_n, ring_free = [0], [[] for _ in range(NR)]

        def unit(src, shape_str, **kw):
            n = ring_n[0]
            ring_n[0] += 1
            s = n % NR
            npart = src.shape[0]
            cols = 1
            for z in src.shape[1:]:
                cols *= z
            dst = AR[0:npart, s * 4096:s * 4096 + cols]
            sp.raw(lambda e: e.dma_start(dst, src).then_inc(ring_sem[s], 16), *ring_free[s])
            return dst.rearrange(shape_str, **kw), (ring_sem[s], 16 * (n // NR + 1)), s

        def done(slot, *tokens):
            ring_free[slot] = list(tokens)

        class Bump:
            def __init__(self, t, lo, hi):
                self.t, self.lo, self.at, self.hi = t, lo, lo, hi

            def __call__(self, n, s=None, p=128, **kw):
                a = self.t[0:p, self.at:self.at + n]
                self.at += n
                assert self.at <= self.hi, (self.at, self.hi)
                return a.rearrange(s, **kw) if s else a

            def reset(self):
                self.at = self.lo

        wk = Bump(Wk, 0, 9200)
        w2 = Bump(AR, NR * 4096, 8 * 4096)

        def mm(o, l, r, start, stop):
            return lambda e: e.matmul(o, l, r, start=start, stop=stop, skip_group_check=True)

        def tr(o, i, n=128):
            return lambda e: e.transpose(o, i, ident[0:n, 0:n])

        def bc(ap, shape):
            return ap.broadcast_to(shape)

        t_x = load(act, H, x.rearrange("(t p) d -> p t d", p=128))
        t_co = load(act, CO[:, :], const)
        t_sm = load(act, SM[:, :], small)
        t_rw = load(act, RW[:, :], rows)
        for q in (pe, act, dve, pool):
            q.wait(t_x, t_co, t_sm, t_rw)

        def rstd(ss, n, width, *tokens):
            a = dve.do(lambda e: e.tensor_scalar(ss, ss, 1.0 / width, EPS, ALU.mult, ALU.add), *tokens)
            b = act.do(lambda e: e.activation(ss, ss, ACT.Sqrt), a)
            return dve.do(lambda e: e.reciprocal(ss, ss), b)

        def square_sum(src, junk, ss, *tokens):
            return act.do(lambda e: e.activation(junk, src, ACT.Square, accum_out=ss), *tokens)

        def turn_all(src, dst, nchunk, gain, first_bank, strided, *tokens):
            toks = []
            for pair in range(nchunk // 2):
                bank = P(first_bank + pair).rearrange("p (c t) -> p c t", c=2)
                for k in range(2):
                    c = 2 * pair + k
                    for tt in range(2):
                        s = src[:, tt, c::nchunk] if strided else src[:, tt, c * 128:(c + 1) * 128]
                        t = pe.do(tr(bank[:, k, tt * 128:(tt + 1) * 128], s), *tokens)
                if gain is None:
                    o = dst[:, 2 * pair:2 * pair + 2, :]
                    if pair % 2:
                        toks.append(act.do(lambda e, o=o, bank=bank: e.activation(o, bank, ACT.Copy), t))
                    else:
                        toks.append(dve.do(lambda e, o=o, bank=bank: e.tensor_copy(o, bank), t))
                else:
                    for k in range(2):
                        c = 2 * pair + k
                        toks.append(dve.do(lambda e, c=c, k=k, bank=bank: e.tensor_scalar(
                            dst[:, c, :], bank[:, k, :], gain(c), None, ALU.mult), t))
            return toks

        def norm_turn(src, dst, gain):
            ts = [square_sum(src[:, tt, :], XS[:, tt, :], ST[:, tt:tt + 1]) for tt in range(2)]
            r = rstd(ST[:, 0:2], 2, D, *ts)
            for tt in range(2):
                t = dve.do(lambda e, tt=tt: e.tensor_scalar(XS[:, tt, :], src[:, tt, :], ST[:, tt:tt + 1], None, ALU.mult), r)
            turn_all(XS, dst, 8, lambda c: gain[:, c:c + 1], 0, True, t)
            bar()

        def proj(o, lhs, rhs, n, *tokens):
            pe.wait(*tokens)
            for c in range(n):
                f = mm(o, lhs(c), rhs(c), c == 0, c == n - 1)
                if c < n - 1:
                    pe.raw(f)
                else:
                    return pe.do(f)

        bank_free = [[] for _ in range(8)]

        def proj_turned(u, src, dst, banks, scale=None):
            w, tw, slot = u
            toks = []
            for m in range(4):
                b = banks[m % len(banks)]
                o = P(b)[:, 0:256]
                t = proj(o, lambda c: w[:, c, m * 128:(m + 1) * 128], lambda c: src[:, c, :], 8, tw, *bank_free[b])
                if scale is None:
                    k = act.do(lambda e, m=m, o=o: e.activation(dst[:, m, :], o, ACT.Copy), t)
                else:
                    k = act.do(lambda e, m=m, o=o: e.activation(dst[:, m, :], o, ACT.Copy, scale=scale), t)
                bank_free[b] = [k]
                toks.append(k)
            done(slot, t)
            return toks

        def proj_tokens(u, src, banks, evac, ncol=512, nchunk=8):
            w, tw, slot = u
            toks = []
            for tt in range(2):
                b = banks[tt]
                o = P(b)[:, 0:ncol]
                t = proj(o, lambda c: src[:, c, tt * 128:(tt + 1) * 128], lambda c: w[:, c, 0:ncol], nchunk, tw, *bank_free[b])
                k = evac(tt, o, t)
                bank_free[b] = [k]
                toks.append(k)
            done(slot, t)
            return toks

        def add_residual(srcs, units, nchunk):
            for j, u in enumerate(units):
                def evac(tt, o, t, j=j):
                    h = H[:, tt, j * 512:(j + 1) * 512]
                    return dve.do(lambda e: e.tensor_tensor(h, o, h, ALU.add), t)
                proj_tokens(u, srcs, [2 * j, 2 * j + 1], evac, nchunk=nchunk)

        def copy_out(dst):
            return lambda tt, o, t: act.do(lambda e: e.activation(dst[:, tt, :], o, ACT.Copy), t)

        def finish(src):
            bar()
            t = dve.do(lambda e: e.tensor_copy(XS, src)) if src is not None else dve.last()
            s = sem("s_out")
            sp.raw(lambda e: e.dma_start(out.rearrange("(t p) d -> p t d", p=128), XS).then_inc(s, 16), t)
            sp.raw(lambda e: e.wait_ge(s, 16))

        def emit():
            with nc.Block() as block:
                for q, reg in ((sp, block.sync), (pe, block.tensor), (act, block.scalar), (dve, block.vector),
                               (pool, block.gpsimd)):
                    @reg
                    def _(e, q=q):
                        for f in q.items:
                            f(e)

        def w8(src, i):
            return unit(src[i], "p (c n) -> p c n", c=8)

        def mixers():
            norm_turn(H, NT, sm["g_attn"])
            qT = wk(1024, "p (m t) -> p m t", m=4)
            kT = wk(1024, "p (m t) -> p m t", m=4)
            V1 = wk(1024, "p (t n) -> p t n", t=2)
            WS = wk(1024, "p (h t) -> p h t", h=8)
            MX = wk(2048, "p (t n) -> p t n", t=2)
            U1 = wk(1024, "p (t n) -> p t n", t=2)
            SP = w2(3072)
            T1 = w2(3072)
            VG = w2(1024, "p (t n) -> p t n", t=2)
            t_ws = load(act, WS, w_sp.rearrange("p (h t) -> p h t", h=8))
            proj_turned(w8(w_in, 0), NT, qT, [0, 1], 0.125)
            proj_turned(w8(w_in, 1), NT, kT, [2, 3])
            proj_tokens(w8(w_in, 2), NT, [4, 5], copy_out(V1))

            def gelu_out(dst):
                return lambda tt, o, t: act.do(lambda e: e.activation(dst[:, tt, :], o, ACT.Gelu_apprx_tanh), t)
            proj_tokens(w8(w_in, 3), NT, [6, 7], gelu_out(U1))
            proj_tokens(w8(w_in, 4), NT, [4, 5], gelu_out(VG))
            bar()

            blocks = [(0, 0), (0, 1), (1, 1)]
            sptok, zt = [], []
            for b, (kt, qt) in enumerate(blocks):
                for h in range(8):
                    r = slice(64 * (h % 2), 64 * (h % 2) + 64)
                    o = P(2 * b + h % 2)[:, (h // 2) * 128:(h // 2) * 128 + 128]
                    t = pe.do(mm(o, kT[r, h // 2, kt * 128:kt * 128 + 128], qT[r, h // 2, qt * 128:qt * 128 + 128],
                                 h < 2, False))
                zt.append(t)
                z = P(2 * b, 2)
                l = T1[:, b * 1024:(b + 1) * 1024]
                s = SP[:, b * 1024:(b + 1) * 1024]
                t = act.do(lambda e, l=l, z=z: e.activation(l, z, ACT.Abs), t)
                t = act.do(lambda e, l=l: e.activation(l, l, ACT.Exp, scale=-1.0), t)
                t = act.do(lambda e, l=l: e.activation(l, l, ACT.Ln, bias=1.0), t)
                t = dve.do(lambda e, s=s, z=z, l=l: e.scalar_tensor_tensor(s, z, 0.0, l, ALU.max, ALU.add), t)
                if kt == qt:
                    v = s.rearrange("p (h t) -> p h t", h=8)
                    m = bc(co["m01"].unsqueeze(1), [128, 8, 128])
                    t = dve.do(lambda e, v=v, m=m: e.tensor_tensor(v, v, m, ALU.mult), t)
                sptok.append(t)
            atok = []
            for b in range(3):
                for j in range(2):
                    o = P(2 * b + j)
                    s = SP[:, b * 1024 + j * 512:b * 1024 + (j + 1) * 512]
                    t = pe.do(mm(o, co["negu"], s, False, b != 1), sptok[b])
                    if b == 1:
                        s = SP[:, 2048 + j * 512:2048 + (j + 1) * 512]
                        t = pe.do(mm(o, co["neg1"], s, False, True), sptok[2])
                z = P(2 * b, 2)
                l = T1[:, b * 1024:(b + 1) * 1024]
                if b != 1:
                    v = l.rearrange("p (h t) -> p h t", h=8)
                    zv = z.rearrange("p (h t) -> p h t", h=8)
                    m = bc(co["neg"].unsqueeze(1), [128, 8, 128])
                    t = dve.do(lambda e, v=v, zv=zv, m=m: e.tensor_tensor(v, zv, m, ALU.min), t)
                    z = l
                atok.append(act.do(lambda e, l=l, z=z: e.activation(l, z, ACT.Exp), t))
            A = T1.rearrange("p (b h t) -> p b h t", b=3, h=8)
            for h in range(8):
                i = h % 2 * 4 + h // 2
                cs = slice(h * 64, h * 64 + 64)
                pe.raw(mm(P(6)[:, cs], A[:, 0, i, :], V1[:, 0, cs], True, True), *atok)
                pe.raw(mm(P(7)[:, cs], A[:, 1, i, :], V1[:, 0, cs], True, False))
                t_pv = pe.do(mm(P(7)[:, cs], A[:, 2, i, :], V1[:, 1, cs], False, True))
            ts = [square_sum(VG[:, tt, :], MX[:, tt, 512:1024], ST[:, 4 + tt:5 + tt]) for tt in range(2)]
            r = rstd(ST[:, 4:6], 2, 512, *ts)
            tv = [dve.do(lambda e, tt=tt: e.scalar_tensor_tensor(VG[:, tt, :], VG[:, tt, :], ST[:, 4 + tt:5 + tt], rw["sg"],
                                                                 ALU.mult, ALU.mult), r) for tt in range(2)]
            tw = pool.do(lambda e: e.tensor_tensor(WS, WS, bc(co["tri"].unsqueeze(1), [128, 8, 128]), ALU.mult), t_ws)
            for h in range(8):
                o = P(h // 4)[:, (h % 4) * 128:(h % 4) * 128 + 128].rearrange("p (c d) -> p c d", c=2)
                t = pe.do(mm(o, WS[:, h, :], VG[:, :, h * 64:h * 64 + 64], True, True), tw, *tv, *atok)
            for c in range(2):
                o = P(0, 2).rearrange("p (h c d) -> p h c d", h=8, c=2)[:, :, c, :]
                v = MX[:, c, 512:1024].rearrange("p (h d) -> p h d", h=8)
                u = U1[:, c, :].rearrange("p (h d) -> p h d", h=8)
                bb = bc(sm["bsp"].unsqueeze(2), [128, 8, 64])
                t1 = dve.do(lambda e, o=o, v=v, bb=bb: e.tensor_tensor(v, o, bb, ALU.add), t)
                t1 = dve.do(lambda e, v=v, u=u: e.tensor_tensor(v, v, u, ALU.mult), t1)
            ts = []
            for tt in range(2):
                ts.append(square_sum(P(6 + tt), SP[:, 1024 * tt:1024 * tt + 512], ST[:, 8 + tt:9 + tt], t_pv))
                ts.append(square_sum(MX[:, tt, 512:1024], SP[:, 1024 * tt + 512:1024 * tt + 1024], ST[:, 10 + tt:11 + tt], t1))
            r = rstd(ST[:, 8:12], 4, 512, *ts)
            for tt in range(2):
                dve.do(lambda e, tt=tt: e.tensor_scalar(MX[:, tt, 0:512], P(6 + tt), ST[:, 8 + tt:9 + tt], None, ALU.mult), r)
                t = dve.do(lambda e, tt=tt: e.tensor_scalar(MX[:, tt, 512:1024], MX[:, tt, 512:1024], ST[:, 10 + tt:11 + tt],
                                                            None, ALU.mult), r)
            turn_all(MX, NT, 8, lambda c: sm["g_mix"][:, c:c + 1], 2, True, t)
            bar()
            add_residual(NT, [w8(w_out, 0), w8(w_out, 1)], 8)
            bar()

        def experts():
            wk.reset()
            w2.reset()
            norm_turn(H, NT, sm["g_ffn"])
            WR = wk(288, "p (c n) -> p c n", c=8)
            LG = wk(72, "p (t n) -> p t n", t=2)
            G8 = wk(16, "p (t n) -> p t n", t=2)
            E8 = wk(16, "p (t n) -> p t n", t=2)
            M8 = wk(32, "p (a t n) -> p a t n", a=2, t=2)
            X8 = ctx.enter_context(nc.sbuf_tensor("X8", [128, 2, 2, 8], U32))
            XF = wk(32, "p (a t n) -> p a t n", a=2, t=2)
            OG = wk(8, "p (t n) -> p t n", t=2)
            OE = wk(32, "p (a t n) -> p a t n", a=2, t=2)
            EX = wk(64, "p (t n) -> p t n", t=2)
            CB = wk(64, "p (t g n) -> p t g n", t=2, g=4)
            sc = wk(16, "p (k t) -> p k t", t=2)
            t_wr = load(act, WR, w_r.rearrange("p (c n) -> p c n", c=8))
            for tt in range(2):
                t = proj(P(tt)[:, 0:36], lambda c: NT[:, c, tt * 128:tt * 128 + 128], lambda c: WR[:, c, :], 8, t_wr)
                t = dve.do(lambda e, tt=tt: e.tensor_tensor(LG[:, tt, :], P(tt)[:, 0:36], sm["rb"], ALU.add), t)
                io = co["iota"]

                def chain(f, q=dve):
                    nonlocal t
                    t = q.do(f, t)

                chain(lambda e, tt=tt: e.memset(G8[:, tt, :], -3e38))
                chain(lambda e, tt=tt: e.tensor_copy(G8[:, tt, 0:4], LG[:, tt, 0:4]))
                chain(lambda e, tt=tt: e.max(M8[:, 0, tt, :], G8[:, tt, :]))
                chain(lambda e, tt=tt: e.max_index(X8[:, 0, tt, :], M8[:, 0, tt, :], G8[:, tt, :]))
                chain(lambda e, tt=tt: e.tensor_copy(XF[:, 0, tt, :], X8[:, 0, tt, :]))
                chain(lambda e, tt=tt: e.tensor_scalar(OG[:, tt, :], io[:, 0:4], XF[:, 0, tt, 0:1], None, ALU.is_equal))
                chain(lambda e, tt=tt: e.tensor_scalar(sc[:, 0, tt:tt + 1], M8[:, 0, tt, 0:1], -1.0, None, ALU.mult))
                chain(lambda e, tt=tt: e.activation(G8[:, tt, 0:4], LG[:, tt, 0:4], ACT.Exp, bias=sc[:, 0, tt:tt + 1],
                                                    accum_out=sc[:, 1, tt:tt + 1]), act)
                chain(lambda e, tt=tt: e.reciprocal(sc[:, 2, tt:tt + 1], sc[:, 1, tt:tt + 1]))
                ev = EX[:, tt, :].rearrange("p (g n) -> p g n", g=4)
                chain(lambda e, tt=tt, ev=ev: e.tensor_tensor(ev, LG[:, tt, 4:36].rearrange("p (g n) -> p g n", g=4),
                                                              bc(OG[:, tt, :].unsqueeze(2), [128, 4, 8]), ALU.mult))
                chain(lambda e, tt=tt, ev=ev: e.tensor_reduce(E8[:, tt, :], ev.rearrange("p g n -> p n g"), AX, ALU.add))
                chain(lambda e, tt=tt: e.max(M8[:, 1, tt, :], E8[:, tt, :]))
                chain(lambda e, tt=tt: e.max_index(X8[:, 1, tt, :], M8[:, 1, tt, :], E8[:, tt, :]))
                chain(lambda e, tt=tt: e.tensor_copy(XF[:, 1, tt, :], X8[:, 1, tt, :]))
                chain(lambda e, tt=tt: e.tensor_scalar(sc[:, 3, tt:tt + 1], M8[:, 1, tt, 0:1], -1.0, None, ALU.mult))
                chain(lambda e, tt=tt: e.activation(M8[:, 0, tt, 0:2], M8[:, 1, tt, 0:2], ACT.Exp, bias=sc[:, 3, tt:tt + 1],
                                                    accum_out=sc[:, 4, tt:tt + 1]), act)
                chain(lambda e, tt=tt: e.reciprocal(sc[:, 5, tt:tt + 1], sc[:, 4, tt:tt + 1]))
                chain(lambda e, tt=tt: e.tensor_scalar(M8[:, 0, tt, 0:2], M8[:, 0, tt, 0:2], sc[:, 5, tt:tt + 1],
                                                       sc[:, 2, tt:tt + 1], ALU.mult, ALU.mult))
                for k in range(2):
                    chain(lambda e, tt=tt, k=k: e.tensor_scalar(OE[:, k, tt, :], io[:, 0:8], XF[:, 1, tt, k:k + 1],
                                                                M8[:, 0, tt, k:k + 1], ALU.is_equal, ALU.mult))
                chain(lambda e, tt=tt: e.tensor_tensor(OE[:, 0, tt, :], OE[:, 0, tt, :], OE[:, 1, tt, :], ALU.add))
                chain(lambda e, tt=tt: e.tensor_tensor(CB[:, tt, :, :], bc(OE[:, 0, tt, :].unsqueeze(1), [128, 4, 8]),
                                                       bc(OG[:, tt, :].unsqueeze(2), [128, 4, 8]), ALU.mult))
            bar()
            moe_dense(CB)
            bar()
            for tt in range(2):
                for j in range(2):
                    h = H[:, tt, j * 512:(j + 1) * 512]
                    dve.do(lambda e, h=h, b=2 * tt + j: e.tensor_tensor(h, P(b), h, ALU.add))
            bar()
            last_norm(rw["fin1"], H)
            bar()

        def moe_dense(CB):
            SG = w2(1024, "p (t n) -> p t n", t=2)
            HM = w2(1024, "p (t n) -> p t n", t=2)
            HT = w2(1024, "p (t c n) -> p t c n", t=2, c=4)
            free = {b: None for b in range(4, 8)}
            ht_free = [None, None]
            for ex in range(32):
                g, tg, sg_ = unit(w_gate[ex].rearrange("(p c) n -> p (c n)", c=8), "p (c n) -> p c n", c=8)
                u, tu, su_ = unit(w_up[ex].rearrange("(p c) n -> p (c n)", c=8), "p (c n) -> p c n", c=8)
                d, td, sd_ = unit(w_down[ex].rearrange("(p c) n -> p (c n)", c=4), "p (c n) -> p c n", c=4)
                hm = []
                for tt in range(2):
                    x8 = lambda c: NT[:, c, tt * 128:tt * 128 + 128]
                    a = proj(P(4 + 2 * tt), x8, lambda c: g[:, c, :], 8, tg, free[4 + 2 * tt])
                    b = proj(P(5 + 2 * tt), x8, lambda c: u[:, c, :], 8, tu, free[5 + 2 * tt])
                    s = act.do(lambda e, tt=tt: e.activation(SG[:, tt, :], P(4 + 2 * tt), ACT.Silu), a)
                    h = dve.do(lambda e, tt=tt, ex=ex: e.scalar_tensor_tensor(
                        HM[:, tt, :], SG[:, tt, :], CB[:, tt, ex // 8, ex % 8:ex % 8 + 1], P(5 + 2 * tt), ALU.mult, ALU.mult),
                        s, b)
                    hm.append(h)
                    free[5 + 2 * tt] = h
                done(sg_, a)
                done(su_, b)
                for tt in range(2):
                    for c in range(4):
                        t = pe.do(tr(P(4 + 2 * tt)[:, c * 128:(c + 1) * 128], HM[:, tt, c::4]), hm[tt])
                    k = act.do(lambda e, tt=tt: e.activation(HT[:, tt, :, :], P(4 + 2 * tt).rearrange("p (c n) -> p c n", c=4),
                                                             ACT.Copy), t)
                    free[4 + 2 * tt] = k
                    for j in range(2):
                        for c in range(4):
                            t = pe.do(mm(P(2 * tt + j), HT[:, tt, c, :], d[:, c, j * 512:(j + 1) * 512],
                                         ex == 0 and c == 0, ex == 31 and c == 3), k, td)
                done(sd_, t)

        def last_norm(gain, dst):
            ts = [square_sum(H[:, tt, :], XS[:, tt, :], ST[:, tt:tt + 1]) for tt in range(2)]
            r = rstd(ST[:, 0:2], 2, D, *ts)
            for tt in range(2):
                dve.do(lambda e, tt=tt: e.scalar_tensor_tensor(dst[:, tt, :], H[:, tt, :], ST[:, tt:tt + 1], gain,
                                                               ALU.mult, ALU.mult), r)

        def mixers2():
            wk.reset()
            w2.reset()
            norm_turn(H, NT, sm["g_nmix"])
            qT = wk(1024, "p (m t) -> p m t", m=4)
            kT = wk(1024, "p (m t) -> p m t", m=4)
            VA = wk(1024, "p (t n) -> p t n", t=2)
            OAT = wk(1024, "p (m t) -> p m t", m=4)
            OBT = wk(1024, "p (m t) -> p m t", m=4)
            S = wk(4 * 384, "p (i n) -> p i n", i=4)
            PT = wk(4 * 384, "p (i n) -> p i n", i=4)
            VB = wk(560, "p (t n) -> p t n", t=2)
            lm = wk(8)
            mx = wk(64, "p (i t) -> p i t", t=2)
            den = wk(64, "p (i t) -> p i t", t=2)
            lam = sm["lam"]
            for i in range(2):
                a = lam[:, 128 * i:128 * i + 64]
                b = lam[:, 128 * i + 64:128 * i + 128]
                t = dve.do(lambda e, i=i, a=a, b=b: e.tensor_tensor_reduce(S[:, i, 0:64], a, b, 1.0, 0.0, ALU.mult, ALU.add,
                                                                           lm[:, i:i + 1]))
            t = act.do(lambda e: e.activation(lm[:, 2:4], lm[:, 0:2], ACT.Exp), t)
            t = dve.do(lambda e: e.tensor_scalar(lm[:, 4:5], lm[:, 3:4], lm[:, 2:3], -0.2, ALU.subtract, ALU.add), t)
            t_lam = t

            proj_turned(w8(w_in2, 0), NT, qT, [0, 1], 0.125)
            proj_turned(w8(w_in2, 1), NT, kT, [2, 3])
            proj_tokens(w8(w_in2, 2), NT, [4, 5], copy_out(VA))
            bar()

            scores_bank = [0]
            s_free = [[] for _ in range(4)]

            def softmax_map(i, lq, rk, slope):
                b = scores_bank[0] % 2
                scores_bank[0] += 1
                pe.raw(mm(P(b)[:, 0:128], lq(0), rk(0, 128), True, True), *bank_free[b])
                t = pe.do(mm(P(b)[:, 128:384], lq(1), rk(0, 256), True, True))
                s = S[:, i % 4, :]
                t = dve.do(lambda e: e.scalar_tensor_tensor(s, co["dist"], slope, P(b)[:, 0:384], ALU.mult, ALU.add),
                           t, *s_free[i % 4])
                bank_free[b] = [t]
                for tt, cs in ((0, slice(0, 128)), (1, slice(128, 384))):
                    m = dve.do(lambda e, tt=tt, cs=cs: e.tensor_reduce(mx[:, i, tt:tt + 1], s[:, cs], AX, ALU.max, negate=True), t)
                    k = act.do(lambda e, tt=tt, cs=cs: e.activation(s[:, cs], s[:, cs], ACT.Exp, bias=mx[:, i, tt:tt + 1],
                                                                    accum_out=den[:, i, tt:tt + 1]), m)
                return k

            turn_bank = [0]
            pt_free = [[] for _ in range(4)]

            def turn_map(i, *tokens):
                b = 2 + turn_bank[0] % 2
                turn_bank[0] += 1
                for j in range(3):
                    t = pe.do(tr(P(b)[:, j * 128:(j + 1) * 128], S[:, i % 4, j * 128:(j + 1) * 128]), *tokens, *bank_free[b])
                s_free[i % 4] = [t]
                k = act.do(lambda e: e.activation(PT[:, i % 4, :], P(b)[:, 0:384], ACT.Copy), t, *pt_free[i % 4])
                bank_free[b] = [k]
                return k

            for h in range(4):
                ks = []
                for c in range(2):
                    r = slice(64 * c, 64 * c + 64)
                    ks.append(softmax_map(2 * h + c, lambda t: qT[r, h, t * 128:t * 128 + 128], lambda a, z: kT[r, h, a:z],
                                          float(2.0 ** (-2.0 * (h + 1)))))
                i = 2 * h
                t = dve.do(lambda e, i=i: e.reciprocal(den[:, i:i + 2, :], den[:, i:i + 2, :]), *ks)
                t = dve.do(lambda e, i=i: e.tensor_scalar(den[:, i + 1, :], den[:, i + 1, :], lm[:, 4:5], None, ALU.mult), t, t_lam)
                for tt, cs in ((0, slice(0, 128)), (1, slice(128, 384))):
                    s0, s1 = S[:, i % 4, cs], S[:, (i + 1) % 4, cs]
                    a = dve.do(lambda e, i=i, tt=tt, s1=s1: e.tensor_scalar(s1, s1, den[:, i + 1, tt:tt + 1], None, ALU.mult), t)
                    a = dve.do(lambda e, i=i, tt=tt, s0=s0, s1=s1: e.scalar_tensor_tensor(s0, s0, den[:, i, tt:tt + 1], s1,
                                                                                         ALU.mult, ALU.add), a)
                s_free[(i + 1) % 4] = [a]
                k = turn_map(i, a)
                cs = slice(h * 128, h * 128 + 128)
                p = PT[:, i % 4, :]
                pe.raw(mm(P(4)[:, cs], p[:, 0:128], VA[:, 0, cs], True, True), k)
                pe.raw(mm(P(5)[:, cs], p[:, 128:256], VA[:, 0, cs], True, False))
                t = pe.do(mm(P(5)[:, cs], p[:, 256:384], VA[:, 1, cs], False, True))
                pt_free[i % 4] = [t]
            ts = []
            for tt in range(2):
                for h in range(4):
                    ts.append(square_sum(P(4 + tt)[:, h * 128:h * 128 + 128], XS[:, tt, h * 128:h * 128 + 128],
                                         ST[:, 16 + 4 * tt + h:17 + 4 * tt + h], t))
            r = rstd(ST[:, 16:24], 8, 128, *ts)
            for tt in range(2):
                v = XS[:, tt, 0:512].rearrange("p (h d) -> p h d", h=4)
                a = dve.do(lambda e, tt=tt, v=v: e.tensor_tensor(
                    v, P(4 + tt).rearrange("p (h d) -> p h d", h=4),
                    bc(ST[:, 16 + 4 * tt:20 + 4 * tt].unsqueeze(2), [128, 4, 128]), ALU.mult), r)
            bar()
            turn_all(XS, OAT, 4, lambda c: sm["g_sub"], 6, False, a)
            bar()
            toks = dve.do(lambda e: e.tensor_scalar(OAT, OAT, 0.8, None, ALU.mult))
            qB, kV = qT, kT
            proj_turned(w8(w_in2, 3), NT, qB, [4, 5], 0.125)
            proj_turned(w8(w_in2, 4), NT, kV, [6, 7])
            proj_tokens(unit(w_in2[5][:, 0:8 * 512], "p (c n) -> p c n", c=8), NT, [4, 5],
                        lambda tt, o, t: act.do(lambda e: e.activation(VB[:, tt, :], o, ACT.Copy), t), ncol=280)
            bar()
            GT = w2(48, "p (t n) -> p t n", t=2)
            act.do(lambda e: e.activation(GT, VB[:, :, 256:280], ACT.Sigmoid))
            KP = w2(512, "p (g c l) -> p g c l", g=2, c=8)
            HID = w2(64, "p (b h n) -> p b h n", b=2, h=2)
            CK2 = w2(256, "p (b h n) -> p b h n", b=2, h=2)
            KCT = w2(8)
            VC = w2(128, p=8)
            BDV = w2(512, p=64)
            SC = w2(128, "p (t h c) -> p t h c", t=2, h=8)
            CS = w2(64, "p (k t h) -> p k t h", k=4, t=2)
            PCT = w2(256, p=64)
            t_c2 = load(act, CK2, ck2.rearrange("p (b h n) -> p b h n", b=2, h=2))
            tk = dve.do(lambda e: e.tensor_tensor(KP[:, :, :, :].rearrange("p g c l -> p (g c) l"),
                                                  kV[:, 0:2, :].rearrange("p g (c l) -> p (g c) l", l=32),
                                                  bc(sm["pos"].unsqueeze(1), [128, 16, 32]), ALU.add))
            ua = unit(ck1[0], "p (l n) -> p l n", l=16)
            ub = unit(ck1[1], "p (l n) -> p l n", l=16)
            for ht in range(2):
                for l in range(32):
                    w = (ua, ub)[l // 16]
                    for b in range(2):
                        r = slice(64 * b, 64 * b + 64)
                        t = pe.do(mm(P(b)[:, ht * 16:ht * 16 + 16].rearrange("p (g c) -> p g c", g=2),
                                     w[0][r, l % 16, ht * 128:ht * 128 + 128], KP[r, :, :, l], l == 0, l == 31), w[1], tk)
            done(ua[2], t)
            done(ub[2], t)
            for b in range(2):
                t2 = act.do(lambda e, b=b: e.activation(HID[:, b, :, :], P(b)[:, 0:32].rearrange("p (h n) -> p h n", h=2), ACT.Gelu), t)
            for g in range(2):
                r = slice(64 * g, 64 * g + 64)
                for ht in range(2):
                    pe.raw(mm(P(2)[r, 0:8], CK2[:, 0, ht, :], HID[:, 0, ht, g * 8:g * 8 + 8], ht == 0, ht == 1), t2, t_c2)
                for ht in range(2):
                    t = pe.do(mm(P(3)[0:8, g * 64:g * 64 + 64], HID[:, 1, ht, g * 8:g * 8 + 8], CK2[:, 1, ht, :], ht == 0, ht == 1))
            t1 = act.do(lambda e: e.activation(KCT, P(2)[:, 0:8], ACT.Copy), t)
            t2 = act.do(lambda e: e.activation(VC, P(3)[0:8, 0:128], ACT.Copy), t)
            vcb = bc(VC.rearrange("p (g d) -> p g d", g=2).unsqueeze(2), [8, 2, 4, 64])
            t = pe.do(mm(P(4)[0:64, :].rearrange("p (g r d) -> p g r d", g=2, r=4), co["esel"][0:8, :], vcb, True, True), t2)
            t_bd = dve.do(lambda e: e.tensor_tensor(BDV, P(4)[0:64, :], co["bd"][0:64, :], ALU.mult), t)
            for tt in range(2):
                for h in range(8):
                    r = slice(64 * (h // 4), 64 * (h // 4) + 64)
                    t = pe.do(mm(P(h // 4)[:, tt * 32 + h % 4 * 8:tt * 32 + h % 4 * 8 + 8], qB[r, h % 4, tt * 128:tt * 128 + 128],
                                 KCT[r, :], True, True), t1)
            scf = SC.rearrange("p t h c -> p (t h) c")

            def chain(f, q=dve):
                nonlocal t
                t = q.do(f, t)
            for g in range(2):
                chain(lambda e, g=g: e.tensor_tensor(
                    SC[:, :, 4 * g:4 * g + 4, :].rearrange("p t h c -> p t (h c)"), P(g)[:, 0:64].rearrange("p (t a) -> p t a", t=2),
                    co["cmpb"].rearrange("p (t a) -> p t a", t=2)[:, :, 32 * g:32 * g + 32], ALU.add))
            csf = [CS[:, k, :, :].rearrange("p t h -> p (t h)") for k in range(4)]
            chain(lambda e: e.tensor_reduce(csf[0], scf, AX, ALU.max))
            chain(lambda e: e.tensor_tensor(scf, scf, bc(csf[0].unsqueeze(2), [128, 16, 8]), ALU.subtract))
            chain(lambda e: e.activation(scf, scf, ACT.Exp), act)
            chain(lambda e: e.tensor_reduce(csf[1], scf, AX, ALU.add))
            chain(lambda e: e.reciprocal(csf[2], csf[1]))
            g3 = GT.rearrange("p t (h j) -> p (t h) j", j=3)
            chain(lambda e: e.tensor_tensor(csf[3], csf[2], g3[:, :, 0], ALU.mult))
            for tt in range(2):
                chain(lambda e, tt=tt: e.tensor_tensor(SC[:, tt, :, :], SC[:, tt, :, :],
                                                       bc(co["cmpv"][:, tt * 8:tt * 8 + 8].unsqueeze(1), [128, 8, 8]), ALU.mult))
            chain(lambda e: e.tensor_tensor(scf, scf, bc(csf[3].unsqueeze(2), [128, 16, 8]), ALU.mult))
            for tt in range(2):
                t3 = pe.do(tr(P(4)[0:64, tt * 128:tt * 128 + 128], SC[:, tt, :, :].rearrange("p h c -> p (h c)")), t, t_bd)
            t3 = act.do(lambda e: e.activation(PCT, P(4)[0:64, 0:256], ACT.Copy), t3)
            for m in range(4):
                t = pe.do(mm(P(6 + m // 2)[:, (m % 2) * 256:(m % 2) * 256 + 256], BDV[:, m * 128:m * 128 + 128], PCT,
                             m % 2 == 0, False), t3, t_bd)
            bar()
            for i in range(16):
                j, h = i // 8, i % 8
                g = h // 4
                r = slice(64 * g, 64 * g + 64)
                k = softmax_map(i, lambda t: qB[r, h % 4, t * 128:t * 128 + 128], lambda a, z: kV[r, 2 + j, a:z],
                                float(2.0 ** -(h + 1.0)))
                t = dve.do(lambda e, i=i: e.reciprocal(den[:, i, :], den[:, i, :]), k)
                t = dve.do(lambda e, i=i, h=h, j=j: e.tensor_tensor(den[:, i, :], den[:, i, :], GT[:, :, h * 3 + 1 + j], ALU.mult), t)
                for tt, cs in ((0, slice(0, 128)), (1, slice(128, 384))):
                    s = S[:, i % 4, cs]
                    a = dve.do(lambda e, i=i, tt=tt, s=s: e.tensor_scalar(s, s, den[:, i, tt:tt + 1], None, ALU.mult), t)
                k = turn_map(i, a)
                o = P(6 + h // 4)[(h % 2) * 64:(h % 2) * 64 + 64, (h // 2 % 2) * 256:(h // 2 % 2) * 256 + 256]
                vs = slice(128 * j + 64 * g, 128 * j + 64 * g + 64)
                p = PT[:, i % 4, :]
                pe.raw(mm(o, VB[:, 0, vs], p[:, 0:256], False, False), k)
                t = pe.do(mm(o[:, 128:256], VB[:, 1, vs], p[:, 256:384], False, i == 15))
                pt_free[i % 4] = [t]
            for m in range(4):
                act.do(lambda e, m=m: e.activation(OBT[:, m, :], P(6 + m // 2)[:, (m % 2) * 256:(m % 2) * 256 + 256], ACT.Copy), t)
            bar()
            SGA = w2(2048, "p (t n) -> p t n", t=2)
            SGB = w2(2048, "p (t n) -> p t n", t=2)
            for j in range(4):
                dst = (SGA, SGB)[j // 2]

                def evac(tt, o, t, dst=dst, j=j):
                    return act.do(lambda e: e.activation(dst[:, tt, (j % 2) * 512:(j % 2) * 512 + 512], o, ACT.Sigmoid), t)
                proj_tokens(w8(w_in2, 6 + j), NT, [2 * (j % 2), 2 * (j % 2) + 1], evac)
            ua = unit(w_a.rearrange("(c p) n -> p c n", c=4), "p (c n) -> p c n", c=4)
            ub = unit(w_b.rearrange("(c p) n -> p c n", c=4), "p (c n) -> p c n", c=4)
            bf = [[], []]
            for tt in range(2):
                for j in range(2):
                    cs = slice(j * 512, j * 512 + 512)
                    a = proj(P(4 + j), lambda c: OAT[:, c, tt * 128:tt * 128 + 128], lambda c: ua[0][:, c, cs], 4, ua[1], *bf[j])
                    b = proj(P(6 + j), lambda c: OBT[:, c, tt * 128:tt * 128 + 128], lambda c: ub[0][:, c, cs], 4, ub[1], *bf[j])
                    t1 = dve.do(lambda e, tt=tt, cs=cs, j=j: e.tensor_tensor(SGA[:, tt, cs], SGA[:, tt, cs], P(4 + j), ALU.mult),
                                a, act.last())
                    t2 = dve.do(lambda e, tt=tt, cs=cs, j=j: e.tensor_tensor(SGB[:, tt, cs], SGB[:, tt, cs], P(6 + j), ALU.mult), b)
                    bf[j] = [t1, t2]
                    t = dve.do(lambda e, tt=tt, cs=cs: e.tensor_tensor(XS[:, tt, cs], SGA[:, tt, cs], SGB[:, tt, cs], ALU.add), t1, t2)
            done(ua[2], a)
            done(ub[2], b)
            bar()
            turn_all(XS, NT, 8, None, 0, True)
            bar()
            add_residual(NT, [w8(w_out2, 0), w8(w_out2, 1)], 8)
            bar()

        def cross():
            wk.reset()
            w2.reset()
            MT = w2(2048, "p (c t) -> p c t", c=8)
            MM = w2(2048, "p (t d) -> p t d", t=2)
            t = load(act, MM, mem.rearrange("(t p) d -> p t d", p=128), dve.last(), pe.last(), pool.last())
            act.wait(t)
            dve.wait(t)
            norm_turn(MM, MT, sm["g_mem"])
            norm_turn(H, NT, sm["g_cross"])
            qT = wk(1024, "p (m t) -> p m t", m=4)
            kT = wk(1024, "p (m t) -> p m t", m=4)
            V = wk(1024, "p (t n) -> p t n", t=2)
            OT = wk(1024, "p (m t) -> p m t", m=4)
            mx = wk(8)
            den = wk(8)
            proj_turned(w8(w_cq, 0), NT, qT, [0, 1])
            proj_turned(w8(w_ckv, 0), MT, kT, [2, 3])
            proj_tokens(w8(w_ckv, 1), MT, [4, 5], copy_out(V))
            bar()
            S = w2(2048, "p (t h n) -> p t h n", t=2, h=4)
            PT = w2(2048, "p (m h n) -> p m h n", m=2, h=4)
            sc = float(128 ** -0.5)
            for tt in range(2):
                for h in range(4):
                    t = pe.do(mm(P(2 * tt + h // 2)[:, (h % 2) * 256:(h % 2) * 256 + 256], qT[:, h, tt * 128:tt * 128 + 128],
                                 kT[:, h, :], True, True))
            t = dve.do(lambda e: e.tensor_reduce(mx, P(0, 4).rearrange("p (a n) -> p a n", n=256), AX, ALU.max), t)
            t = dve.do(lambda e: e.tensor_scalar(mx, mx, -sc, None, ALU.mult), t)
            for a in range(8):
                k = act.do(lambda e, a=a: e.activation(S[:, a // 4, a % 4, :], P(a // 2)[:, (a % 2) * 256:(a % 2) * 256 + 256],
                                                       ACT.Exp, bias=mx[:, a:a + 1], scale=sc, accum_out=den[:, a:a + 1]), t)
            t = dve.do(lambda e: e.reciprocal(den, den), k)
            for a in range(8):
                s = S[:, a // 4, a % 4, :]
                t1 = dve.do(lambda e, a=a, s=s: e.tensor_scalar(s, s, den[:, a:a + 1], None, ALU.mult), t)
            for m in range(2):
                for pair in range(2):
                    o = P(4 + 2 * m + pair).rearrange("p (h t) -> p h t", h=2)
                    for h in range(2):
                        for tt in range(2):
                            t = pe.do(tr(o[:, h, tt * 128:tt * 128 + 128], S[:, tt, 2 * pair + h, m * 128:m * 128 + 128]), t1)
                    k = act.do(lambda e, m=m, pair=pair, o=o: e.activation(PT[:, m, 2 * pair:2 * pair + 2, :], o, ACT.Copy), t)
            for h in range(4):
                o = P(h // 2)[:, (h % 2) * 256:(h % 2) * 256 + 256]
                pe.raw(mm(o, V[:, 0, h * 128:h * 128 + 128], PT[:, 0, h, :], True, False), k)
                t = pe.do(mm(o, V[:, 1, h * 128:h * 128 + 128], PT[:, 1, h, :], False, True))
                if h % 2:
                    act.do(lambda e, h=h: e.activation(OT[:, h - 1:h + 1, :], P(h // 2).rearrange("p (h t) -> p h t", h=2),
                                                       ACT.Copy), t)
            bar()
            u = unit(w_co.rearrange("(c p) n -> p c n", c=4), "p (c n) -> p c n", c=4)
            for j in range(2):
                for tt in range(2):
                    cs = slice(j * 512, j * 512 + 512)
                    t = proj(P(2 + 2 * j + tt), lambda c: OT[:, c, tt * 128:tt * 128 + 128], lambda c: u[0][:, c, cs], 4, u[1])
                    dve.do(lambda e, j=j, tt=tt, cs=cs: e.tensor_tensor(H[:, tt, cs], P(2 + 2 * j + tt), H[:, tt, cs], ALU.add), t)
            done(u[2], t)
            bar()

        def peer():
            wk.reset()
            w2.reset()
            norm_turn(H, NT, sm["g_peer"])
            RG = wk(8192)
            b1 = Bump(Wk, 0, 8192)
            I1T, I2T, GTT = wk(256), wk(256), wk(256)
            SK = b1(2048, "p (a n) -> p a n", a=16)
            QP = b1(1024, "p (a t) -> p a t", a=4)
            TS = b1(512, "p (a k) -> p a k", a=32)
            TF = b1(512, "p (a k) -> p a k", a=32)
            TIi = b1(512, "p (a k) -> p a k", a=32).bitcast(U32)
            BS = b1(256, "p (a k) -> p a k", a=16)
            BJ = b1(256, "p (a k) -> p a k", a=16).bitcast(U32)
            BA = b1(256, "p (a k) -> p a k", a=16).bitcast(U32)
            BF = b1(512, "p (c a k) -> p c a k", c=2, a=16)
            BG = b1(256, "p (a k) -> p a k", a=16)
            II = b1(512, "p (c t n) -> p c t n", c=2, t=2)
            gs = b1(32, "p (k a) -> p k a", k=2)
            S = w2(4096, "p (a n) -> p a n", a=32)
            CA = w2(4096, "p (a n) -> p a n", a=16)
            t_sk = load(act, SK, subk.rearrange("p (a n) -> p a n", a=16), dve.last(), pe.last(), pool.last())
            qp_free = [[] for _ in range(4)]
            for ui in range(4):
                w, tw, slot = w8(w_pq, ui)
                for m in range(4):
                    hc = ui * 4 + m
                    b = hc % 4
                    o = P(b)[:, 0:256]
                    t = proj(o, lambda c: w[:, c, m * 128:(m + 1) * 128], lambda c: NT[:, c, :], 8, tw, *bank_free[b])
                    k = act.do(lambda e, m=m, o=o: e.activation(QP[:, m, :], o, ACT.Copy), t, *qp_free[m])
                    bank_free[b] = [k]
                    b = 4 + hc % 4
                    for tt in range(2):
                        t2 = pe.do(mm(P(b)[:, tt * 128:tt * 128 + 128], QP[:, m, tt * 128:tt * 128 + 128], SK[:, hc, :], True, True),
                                   k, t_sk, *bank_free[b])
                    qp_free[m] = [t2]
                    v = S.rearrange("p (t a) n -> p t a n", t=2)[:, :, hc, :]
                    k = act.do(lambda e, v=v, b=b: e.activation(v, P(b)[:, 0:256].rearrange("p (t n) -> p t n", t=2), ACT.Copy), t2)
                    bank_free[b] = [k]
                done(slot, t)
            bar()

            def top16(src, vals, idx, n):
                for a in range(n):
                    t = dve.do(lambda e, a=a: e.max(vals[:, a, 0:8], src[:, a, :]))
                dve.wait(t)
                for a in range(n):
                    t = dve.do(lambda e, a=a: e.max_index(idx[:, a, 0:8], vals[:, a, 0:8], src[:, a, :]))
                dve.wait(t)
                for a in range(n):
                    t = dve.do(lambda e, a=a: e.match_replace(src[:, a, :], vals[:, a, 0:8], src[:, a, :], -3e38))
                dve.wait(t)
                for a in range(n):
                    t = dve.do(lambda e, a=a: e.max(vals[:, a, 8:16], src[:, a, :]))
                dve.wait(t)
                for a in range(n):
                    t = dve.do(lambda e, a=a: e.max_index(idx[:, a, 8:16], vals[:, a, 8:16], src[:, a, :]))
                dve.wait(t)

            top16(S, TS, TIi, 32)
            t = dve.do(lambda e: e.tensor_copy(TF, TIi))
            ts5 = TS.rearrange("p (t h c) k -> p t h c k", t=2, c=2)
            for tt in range(2):
                v = CA.rearrange("p (t h) (a b) -> p t h a b", t=2, a=16)[:, tt]
                t = dve.do(lambda e, v=v, tt=tt: e.tensor_tensor(v, bc(ts5[:, tt, :, 0, :].unsqueeze(3), [128, 8, 16, 16]),
                                                                 bc(ts5[:, tt, :, 1, :].unsqueeze(2), [128, 8, 16, 16]), ALU.add), t)
            dve.wait(t)
            top16(CA, BS, BJ, 16)

            def chain(f, q=dve):
                nonlocal t
                t = q.do(f, t)
            chain(lambda e: e.tensor_tensor(BG, BS, bc(BS[:, :, 0:1], [128, 16, 16]), ALU.subtract))
            chain(lambda e: e.activation(BG, BG, ACT.Exp), act)
            chain(lambda e: e.tensor_reduce(gs[:, 0, :], BG, AX, ALU.add))
            chain(lambda e: e.reciprocal(gs[:, 1, :], gs[:, 0, :]))
            chain(lambda e: e.tensor_tensor(BG, BG, bc(gs[:, 1, :].unsqueeze(2), [128, 16, 16]), ALU.mult))
            chain(lambda e: e.tensor_scalar(BA, BJ, 4, None, ALU.logical_shift_right))
            chain(lambda e: e.tensor_copy(BF[:, 0], BA))
            chain(lambda e: e.tensor_scalar(BA, BJ, 15, None, ALU.bitwise_and))
            chain(lambda e: e.tensor_copy(BF[:, 1], BA))
            tf5 = TF.rearrange("p (t h c) k -> p t h c k", t=2, c=2)
            EQ = S.rearrange("p (z a) n -> p z (a n)", z=2)
            for c in range(2):
                for tt in range(2):
                    q = EQ[:, tt, :].rearrange("p (h k a) -> p h k a", h=8, k=16)
                    bf = BF[:, c].rearrange("p (t h) k -> p t h k", t=2)[:, tt]
                    chain(lambda e, q=q, bf=bf: e.tensor_tensor(q, bc(bf.unsqueeze(3), [128, 8, 16, 16]),
                                                                bc(co["iota"][:, 0:16].unsqueeze(1).unsqueeze(1), [128, 8, 16, 16]),
                                                                ALU.is_equal))
                    chain(lambda e, q=q, tt=tt, c=c: e.tensor_tensor(q, q, bc(tf5[:, tt, :, c, :].unsqueeze(2), [128, 8, 16, 16]),
                                                                     ALU.mult))
                    chain(lambda e, q=q, tt=tt, c=c: e.tensor_reduce(II[:, c, tt, :].rearrange("p (h k) -> p h k", h=8), q, AX,
                                                                     ALU.add))
            bg = BG.rearrange("p (t h) k -> p t (h k)", t=2)
            for n, (src, dst) in enumerate(((II[:, 0], I1T), (II[:, 1], I2T), (bg, GTT))):
                for tt in range(2):
                    t1 = pe.do(tr(P(n)[:, tt * 128:tt * 128 + 128], src[:, tt, :]), t)
                act.do(lambda e, n=n, dst=dst: e.activation(dst, P(n)[:, 0:256], ACT.Copy), t1)
            bar()

            C = AR[:, :].rearrange("p (t n) -> p t n", t=256)
            OA = XSs[:, 0:1024].rearrange("p (b k n) -> p b k n", b=2, k=4)
            OB = XSs[:, 1024:2048].rearrange("p (b k n) -> p b k n", b=2, k=4)
            io = co["iota"]
            oh_free, pf = [None, None], [None] * 4
            for g in range(64):
                b = g % 2
                for k in range(4):
                    tok = g * 4 + k
                    ta = dve.do(lambda e, b=b, k=k, tok=tok: e.tensor_scalar(OA[:, b, k, :], io, I1T[:, tok:tok + 1],
                                                                            GTT[:, tok:tok + 1], ALU.is_equal, ALU.mult), oh_free[b])
                    tb = pool.do(lambda e, b=b, k=k, tok=tok: e.tensor_scalar(OB[:, b, k, :], io, I2T[:, tok:tok + 1], None,
                                                                             ALU.is_equal), oh_free[b])
                pb = 4 + g % 4
                for k in range(4):
                    t = pe.do(mm(P(pb)[:, k * 128:k * 128 + 128], OA[:, b, k, :], OB[:, b, k, :], True, True), ta, tb, pf[g % 4])
                oh_free[b] = t
                pf[g % 4] = act.do(lambda e, g=g, pb=pb: e.activation(C[:, 4 * g:4 * g + 4, :],
                                                                     P(pb).rearrange("p (k n) -> p k n", k=4), ACT.Copy), t)
            t_c = act.last()
            first = [dve.last(), pe.last(), act.last()]
            UR = RG[:, 0:4096].rearrange("p (b c n) -> p b c n", b=4, c=8)
            VR = RG[:, 4096:8192].rearrange("p (b n) -> p b n", b=4)
            us, vs = [sem(f"us{i}") for i in range(4)], [sem(f"vs{i}") for i in range(4)]
            GE = XSs[:, 0:512].rearrange("p (b n) -> p b n", b=2)
            WT = XSs[:, 512:1024].rearrange("p (b n) -> p b n", b=2)
            u_free = [first] * 4
            v_free = [first] * 4
            s_tok, w_tok = {}, {}
            ge_free, wt_free, sf = [None] * 2, [None] * 2, [pf[i] for i in range(4)]
            dve.wait(t_c)

            def stage1(i):
                s = i % 4
                sp.raw(lambda e: e.dma_start(UR[:, s], peer_u[i].rearrange("p (c n) -> p c n", c=8)).then_inc(us[s], 16), *u_free[s])
                sp.raw(lambda e: e.dma_start(VR[:, s], peer_v[:, i, :]).then_inc(vs[s], 16), *v_free[s])
                o = P(4 + s)[:, 0:256]
                t = proj(o, lambda c: UR[:, s, c, :], lambda c: NT[:, c, :], 8, (us[s], 16 * (i // 4 + 1)), sf[s])
                u_free[s] = [t]
                b = i % 2
                a = act.do(lambda e: e.activation(GE[:, b, :], o, ACT.Gelu), t, ge_free[b], oh_free[0], oh_free[1])
                sf[s] = a
                w = dve.do(lambda e: e.tensor_tensor(WT[:, b, :], GE[:, b, :], C[:, :, i], ALU.mult), a, wt_free[b])
                ge_free[b] = w
                w_tok[i] = w

            def stage2(i):
                s, b = i % 4, i % 2
                for tt in range(2):
                    for j in range(2):
                        t = pe.do(mm(P(2 * tt + j), WT[:, b, tt * 128:tt * 128 + 128], VR[:, s, j * 512:j * 512 + 512],
                                     i == 0, i == 127), w_tok[i], (vs[s], 16 * (i // 4 + 1)))
                v_free[s] = [t]
                wt_free[b] = t

            for i in range(128):
                stage1(i)
                if i:
                    stage2(i - 1)
            stage2(127)
            bar()
            for tt in range(2):
                for j in range(2):
                    h = H[:, tt, j * 512:(j + 1) * 512]
                    dve.do(lambda e, h=h, b=2 * tt + j: e.tensor_tensor(h, P(b), h, ALU.add))
            bar()
            last_norm(rw["fin2"], XS)

        for n, f in enumerate((mixers, experts, mixers2, cross, peer)):
            f()
            if stage == n + 1 and stage < 5:
                finish(H)
                break
        else:
            finish(None)
        emit()


def constants():
    import numpy as np
    p = np.arange(128)
    a = p[:, None]
    b = p[None, :]
    d = {}
    d["ident"] = (a == b)
    d["tri"] = (a <= b)
    d["neg"] = np.where(a < b, 0.0, -1e30)
    d["m01"] = (a < b)
    d["negu"] = -1.0 * (a >= b)
    d["neg1"] = -np.ones((128, 128))
    k2 = np.arange(256)[None, :]
    d["dist"] = np.concatenate([np.where(b <= a, b - a, -1e30), np.where(k2 <= a + 128, k2 - a - 128.0, -1e30)], 1)
    slope = 2.0 ** -np.arange(1.0, 9.0)
    cpos = np.arange(8) * 32 + 31
    q = np.stack([p, p + 128], 1)
    dc = q[:, :, None] - cpos
    d["cmpb"] = np.where(dc[:, :, None, :] >= 0, -slope[None, None, :, None] * dc[:, :, None, :], -1e30)
    d["cmpv"] = dc >= 0
    hc = np.arange(64)[:, None]
    bd = np.zeros((128, 512))
    bd[:64] = (hc // 8) == (np.arange(512)[None, :] // 64)
    d["bd"] = bd
    es = np.zeros((128, 64))
    es[:8] = (hc.T % 8) == np.arange(8)[:, None]
    d["esel"] = es
    d["iota"] = np.broadcast_to(b, (128, 128))
    return np.concatenate([np.asarray(d[k], np.float32).reshape(128, -1) for k in NC_CONST], 1)


def layout(i):
    import numpy as np
    f = {k: np.asarray(v) for k, v in i.items()}

    def pc(v):
        return v.reshape(128, -1)

    def tile(v):
        return np.broadcast_to(v.reshape(1, -1), (128, v.size))

    small = dict(g_attn=pc(f["attn_norm_g"][0]),
                 g_mix=pc(np.concatenate([f["sb_out_norm_g"][0], f["sg_out_norm_g"][0]])),
                 g_ffn=pc(f["ffn_norm_g"][0]), g_nmix=pc(f["norm_mix_2"][0]), g_sub=pc(f["diff_subln_2"][0]),
                 g_cross=pc(f["norm_cross_2"][0]), g_mem=pc(f["norm_mem_2"][0]), g_peer=pc(f["norm_ffn_2"][0]),
                 bsp=f["b_spatial"][0].T, pos=np.concatenate([f["nsa_cmp_pos_2"][0].T] * 2, 0),
                 lam=tile(f["diff_lambda_2"][0]),
                 rb=tile(np.concatenate([f["b_router_group"][0], f["b_router_expert"][0].reshape(-1)])))
    rows = dict(sg=tile(f["sg_norm_g"][0]), fin1=tile(f["final_norm_g"]), fin2=tile(f["norm_final_2"]))

    def units(w):
        return np.ascontiguousarray(w.reshape(128, 8, -1, 512).transpose(2, 0, 1, 3)).reshape(-1, 128, 4096)

    w2 = f["w_in_2"][0]
    qa, ka, va, qb, kv, gb, ga, gbb = np.split(w2, np.cumsum([512, 512, 512, 512, 768, 24, 1024]), axis=1)
    qb = qb.reshape(1024, 2, 4, 64).transpose(0, 2, 1, 3).reshape(1024, 512)
    kv = kv.reshape(1024, 6, 2, 64)
    kva = np.concatenate([kv[:, 0, 0], kv[:, 1, 0], kv[:, 0, 1], kv[:, 1, 1], kv[:, 2, 0], kv[:, 2, 1],
                          kv[:, 4, 0], kv[:, 4, 1]], 1)
    kvb = np.concatenate([kv[:, 3, 0], kv[:, 3, 1], kv[:, 5, 0], kv[:, 5, 1], gb, np.zeros((1024, 232), w2.dtype)], 1)
    w_in2 = units(np.concatenate([qa, ka, va, qb, kva, kvb, ga, gbb], 1))
    wr = np.concatenate([f["w_router_group"][0], f["w_router_expert"][0].transpose(1, 0, 2).reshape(1024, 32)], 1)
    c1 = np.concatenate([f["nsa_ck_w1_2"][0].reshape(32, 64, 256), f["nsa_cv_w1_2"][0].reshape(32, 64, 256)], 1)
    c1 = c1.reshape(2, 16, 128, 256).transpose(0, 2, 1, 3).reshape(2, 128, 4096)
    c2 = np.stack([f["nsa_ck_w2_2"][0].reshape(2, 128, 64), f["nsa_cv_w2_2"][0].reshape(2, 128, 64)], 0)
    a = dict(
        x=f["x"][0], const=constants(), small=np.concatenate([small[k] for k in NC_SMALL], 1),
        rows=np.concatenate([rows[k] for k in NC_ROWS], 1),
        w_in=units(f["w_in"][0]), w_sp=f["w_spatial"][0].transpose(2, 0, 1).reshape(128, 1024), w_out=units(f["w_out"][0]),
        w_r=wr.reshape(128, 288), w_gate=f["w_gate"].reshape(32, 1024, 512), w_up=f["w_up"].reshape(32, 1024, 512),
        w_down=f["w_down"].reshape(32, 512, 1024), mem=f["mem_2"][0], w_in2=w_in2, ck1=c1,
        ck2=c2.transpose(2, 0, 1, 3).reshape(128, 256), w_a=f["w_branch_a_2"][0], w_b=f["w_branch_b_2"][0],
        w_out2=units(f["w_out_2"][0]), w_cq=units(f["w_cross_q_2"][0]), w_ckv=units(f["w_cross_kv_2"][0]),
        w_co=f["w_cross_o_2"][0], w_pq=units(f["peer_wq_2"][0]),
        subk=f["peer_subkeys_2"][0].transpose(3, 0, 1, 2).reshape(128, 2048),
        peer_u=f["peer_u_2"][0].reshape(128, 128, 128, 8).transpose(1, 2, 3, 0).reshape(128, 128, 1024),
        peer_v=f["peer_v_2"][0].reshape(128, 128, 1024),
    )
    return {k: np.ascontiguousarray(v) for k, v in a.items()}


STAGE = 5


def kernel(**inputs):
    import numpy as np
    import concourse.bacc as bacc
    from concourse.bass_utils import run_bass_kernel_spmd

    nc = bacc.Bacc("TRN2", target_bir_lowering=False, num_devices=1)
    arrays, args = {}, {}
    for name, a in layout(inputs).items():
        arrays[f"in_{name}"] = a
        args[name] = nc.dram_tensor(f"in_{name}", a.shape, mybir.dt.from_np(a.dtype), kind="ExternalInput").ap()
    args["out"] = nc.dram_tensor("out_0", (256, D), F32, kind="ExternalOutput").ap()
    program(nc, STAGE, **args)
    r = run_bass_kernel_spmd(nc, [arrays], core_ids=[0])
    return np.asarray(r.results[0]["out_0"]).reshape(1, 256, D)
```

```python
from contextlib import ExitStack

import concourse.bass as bass
from concourse import mybir

F32 = mybir.dt.float32
F32R = mybir.dt.float32r
U32 = mybir.dt.uint32
ALU = mybir.AluOpType
ACT = mybir.ActivationFunctionType
AX = mybir.AxisListType.X

EPS = 1e-6
SLOTS = 64
D = 1024
NC_CONST = dict(ident=128, tri=128, neg=128, m01=128, negu=128, neg1=128, one=128, dist=384, cmpb=128, cmpv=16,
                bd=512, esel=64, iota=128)
NC_SMALL = dict(g_attn=8, g_mix=8, g_ffn=8, g_nmix=8, g_sub=1, g_cross=8, g_mem=8, g_peer=8, bsp=8, pos=32,
                lam=256, rb=36)
NC_ROWS = dict(sg=512, fin1=1024)


class Queue:

    def __init__(self, sem):
        self.sem, self.n, self.items, self.seen = sem, 0, [], {}

    def wait(self, *tokens):
        for t in tokens:
            if t is None:
                continue
            sem, v = t
            if self.seen.get(id(sem), 0) < v:
                self.seen[id(sem)] = v
                self.items.append(lambda e, sem=sem, v=v: e.wait_ge(sem, v))

    def raw(self, f, *tokens):
        self.wait(*tokens)
        self.items.append(f)

    def do(self, f, *tokens):
        self.wait(*tokens)
        self.n += 1
        self.items.append(lambda e: f(e).then_inc(self.sem, 1))
        return (self.sem, self.n)

    def last(self):
        return (self.sem, self.n) if self.n else None

    def branch(self, sem, flag):
        q = Queue(sem)
        q.seen = dict(self.seen)
        self.items.append((flag, q.items))
        return q


def replay(e, items):
    for f in items:
        if isinstance(f, tuple):
            v = e.value_load(f[0], min_val=0, max_val=1)
            with e.If(v > 0):
                replay(e, f[1])
        else:
            f(e)


def program(nc, stage, x, const, small, rows, w_in, w_sp, w_out, w_r, w_gate, w_up, w_down, mem, w_in2, ck1, ck2,
            w_a, w_b, w_out2, w_cq, w_ckv, w_co, w_pq, subk, peer_u, peer_v, fin2, out):
    ctx = ExitStack()
    with ctx:
        place = {}

        def sb(name, shape, dt=F32):
            t = ctx.enter_context(nc.sbuf_tensor(name, shape, dt))
            place[name] = nc.sbuf_base - 4 * shape[1]
            return t

        def rounded(name, over, at, n):
            return nc.alloc_sbuf_tensor_at(name, [128, n], F32R, offset=place[over] + 4 * at)

        def sem(name):
            return ctx.enter_context(nc.semaphore(name))

        NR = 6
        AR = sb("AR", [128, 8 * 4096])
        Wk = sb("Wk", [128, 9200])
        Hs = sb("Hs", [128, 2 * D])
        XSs = sb("XSs", [128, 2 * D])
        NTs = sb("NTs", [128, 8 * 256])
        CO = sb("CO", [128, sum(NC_CONST.values())])
        SM = sb("SM", [128, sum(NC_SMALL.values())])
        RW = sb("RW", [128, sum(NC_ROWS.values())])
        ST = sb("ST", [128, 64])
        PSt = ctx.enter_context(nc.psum_tensor("PS", [128, 8 * 512], F32))

        def parts(t, widths):
            at, d = 0, {}
            for k, n in widths.items():
                d[k] = t[:, at:at + n]
                at += n
            return d

        co, sm, rw = parts(CO, NC_CONST), parts(SM, NC_SMALL), parts(RW, NC_ROWS)
        ident = co["ident"]
        H = Hs[:, :].rearrange("p (t d) -> p t d", t=2)
        XS = XSs[:, :].rearrange("p (t d) -> p t d", t=2)
        NT = NTs[:, :].rearrange("p (c t) -> p c t", c=8)

        def P(b, n=1):
            return PSt[:, b * 512:(b + n) * 512]

        pe, act, dve, pool = (Queue(sem(f"s_{n}")) for n in ("pe", "act", "dve", "pool"))
        sp = Queue(sem("s_sp"))
        qs = (pe, act, dve, pool)

        def bar():
            for a in qs:
                for b in qs:
                    a.wait(b.last())

        nload = [0]

        def load(q, dst, src, *tokens):
            nload[0] += 1
            s = sem(f"ld{nload[0]}")
            q.raw(lambda e: e.dma_start(dst, src).then_inc(s, 16), *tokens)
            return (s, 16)

        ring_sem = [sem(f"ring{i}") for i in range(NR)]
        ring_n, ring_free = [0], [[] for _ in range(NR)]

        def unit(src, shape_str, **kw):
            n = ring_n[0]
            ring_n[0] += 1
            s = n % NR
            npart = src.shape[0]
            cols = 1
            for z in src.shape[1:]:
                cols *= z
            dst = AR[0:npart, s * 4096:s * 4096 + cols]
            to = dst.rearrange("p (a n) -> p a n", a=src.shape[1]) if len(src.shape) == 3 else dst
            sp.raw(lambda e: e.dma_start(to, src).then_inc(ring_sem[s], 16), *ring_free[s])
            return dst.rearrange(shape_str, **kw), (ring_sem[s], 16 * (n // NR + 1)), s

        def done(slot, *tokens):
            ring_free[slot] = list(tokens)

        class Bump:
            def __init__(self, t, lo, hi):
                self.t, self.lo, self.at, self.hi = t, lo, lo, hi

            def __call__(self, n, s=None, p=128, **kw):
                a = self.t[0:p, self.at:self.at + n]
                self.at += n
                assert self.at <= self.hi, (self.at, self.hi)
                return a.rearrange(s, **kw) if s else a

            def reset(self):
                self.at = self.lo

        wk = Bump(Wk, 0, 9200)
        w2 = Bump(AR, NR * 4096, 8 * 4096)

        def mm(o, l, r, start, stop):
            return lambda e: e.matmul(o, l, r, start=start, stop=stop, skip_group_check=True)

        def tr(o, i, n=128):
            return lambda e: e.transpose(o, i, ident[0:n, 0:n])

        def bc(ap, shape):
            return ap.broadcast_to(shape)

        t_x = load(act, H, x.rearrange("(t p) d -> p t d", p=128))
        t_co = load(act, CO[:, :], const)
        t_sm = load(act, SM[:, :], small)
        t_rw = load(act, RW[:, :], rows)
        for q in (pe, act, dve, pool):
            q.wait(t_x, t_co, t_sm, t_rw)

        def rstd(ss, n, width, *tokens):
            a = dve.do(lambda e: e.tensor_scalar(ss, ss, 1.0 / width, EPS, ALU.mult, ALU.add), *tokens)
            b = act.do(lambda e: e.activation(ss, ss, ACT.Sqrt), a)
            return dve.do(lambda e: e.reciprocal(ss, ss), b)

        def square_sum(src, junk, ss, *tokens):
            return act.do(lambda e: e.activation(junk, src, ACT.Square, accum_out=ss), *tokens)

        def turn_all(src, dst, nchunk, gain, first_bank, strided, *tokens):
            toks = []
            for pair in range(nchunk // 2):
                bank = P(first_bank + pair).rearrange("p (c t) -> p c t", c=2)
                for k in range(2):
                    c = 2 * pair + k
                    for tt in range(2):
                        s = src[:, tt, c::nchunk] if strided else src[:, tt, c * 128:(c + 1) * 128]
                        t = pe.do(tr(bank[:, k, tt * 128:(tt + 1) * 128], s), *tokens)
                if gain is None:
                    o = dst[:, 2 * pair:2 * pair + 2, :]
                    if pair % 2:
                        toks.append(act.do(lambda e, o=o, bank=bank: e.activation(o, bank, ACT.Copy), t))
                    else:
                        toks.append(dve.do(lambda e, o=o, bank=bank: e.tensor_copy(o, bank), t))
                else:
                    for k in range(2):
                        c = 2 * pair + k
                        toks.append(dve.do(lambda e, c=c, k=k, bank=bank: e.tensor_scalar(
                            dst[:, c, :], bank[:, k, :], gain(c), None, ALU.mult), t))
            return toks

        def norm_turn(src, dst, gain):
            ts = [square_sum(src[:, tt, :], XS[:, tt, :], ST[:, tt:tt + 1]) for tt in range(2)]
            r = rstd(ST[:, 0:2], 2, D, *ts)
            for tt in range(2):
                t = dve.do(lambda e, tt=tt: e.tensor_scalar(XS[:, tt, :], src[:, tt, :], ST[:, tt:tt + 1], None, ALU.mult), r)
            turn_all(XS, dst, 8, lambda c: gain[:, c:c + 1], 0, True, t)
            bar()

        def proj(o, lhs, rhs, n, *tokens, q=pe):
            q.wait(*tokens)
            for c in range(n):
                f = mm(o, lhs(c), rhs(c), c == 0, c == n - 1)
                if c < n - 1:
                    q.raw(f)
                else:
                    return q.do(f)

        bank_free = [[] for _ in range(8)]

        def proj_turned(u, src, dst, banks, scale=None):
            w, tw, slot = u
            toks = []
            for m in range(4):
                b = banks[m % len(banks)]
                o = P(b)[:, 0:256]
                t = proj(o, lambda c: w[:, c, m * 128:(m + 1) * 128], lambda c: src[:, c, :], 8, tw, *bank_free[b])
                if scale is None:
                    k = act.do(lambda e, m=m, o=o: e.activation(dst[:, m, :], o, ACT.Copy), t)
                else:
                    k = act.do(lambda e, m=m, o=o: e.activation(dst[:, m, :], o, ACT.Copy, scale=scale), t)
                bank_free[b] = [k]
                toks.append(k)
            done(slot, t)
            return toks

        def proj_tokens(u, src, banks, evac, ncol=512, nchunk=8):
            w, tw, slot = u
            toks = []
            for tt in range(2):
                b = banks[tt]
                o = P(b)[:, 0:ncol]
                t = proj(o, lambda c: src[:, c, tt * 128:(tt + 1) * 128], lambda c: w[:, c, 0:ncol], nchunk, tw, *bank_free[b])
                k = evac(tt, o, t)
                bank_free[b] = [k]
                toks.append(k)
            done(slot, t)
            return toks

        def add_residual(srcs, units, nchunk):
            for j, u in enumerate(units):
                def evac(tt, o, t, j=j):
                    h = H[:, tt, j * 512:(j + 1) * 512]
                    return dve.do(lambda e: e.tensor_tensor(h, o, h, ALU.add), t)
                proj_tokens(u, srcs, [2 * j, 2 * j + 1], evac, nchunk=nchunk)

        def copy_out(dst):
            return lambda tt, o, t: act.do(lambda e: e.activation(dst[:, tt, :], o, ACT.Copy), t)

        def finish(src):
            bar()
            t = dve.do(lambda e: e.tensor_copy(XS, src)) if src is not None else dve.last()
            s = sem("s_out")
            sp.raw(lambda e: e.dma_start(out.rearrange("(t p) d -> p t d", p=128), XS).then_inc(s, 16), t)
            sp.raw(lambda e: e.wait_ge(s, 16))

        def emit():
            with nc.Block() as block:
                for q, reg in ((sp, block.sync), (pe, block.tensor), (act, block.scalar), (dve, block.vector),
                               (pool, block.gpsimd)):
                    @reg
                    def _(e, q=q):
                        replay(e, q.items)

        def w8(src, i):
            return unit(src[i], "p (c n) -> p c n", c=8)

        def mixers():
            norm_turn(H, NT, sm["g_attn"])
            qT = wk(1024, "p (m t) -> p m t", m=4)
            kT = wk(1024, "p (m t) -> p m t", m=4)
            V1 = wk(1024, "p (t n) -> p t n", t=2)
            WS = wk(1024, "p (h t) -> p h t", h=8)
            MX = wk(2048, "p (t n) -> p t n", t=2)
            U1 = wk(1024, "p (t n) -> p t n", t=2)
            SP = w2(3072)
            T1 = w2(3072)
            VG = w2(1024, "p (t n) -> p t n", t=2)
            t_ws = load(act, WS, w_sp.rearrange("p (h t) -> p h t", h=8))
            proj_turned(w8(w_in, 0), NT, qT, [0, 1], 0.125)
            proj_turned(w8(w_in, 1), NT, kT, [2, 3])
            proj_tokens(w8(w_in, 2), NT, [4, 5], copy_out(V1))

            def gelu_out(dst):
                return lambda tt, o, t: act.do(lambda e: e.activation(dst[:, tt, :], o, ACT.Gelu_apprx_tanh), t)
            proj_tokens(w8(w_in, 3), NT, [6, 7], gelu_out(U1))
            proj_tokens(w8(w_in, 4), NT, [4, 5], gelu_out(VG))
            bar()

            blocks = [(0, 0), (0, 1), (1, 1)]
            sptok, zt = [], []
            for b, (kt, qt) in enumerate(blocks):
                for h in range(8):
                    r = slice(64 * (h % 2), 64 * (h % 2) + 64)
                    o = P(2 * b + h % 2)[:, (h // 2) * 128:(h // 2) * 128 + 128]
                    t = pe.do(mm(o, kT[r, h // 2, kt * 128:kt * 128 + 128], qT[r, h // 2, qt * 128:qt * 128 + 128],
                                 h < 2, False))
                zt.append(t)
                z = P(2 * b, 2)
                l = T1[:, b * 1024:(b + 1) * 1024]
                s = SP[:, b * 1024:(b + 1) * 1024]
                t = act.do(lambda e, l=l, z=z: e.activation(l, z, ACT.Abs), t)
                t = act.do(lambda e, l=l: e.activation(l, l, ACT.Exp, scale=-1.0), t)
                t = act.do(lambda e, l=l: e.activation(l, l, ACT.Ln, bias=1.0), t)
                t = dve.do(lambda e, s=s, z=z, l=l: e.scalar_tensor_tensor(s, z, 0.0, l, ALU.max, ALU.add), t)
                if kt == qt:
                    v = s.rearrange("p (h t) -> p h t", h=8)
                    m = bc(co["m01"].unsqueeze(1), [128, 8, 128])
                    t = dve.do(lambda e, v=v, m=m: e.tensor_tensor(v, v, m, ALU.mult), t)
                sptok.append(t)
            atok = []
            for b in range(3):
                for j in range(2):
                    o = P(2 * b + j)
                    s = SP[:, b * 1024 + j * 512:b * 1024 + (j + 1) * 512]
                    t = pe.do(mm(o, co["negu"], s, False, b != 1), sptok[b])
                    if b == 1:
                        s = SP[:, 2048 + j * 512:2048 + (j + 1) * 512]
                        t = pe.do(mm(o, co["neg1"], s, False, True), sptok[2])
                z = P(2 * b, 2)
                l = T1[:, b * 1024:(b + 1) * 1024]
                if b != 1:
                    v = l.rearrange("p (h t) -> p h t", h=8)
                    zv = z.rearrange("p (h t) -> p h t", h=8)
                    m = bc(co["neg"].unsqueeze(1), [128, 8, 128])
                    t = dve.do(lambda e, v=v, zv=zv, m=m: e.tensor_tensor(v, zv, m, ALU.min), t)
                    z = l
                atok.append(act.do(lambda e, l=l, z=z: e.activation(l, z, ACT.Exp), t))
            A = T1.rearrange("p (b h t) -> p b h t", b=3, h=8)
            for h in range(8):
                i = h % 2 * 4 + h // 2
                cs = slice(h * 64, h * 64 + 64)
                pe.raw(mm(P(6)[:, cs], A[:, 0, i, :], V1[:, 0, cs], True, True), *atok)
                pe.raw(mm(P(7)[:, cs], A[:, 1, i, :], V1[:, 0, cs], True, False))
                t_pv = pe.do(mm(P(7)[:, cs], A[:, 2, i, :], V1[:, 1, cs], False, True))
            ts = [square_sum(VG[:, tt, :], MX[:, tt, 512:1024], ST[:, 4 + tt:5 + tt]) for tt in range(2)]
            r = rstd(ST[:, 4:6], 2, 512, *ts)
            tv = [dve.do(lambda e, tt=tt: e.scalar_tensor_tensor(VG[:, tt, :], VG[:, tt, :], ST[:, 4 + tt:5 + tt], rw["sg"],
                                                                 ALU.mult, ALU.mult), r) for tt in range(2)]
            tw = pool.do(lambda e: e.tensor_tensor(WS, WS, bc(co["tri"].unsqueeze(1), [128, 8, 128]), ALU.mult), t_ws)
            for h in range(8):
                o = P(h // 4)[:, (h % 4) * 128:(h % 4) * 128 + 128].rearrange("p (c d) -> p c d", c=2)
                t = pe.do(mm(o, WS[:, h, :], VG[:, :, h * 64:h * 64 + 64], True, True), tw, *tv, *atok)
            for c in range(2):
                o = P(0, 2).rearrange("p (h c d) -> p h c d", h=8, c=2)[:, :, c, :]
                v = MX[:, c, 512:1024].rearrange("p (h d) -> p h d", h=8)
                u = U1[:, c, :].rearrange("p (h d) -> p h d", h=8)
                bb = bc(sm["bsp"].unsqueeze(2), [128, 8, 64])
                t1 = dve.do(lambda e, o=o, v=v, bb=bb: e.tensor_tensor(v, o, bb, ALU.add), t)
                t1 = dve.do(lambda e, v=v, u=u: e.tensor_tensor(v, v, u, ALU.mult), t1)
            ts = []
            for tt in range(2):
                ts.append(square_sum(P(6 + tt), SP[:, 1024 * tt:1024 * tt + 512], ST[:, 8 + tt:9 + tt], t_pv))
                ts.append(square_sum(MX[:, tt, 512:1024], SP[:, 1024 * tt + 512:1024 * tt + 1024], ST[:, 10 + tt:11 + tt], t1))
            r = rstd(ST[:, 8:12], 4, 512, *ts)
            for tt in range(2):
                dve.do(lambda e, tt=tt: e.tensor_scalar(MX[:, tt, 0:512], P(6 + tt), ST[:, 8 + tt:9 + tt], None, ALU.mult), r)
                t = dve.do(lambda e, tt=tt: e.tensor_scalar(MX[:, tt, 512:1024], MX[:, tt, 512:1024], ST[:, 10 + tt:11 + tt],
                                                            None, ALU.mult), r)
            turn_all(MX, NT, 8, lambda c: sm["g_mix"][:, c:c + 1], 2, True, t)
            bar()
            add_residual(NT, [w8(w_out, 0), w8(w_out, 1)], 8)
            bar()

        def experts():
            wk.reset()
            w2.reset()
            norm_turn(H, NT, sm["g_ffn"])
            WR = wk(288, "p (c n) -> p c n", c=8)
            LG = wk(72, "p (t n) -> p t n", t=2)
            G8 = wk(16, "p (t n) -> p t n", t=2)
            E8 = wk(16, "p (t n) -> p t n", t=2)
            M8 = wk(32, "p (a t n) -> p a t n", a=2, t=2)
            X8 = ctx.enter_context(nc.sbuf_tensor("X8", [128, 2, 2, 8], U32))
            XF = wk(32, "p (a t n) -> p a t n", a=2, t=2)
            OG = wk(8, "p (t n) -> p t n", t=2)
            OE = wk(32, "p (a t n) -> p a t n", a=2, t=2)
            EX = wk(64, "p (t n) -> p t n", t=2)
            CB = wk(64, "p (t n) -> p t n", t=2)
            SL = wk(64, "p (t n) -> p t n", t=2)
            FL = ctx.enter_context(nc.sbuf_tensor("FL", [128, 1], mybir.dt.int32))
            sc = wk(16, "p (k t) -> p k t", t=2)
            t_wr = load(act, WR, w_r.rearrange("p (c n) -> p c n", c=8))
            for tt in range(2):
                t = proj(P(tt)[:, 0:36], lambda c: NT[:, c, tt * 128:tt * 128 + 128], lambda c: WR[:, c, :], 8, t_wr)
                t = dve.do(lambda e, tt=tt: e.tensor_tensor(LG[:, tt, :], P(tt)[:, 0:36], sm["rb"], ALU.add), t)
                io = co["iota"]

                def chain(f, q=dve):
                    nonlocal t
                    t = q.do(f, t)

                chain(lambda e, tt=tt: e.memset(G8[:, tt, :], -3e38))
                chain(lambda e, tt=tt: e.tensor_copy(G8[:, tt, 0:4], LG[:, tt, 0:4]))
                chain(lambda e, tt=tt: e.max(M8[:, 0, tt, :], G8[:, tt, :]))
                chain(lambda e, tt=tt: e.max_index(X8[:, 0, tt, :], M8[:, 0, tt, :], G8[:, tt, :]))
                chain(lambda e, tt=tt: e.tensor_copy(XF[:, 0, tt, :], X8[:, 0, tt, :]))
                chain(lambda e, tt=tt: e.tensor_scalar(OG[:, tt, :], io[:, 0:4], XF[:, 0, tt, 0:1], None, ALU.is_equal))
                chain(lambda e, tt=tt: e.tensor_scalar(sc[:, 0, tt:tt + 1], M8[:, 0, tt, 0:1], -1.0, None, ALU.mult))
                chain(lambda e, tt=tt: e.activation(G8[:, tt, 0:4], LG[:, tt, 0:4], ACT.Exp, bias=sc[:, 0, tt:tt + 1],
                                                    accum_out=sc[:, 1, tt:tt + 1]), act)
                chain(lambda e, tt=tt: e.reciprocal(sc[:, 2, tt:tt + 1], sc[:, 1, tt:tt + 1]))
                ev = EX[:, tt, :].rearrange("p (g n) -> p g n", g=4)
                chain(lambda e, tt=tt, ev=ev: e.tensor_tensor(ev, LG[:, tt, 4:36].rearrange("p (g n) -> p g n", g=4),
                                                              bc(OG[:, tt, :].unsqueeze(2), [128, 4, 8]), ALU.mult))
                chain(lambda e, tt=tt, ev=ev: e.tensor_reduce(E8[:, tt, :], ev.rearrange("p g n -> p n g"), AX, ALU.add))
                chain(lambda e, tt=tt: e.max(M8[:, 1, tt, :], E8[:, tt, :]))
                chain(lambda e, tt=tt: e.max_index(X8[:, 1, tt, :], M8[:, 1, tt, :], E8[:, tt, :]))
                chain(lambda e, tt=tt: e.tensor_copy(XF[:, 1, tt, :], X8[:, 1, tt, :]))
                chain(lambda e, tt=tt: e.tensor_scalar(sc[:, 3, tt:tt + 1], M8[:, 1, tt, 0:1], -1.0, None, ALU.mult))
                chain(lambda e, tt=tt: e.activation(M8[:, 0, tt, 0:2], M8[:, 1, tt, 0:2], ACT.Exp, bias=sc[:, 3, tt:tt + 1],
                                                    accum_out=sc[:, 4, tt:tt + 1]), act)
                chain(lambda e, tt=tt: e.reciprocal(sc[:, 5, tt:tt + 1], sc[:, 4, tt:tt + 1]))
                chain(lambda e, tt=tt: e.tensor_scalar(M8[:, 0, tt, 0:2], M8[:, 0, tt, 0:2], sc[:, 5, tt:tt + 1],
                                                       sc[:, 2, tt:tt + 1], ALU.mult, ALU.mult))
                for k in range(2):
                    chain(lambda e, tt=tt, k=k: e.tensor_scalar(OE[:, k, tt, :], io[:, 0:8], XF[:, 1, tt, k:k + 1], None,
                                                                ALU.is_equal))
                chain(lambda e, tt=tt: e.tensor_tensor(EX[:, tt, 0:8], OE[:, 0, tt, :], OE[:, 1, tt, :], ALU.add))
                chain(lambda e, tt=tt: e.tensor_tensor(SL[:, tt, :].rearrange("p (g n) -> p g n", g=4),
                                                       bc(EX[:, tt, 0:8].unsqueeze(1), [128, 4, 8]),
                                                       bc(OG[:, tt, :].unsqueeze(2), [128, 4, 8]), ALU.mult))
                for k in range(2):
                    chain(lambda e, tt=tt, k=k: e.tensor_scalar(OE[:, k, tt, :], OE[:, k, tt, :], M8[:, 0, tt, k:k + 1], None,
                                                                ALU.mult))
                chain(lambda e, tt=tt: e.tensor_tensor(EX[:, tt, 0:8], OE[:, 0, tt, :], OE[:, 1, tt, :], ALU.add))
                chain(lambda e, tt=tt: e.tensor_tensor(CB[:, tt, :].rearrange("p (g n) -> p g n", g=4),
                                                       bc(EX[:, tt, 0:8].unsqueeze(1), [128, 4, 8]),
                                                       bc(OG[:, tt, :].unsqueeze(2), [128, 4, 8]), ALU.mult))
            bar()
            pe.raw(mm(P(0)[:, 0:32], co["m01"], SL[:, 0, :], True, True))
            pe.raw(mm(P(0)[:, 32:64], co["one"], SL[:, 0, :], True, False))
            pe.raw(mm(P(0)[:, 32:64], co["m01"], SL[:, 1, :], False, True))
            pe.raw(mm(P(0)[:, 64:96], co["one"], SL[:, 0, :], True, False))
            t = pe.do(mm(P(0)[:, 64:96], co["one"], SL[:, 1, :], False, True))
            RK = wk(64, "p (t n) -> p t n", t=2)
            CR = wk(64, "p (t n) -> p t n", t=2)
            rkf, crf = (v.rearrange("p t n -> p (t n)") for v in (RK, CR))
            slf, cbf = (v.rearrange("p t n -> p (t n)") for v in (SL, CB))
            t = dve.do(lambda e: e.scalar_tensor_tensor(rkf, slf, -1000.0, P(0)[:, 0:64], ALU.mult, ALU.add), t)
            t = dve.do(lambda e: e.tensor_scalar(rkf, rkf, 1000.0, None, ALU.add), t)
            t_rk = t
            t = dve.do(lambda e: e.tensor_scalar(crf, rkf, float(SLOTS), None, ALU.is_ge), t)
            t = dve.do(lambda e: e.tensor_tensor(crf, crf, cbf, ALU.mult), t)
            t = dve.do(lambda e: e.tensor_reduce(sc[:, 6, 0:1], P(0)[:, 64:96], AX, ALU.max), t)
            t_flag = dve.do(lambda e: e.tensor_scalar(FL[:, :], sc[:, 6, 0:1], float(SLOTS), None, ALU.is_gt), t)
            moe_slots(CB, RK, t_rk)
            bar()
            for tt in range(2):
                for j in range(2):
                    h = H[:, tt, j * 512:(j + 1) * 512]
                    dve.do(lambda e, h=h, b=2 * tt + j: e.tensor_tensor(h, P(b), h, ALU.add))
            bar()
            wk.reset()
            w2.reset()
            wk(1200)
            moe_rest(CR, FL[0:1, 0:1], t_flag)
            last_norm(rw["fin1"], H)
            bar()

        def moe_slots(CB, RK, t_rk):
            XG = w2(4096, "p (b c n) -> p b c n", b=2, c=8)
            PG = wk(1024, "p (b t n) -> p b t n", b=2, t=2)
            PC = wk(1024, "p (b t n) -> p b t n", b=2, t=2)
            HP = wk(1024, "p (b n) -> p b n", b=2)
            SG = w2(512, "p (b n) -> p b n", b=2)
            HM = w2(512, "p (b n) -> p b n", b=2)
            YS = w2(1024, "p (b n) -> p b n", b=2)
            slot = bc(co["iota"][:, 0:64].unsqueeze(1), [128, 4, 64])
            pg_tok, pc_tok, xg_tok = {}, {}, {}
            pg_free, pc_free, xg_free = [None, None], [None, None], [None, None]
            g_free, hp_free, ys_free, step_free = [None, None], [None, None], [None, None], [[], []]

            def prep(g):
                b = g % 2
                for tt in range(2):
                    pg = PG[:, b, tt, :].rearrange("p (e s) -> p e s", e=4)
                    pc = PC[:, b, tt, :].rearrange("p (e s) -> p e s", e=4)
                    rk = bc(RK[:, tt, 4 * g:4 * g + 4].unsqueeze(2), [128, 4, 64])
                    cb = bc(CB[:, tt, 4 * g:4 * g + 4].unsqueeze(2), [128, 4, 64])
                    t = dve.do(lambda e, pg=pg, rk=rk: e.tensor_tensor(pg, slot, rk, ALU.is_equal), t_rk, pg_free[b])
                    t2 = dve.do(lambda e, pg=pg, pc=pc, cb=cb: e.tensor_tensor(pc, pg, cb, ALU.mult), t, pc_free[b])
                pg_tok[g], pc_tok[g] = t, t2
                xg_tok[g] = []

            def gather(g, s):
                b = g % 2
                o = P(7).rearrange("p (c n) -> p c n", c=2)
                for k in range(2):
                    for tt in range(2):
                        t = pe.do(mm(o[:, k, :], XS[:, tt, 2 * s + k::8], PG[:, b, tt, :], tt == 0, tt == 1),
                                  pg_tok[g], *step_free[0])
                pg_free[b] = t
                ks = []
                for k in range(2):
                    c = 2 * s + k
                    ks.append(dve.do(lambda e, k=k, c=c: e.tensor_scalar(XG[:, b, c, :], o[:, k, :], sm["g_ffn"][:, c:c + 1],
                                                                         None, ALU.mult), t, xg_free[b]))
                step_free[0] = ks
                xg_tok[g] += ks

            ys_tok, pct = {}, {}

            def scatter(ex):
                b = ex % 2
                for tt in range(2):
                    for j in range(2):
                        r = slice(64 * j, 64 * j + 64)
                        t = pe.do(mm(P(2 * tt + j), HP[r, b, 256 + tt * 128:384 + tt * 128], YS[r, b, :], ex == 0, ex == 31),
                                  ys_tok[ex])
                ys_free[b] = hp_free[b] = t

            prep(0)
            for s in range(4):
                gather(0, s)
            y_free = None
            for ex in range(32):
                g, k4, b = ex // 4, ex % 4, ex % 2
                if k4 == 0 and g < 7:
                    prep(g + 1)
                wg, tg, s1 = unit(w_gate[ex].rearrange("(p c) n -> p (c n)", c=8), "p (c n) -> p c n", c=8)
                wu, tu, s2 = unit(w_up[ex].rearrange("(p c) n -> p (c n)", c=8), "p (c n) -> p c n", c=8)
                wd, td, s3 = unit(w_down[ex].rearrange("(h p c) n -> p h (c n)", h=2, c=2), "p (h c n) -> p h c n", h=2, c=2)
                G = P(4 + b)
                x = XG[:, g % 2, :, k4 * 64:k4 * 64 + 64]
                for w, tw, z in ((wg, tg, 0), (wu, tu, 256)):
                    for c in range(8):
                        for j in range(2):
                            t = pe.do(mm(G[64 * j:64 * j + 64, z:z + 256], x[:, c, :], w[:, c, 256 * j:256 * j + 256], c == 0, c == 7),
                                      tw, g_free[b], *xg_tok[g])
                    done(s1 if z == 0 else s2, t)
                if k4 == 3:
                    xg_free[g % 2] = t
                s = act.do(lambda e, b=b, G=G: e.activation(SG[:, b, :], G[:, 0:256], ACT.Silu), t)
                h = dve.do(lambda e, b=b, G=G: e.tensor_tensor(HM[:, b, :], SG[:, b, :], G[:, 256:512], ALU.mult), s)
                if ex:
                    scatter(ex - 1)
                for c in range(2):
                    t = pe.do(tr(G[:, c * 128:c * 128 + 128], HM[:, b, c::2]), h)
                for tt in range(2):
                    pc = PC[:, g % 2, tt, k4 * 64:k4 * 64 + 64]
                    for j in range(2):
                        t = pe.do(mm(G[64 * j:64 * j + 64, 256 + tt * 128:384 + tt * 128], pc, ident, True, True), pc_tok[g])
                if k4 == 3:
                    pc_free[g % 2] = t
                k = act.do(lambda e, b=b, G=G: e.activation(HP[:, b, :], G, ACT.Copy), t, hp_free[b])
                g_free[b] = k
                if g < 7:
                    gather(g + 1, k4)
                ht = HP[:, b, 0:256].rearrange("p (c h s) -> p h c s", c=2, h=2)
                for c in range(4):
                    for j in range(2):
                        t = pe.do(mm(P(6)[64 * j:64 * j + 64, :], ht[:, c // 2, c % 2, :], wd[:, c // 2, c % 2, 512 * j:512 * j + 512],
                                     c == 0, c == 3), k, td, y_free)
                done(s3, t)
                ys_tok[ex] = y_free = dve.do(lambda e, b=b: e.tensor_copy(YS[:, b, :], P(6)), t, ys_free[b])
            scatter(31)

        def moe_rest(CR, flag, t_flag):
            for q in (pe, act, dve, sp):
                q.wait(t_flag)
            fp, fa, fd, fs = (q.branch(sem(f"f_{n}"), flag) for n, q in (("pe", pe), ("act", act), ("dve", dve), ("sp", sp)))
            fs.wait(*(q.last() for q in qs), *(t for f in ring_free for t in f))
            SG = w2(1024, "p (t n) -> p t n", t=2)
            HM = w2(1024, "p (t n) -> p t n", t=2)
            HT = w2(1024, "p (t c n) -> p t c n", t=2, c=4)
            sems = [sem(f"f_ld{i}") for i in range(NR)]
            slot_free = [None] * NR
            free = {b: None for b in range(4, 8)}

            def weights(n, src, c):
                s = n % NR
                dst = AR[:, s * 4096:(s + 1) * 4096]
                fs.raw(lambda e: e.dma_start(dst, src.rearrange("(p c) n -> p (c n)", c=c)).then_inc(sems[s], 16), slot_free[s])
                return dst.rearrange("p (c n) -> p c n", c=c), (sems[s], 16 * (n // NR + 1)), s

            for ex in range(32):
                g, tg, sg_ = weights(3 * ex, w_gate[ex], 8)
                u, tu, su_ = weights(3 * ex + 1, w_up[ex], 8)
                d, td, sd_ = weights(3 * ex + 2, w_down[ex], 4)
                hm = []
                for tt in range(2):
                    x8 = lambda c: NT[:, c, tt * 128:tt * 128 + 128]
                    a = proj(P(4 + 2 * tt), x8, lambda c: g[:, c, :], 8, tg, free[4 + 2 * tt], q=fp)
                    b = proj(P(5 + 2 * tt), x8, lambda c: u[:, c, :], 8, tu, free[5 + 2 * tt], q=fp)
                    s = fa.do(lambda e, tt=tt: e.activation(SG[:, tt, :], P(4 + 2 * tt), ACT.Silu), a)
                    h = fd.do(lambda e, tt=tt, ex=ex: e.scalar_tensor_tensor(
                        HM[:, tt, :], SG[:, tt, :], CR[:, tt, ex:ex + 1], P(5 + 2 * tt), ALU.mult, ALU.mult), s, b)
                    hm.append(h)
                    free[5 + 2 * tt] = h
                slot_free[sg_], slot_free[su_] = a, b
                for tt in range(2):
                    for c in range(4):
                        t = fp.do(tr(P(4 + 2 * tt)[:, c * 128:(c + 1) * 128], HM[:, tt, c::4]), hm[tt])
                    k = fa.do(lambda e, tt=tt: e.activation(HT[:, tt, :, :], P(4 + 2 * tt).rearrange("p (c n) -> p c n", c=4),
                                                            ACT.Copy), t)
                    free[4 + 2 * tt] = k
                    for j in range(2):
                        for c in range(4):
                            t = fp.do(mm(P(2 * tt + j), HT[:, tt, c, :], d[:, c, j * 512:(j + 1) * 512],
                                         ex == 0 and c == 0, ex == 31 and c == 3), k, td)
                slot_free[sd_] = t
            for tt in range(2):
                for j in range(2):
                    h = H[:, tt, j * 512:(j + 1) * 512]
                    fd.do(lambda e, h=h, b=2 * tt + j: e.tensor_tensor(h, P(b), h, ALU.add), t)
            for q in (fp, fa, fd, fs):
                q.wait(fp.last(), fa.last(), fd.last())

        def last_norm(gain, dst):
            ts = [square_sum(H[:, tt, :], XS[:, tt, :], ST[:, tt:tt + 1]) for tt in range(2)]
            r = rstd(ST[:, 0:2], 2, D, *ts)
            for tt in range(2):
                dve.do(lambda e, tt=tt: e.scalar_tensor_tensor(dst[:, tt, :], H[:, tt, :], ST[:, tt:tt + 1], gain,
                                                               ALU.mult, ALU.mult), r)

        def mixers2():
            wk.reset()
            w2.reset()
            norm_turn(H, NT, sm["g_nmix"])
            qT = wk(1024, "p (m t) -> p m t", m=4)
            kT = wk(1024, "p (m t) -> p m t", m=4)
            VA = wk(1024, "p (t n) -> p t n", t=2)
            OAT = wk(1024, "p (m t) -> p m t", m=4)
            OBT = wk(1024, "p (m t) -> p m t", m=4)
            S = wk(4 * 384, "p (i n) -> p i n", i=4)
            PT = wk(4 * 384, "p (i n) -> p i n", i=4)
            VB = wk(560, "p (t n) -> p t n", t=2)
            lm = wk(8)
            mx = wk(64, "p (i t) -> p i t", t=2)
            den = wk(64, "p (i t) -> p i t", t=2)
            lam = sm["lam"]
            for i in range(2):
                a = lam[:, 128 * i:128 * i + 64]
                b = lam[:, 128 * i + 64:128 * i + 128]
                t = dve.do(lambda e, i=i, a=a, b=b: e.tensor_tensor_reduce(S[:, i, 0:64], a, b, 1.0, 0.0, ALU.mult, ALU.add,
                                                                           lm[:, i:i + 1]))
            t = act.do(lambda e: e.activation(lm[:, 2:4], lm[:, 0:2], ACT.Exp), t)
            t = dve.do(lambda e: e.tensor_scalar(lm[:, 4:5], lm[:, 3:4], lm[:, 2:3], -0.2, ALU.subtract, ALU.add), t)
            t_lam = t

            proj_turned(w8(w_in2, 0), NT, qT, [0, 1], 0.125)
            proj_turned(w8(w_in2, 1), NT, kT, [2, 3])
            proj_tokens(w8(w_in2, 2), NT, [4, 5], copy_out(VA))
            bar()

            scores_bank = [0]
            s_free = [[] for _ in range(4)]

            def softmax_map(i, lq, rk, slope):
                b = scores_bank[0] % 2
                scores_bank[0] += 1
                pe.raw(mm(P(b)[:, 0:128], lq(0), rk(0, 128), True, True), *bank_free[b])
                t = pe.do(mm(P(b)[:, 128:384], lq(1), rk(0, 256), True, True))
                s = S[:, i % 4, :]
                t = dve.do(lambda e: e.scalar_tensor_tensor(s, co["dist"], slope, P(b)[:, 0:384], ALU.mult, ALU.add),
                           t, *s_free[i % 4])
                bank_free[b] = [t]
                for tt, cs in ((0, slice(0, 128)), (1, slice(128, 384))):
                    m = dve.do(lambda e, tt=tt, cs=cs: e.tensor_reduce(mx[:, i, tt:tt + 1], s[:, cs], AX, ALU.max, negate=True), t)
                    k = act.do(lambda e, tt=tt, cs=cs: e.activation(s[:, cs], s[:, cs], ACT.Exp, bias=mx[:, i, tt:tt + 1],
                                                                    accum_out=den[:, i, tt:tt + 1]), m)
                return k

            turn_bank = [0]
            pt_free = [[] for _ in range(4)]

            def turn_map(i, *tokens):
                b = 2 + turn_bank[0] % 2
                turn_bank[0] += 1
                for j in range(3):
                    t = pe.do(tr(P(b)[:, j * 128:(j + 1) * 128], S[:, i % 4, j * 128:(j + 1) * 128]), *tokens, *bank_free[b])
                s_free[i % 4] = [t]
                k = act.do(lambda e: e.activation(PT[:, i % 4, :], P(b)[:, 0:384], ACT.Copy), t, *pt_free[i % 4])
                bank_free[b] = [k]
                return k

            for h in range(4):
                ks = []
                for c in range(2):
                    r = slice(64 * c, 64 * c + 64)
                    ks.append(softmax_map(2 * h + c, lambda t: qT[r, h, t * 128:t * 128 + 128], lambda a, z: kT[r, h, a:z],
                                          float(2.0 ** (-2.0 * (h + 1)))))
                i = 2 * h
                t = dve.do(lambda e, i=i: e.reciprocal(den[:, i:i + 2, :], den[:, i:i + 2, :]), *ks)
                t = dve.do(lambda e, i=i: e.tensor_scalar(den[:, i + 1, :], den[:, i + 1, :], lm[:, 4:5], None, ALU.mult), t, t_lam)
                for tt, cs in ((0, slice(0, 128)), (1, slice(128, 384))):
                    s0, s1 = S[:, i % 4, cs], S[:, (i + 1) % 4, cs]
                    a = dve.do(lambda e, i=i, tt=tt, s1=s1: e.tensor_scalar(s1, s1, den[:, i + 1, tt:tt + 1], None, ALU.mult), t)
                    a = dve.do(lambda e, i=i, tt=tt, s0=s0, s1=s1: e.scalar_tensor_tensor(s0, s0, den[:, i, tt:tt + 1], s1,
                                                                                         ALU.mult, ALU.add), a)
                s_free[(i + 1) % 4] = [a]
                k = turn_map(i, a)
                cs = slice(h * 128, h * 128 + 128)
                p = PT[:, i % 4, :]
                pe.raw(mm(P(4)[:, cs], p[:, 0:128], VA[:, 0, cs], True, True), k)
                pe.raw(mm(P(5)[:, cs], p[:, 128:256], VA[:, 0, cs], True, False))
                t = pe.do(mm(P(5)[:, cs], p[:, 256:384], VA[:, 1, cs], False, True))
                pt_free[i % 4] = [t]
            ts = []
            for tt in range(2):
                for h in range(4):
                    ts.append(square_sum(P(4 + tt)[:, h * 128:h * 128 + 128], XS[:, tt, h * 128:h * 128 + 128],
                                         ST[:, 16 + 4 * tt + h:17 + 4 * tt + h], t))
            r = rstd(ST[:, 16:24], 8, 128, *ts)
            for tt in range(2):
                v = XS[:, tt, 0:512].rearrange("p (h d) -> p h d", h=4)
                a = dve.do(lambda e, tt=tt, v=v: e.tensor_tensor(
                    v, P(4 + tt).rearrange("p (h d) -> p h d", h=4),
                    bc(ST[:, 16 + 4 * tt:20 + 4 * tt].unsqueeze(2), [128, 4, 128]), ALU.mult), r)
            bar()
            turn_all(XS, OAT, 4, lambda c: sm["g_sub"], 6, False, a)
            bar()
            toks = dve.do(lambda e: e.tensor_scalar(OAT, OAT, 0.8, None, ALU.mult))
            qB, kV = qT, kT
            proj_turned(w8(w_in2, 3), NT, qB, [4, 5], 0.125)
            proj_turned(w8(w_in2, 4), NT, kV, [6, 7])
            proj_tokens(unit(w_in2[5][:, 0:8 * 512], "p (c n) -> p c n", c=8), NT, [4, 5],
                        lambda tt, o, t: act.do(lambda e: e.activation(VB[:, tt, :], o, ACT.Copy), t), ncol=280)
            bar()
            GT = w2(48, "p (t n) -> p t n", t=2)
            act.do(lambda e: e.activation(GT, VB[:, :, 256:280], ACT.Sigmoid))
            KP = w2(512, "p (g c l) -> p g c l", g=2, c=8)
            HID = w2(64, "p (b h n) -> p b h n", b=2, h=2)
            CK2 = w2(256, "p (b h n) -> p b h n", b=2, h=2)
            KCT = w2(8)
            VC = w2(128, p=8)
            BDV = w2(512, p=64)
            SC = w2(128, "p (t h c) -> p t h c", t=2, h=8)
            CS = w2(64, "p (k t h) -> p k t h", k=4, t=2)
            PCT = w2(256, p=64)
            t_c2 = load(act, CK2, ck2.rearrange("p (b h n) -> p b h n", b=2, h=2))
            tk = dve.do(lambda e: e.tensor_tensor(KP[:, :, :, :].rearrange("p g c l -> p (g c) l"),
                                                  kV[:, 0:2, :].rearrange("p g (c l) -> p (g c) l", l=32),
                                                  bc(sm["pos"].unsqueeze(1), [128, 16, 32]), ALU.add))
            ua = unit(ck1[0], "p (l n) -> p l n", l=16)
            ub = unit(ck1[1], "p (l n) -> p l n", l=16)
            for ht in range(2):
                for l in range(32):
                    w = (ua, ub)[l // 16]
                    for b in range(2):
                        r = slice(64 * b, 64 * b + 64)
                        t = pe.do(mm(P(b)[:, ht * 16:ht * 16 + 16].rearrange("p (g c) -> p g c", g=2),
                                     w[0][r, l % 16, ht * 128:ht * 128 + 128], KP[r, :, :, l], l == 0, l == 31), w[1], tk)
            done(ua[2], t)
            done(ub[2], t)
            for b in range(2):
                t2 = act.do(lambda e, b=b: e.activation(HID[:, b, :, :], P(b)[:, 0:32].rearrange("p (h n) -> p h n", h=2), ACT.Gelu), t)
            for g in range(2):
                r = slice(64 * g, 64 * g + 64)
                for ht in range(2):
                    pe.raw(mm(P(2)[r, 0:8], CK2[:, 0, ht, :], HID[:, 0, ht, g * 8:g * 8 + 8], ht == 0, ht == 1), t2, t_c2)
                for ht in range(2):
                    t = pe.do(mm(P(3)[0:8, g * 64:g * 64 + 64], HID[:, 1, ht, g * 8:g * 8 + 8], CK2[:, 1, ht, :], ht == 0, ht == 1))
            t1 = act.do(lambda e: e.activation(KCT, P(2)[:, 0:8], ACT.Copy), t)
            t2 = act.do(lambda e: e.activation(VC, P(3)[0:8, 0:128], ACT.Copy), t)
            vcb = bc(VC.rearrange("p (g d) -> p g d", g=2).unsqueeze(2), [8, 2, 4, 64])
            t = pe.do(mm(P(4)[0:64, :].rearrange("p (g r d) -> p g r d", g=2, r=4), co["esel"][0:8, :], vcb, True, True), t2)
            t_bd = dve.do(lambda e: e.tensor_tensor(BDV, P(4)[0:64, :], co["bd"][0:64, :], ALU.mult), t)
            for tt in range(2):
                for h in range(8):
                    r = slice(64 * (h // 4), 64 * (h // 4) + 64)
                    t = pe.do(mm(P(h // 4)[:, tt * 32 + h % 4 * 8:tt * 32 + h % 4 * 8 + 8], qB[r, h % 4, tt * 128:tt * 128 + 128],
                                 KCT[r, :], True, True), t1)
            scf = SC.rearrange("p t h c -> p (t h) c")

            def chain(f, q=dve):
                nonlocal t
                t = q.do(f, t)
            for g in range(2):
                chain(lambda e, g=g: e.tensor_tensor(
                    SC[:, :, 4 * g:4 * g + 4, :].rearrange("p t h c -> p t (h c)"), P(g)[:, 0:64].rearrange("p (t a) -> p t a", t=2),
                    co["cmpb"].rearrange("p (t a) -> p t a", t=2)[:, :, 32 * g:32 * g + 32], ALU.add))
            csf = [CS[:, k, :, :].rearrange("p t h -> p (t h)") for k in range(4)]
            chain(lambda e: e.tensor_reduce(csf[0], scf, AX, ALU.max))
            chain(lambda e: e.tensor_tensor(scf, scf, bc(csf[0].unsqueeze(2), [128, 16, 8]), ALU.subtract))
            chain(lambda e: e.activation(scf, scf, ACT.Exp), act)
            chain(lambda e: e.tensor_reduce(csf[1], scf, AX, ALU.add))
            chain(lambda e: e.reciprocal(csf[2], csf[1]))
            g3 = GT.rearrange("p t (h j) -> p (t h) j", j=3)
            chain(lambda e: e.tensor_tensor(csf[3], csf[2], g3[:, :, 0], ALU.mult))
            for tt in range(2):
                chain(lambda e, tt=tt: e.tensor_tensor(SC[:, tt, :, :], SC[:, tt, :, :],
                                                       bc(co["cmpv"][:, tt * 8:tt * 8 + 8].unsqueeze(1), [128, 8, 8]), ALU.mult))
            chain(lambda e: e.tensor_tensor(scf, scf, bc(csf[3].unsqueeze(2), [128, 16, 8]), ALU.mult))
            for tt in range(2):
                t3 = pe.do(tr(P(4)[0:64, tt * 128:tt * 128 + 128], SC[:, tt, :, :].rearrange("p h c -> p (h c)")), t, t_bd)
            t3 = act.do(lambda e: e.activation(PCT, P(4)[0:64, 0:256], ACT.Copy), t3)
            for m in range(4):
                t = pe.do(mm(P(6 + m // 2)[:, (m % 2) * 256:(m % 2) * 256 + 256], BDV[:, m * 128:m * 128 + 128], PCT,
                             m % 2 == 0, False), t3, t_bd)
            bar()
            for i in range(16):
                j, h = i // 8, i % 8
                g = h // 4
                r = slice(64 * g, 64 * g + 64)
                k = softmax_map(i, lambda t: qB[r, h % 4, t * 128:t * 128 + 128], lambda a, z: kV[r, 2 + j, a:z],
                                float(2.0 ** -(h + 1.0)))
                t = dve.do(lambda e, i=i: e.reciprocal(den[:, i, :], den[:, i, :]), k)
                t = dve.do(lambda e, i=i, h=h, j=j: e.tensor_tensor(den[:, i, :], den[:, i, :], GT[:, :, h * 3 + 1 + j], ALU.mult), t)
                for tt, cs in ((0, slice(0, 128)), (1, slice(128, 384))):
                    s = S[:, i % 4, cs]
                    a = dve.do(lambda e, i=i, tt=tt, s=s: e.tensor_scalar(s, s, den[:, i, tt:tt + 1], None, ALU.mult), t)
                k = turn_map(i, a)
                o = P(6 + h // 4)[(h % 2) * 64:(h % 2) * 64 + 64, (h // 2 % 2) * 256:(h // 2 % 2) * 256 + 256]
                vs = slice(128 * j + 64 * g, 128 * j + 64 * g + 64)
                p = PT[:, i % 4, :]
                pe.raw(mm(o, VB[:, 0, vs], p[:, 0:256], False, False), k)
                t = pe.do(mm(o[:, 128:256], VB[:, 1, vs], p[:, 256:384], False, i == 15))
                pt_free[i % 4] = [t]
            for m in range(4):
                act.do(lambda e, m=m: e.activation(OBT[:, m, :], P(6 + m // 2)[:, (m % 2) * 256:(m % 2) * 256 + 256], ACT.Copy), t)
            bar()
            SGA = w2(2048, "p (t n) -> p t n", t=2)
            SGB = w2(2048, "p (t n) -> p t n", t=2)
            for j in range(4):
                dst = (SGA, SGB)[j // 2]

                def evac(tt, o, t, dst=dst, j=j):
                    return act.do(lambda e: e.activation(dst[:, tt, (j % 2) * 512:(j % 2) * 512 + 512], o, ACT.Sigmoid), t)
                proj_tokens(w8(w_in2, 6 + j), NT, [2 * (j % 2), 2 * (j % 2) + 1], evac)
            ua = unit(w_a.rearrange("(c p) n -> p c n", c=4), "p (c n) -> p c n", c=4)
            ub = unit(w_b.rearrange("(c p) n -> p c n", c=4), "p (c n) -> p c n", c=4)
            bf = [[], []]
            for tt in range(2):
                for j in range(2):
                    cs = slice(j * 512, j * 512 + 512)
                    a = proj(P(4 + j), lambda c: OAT[:, c, tt * 128:tt * 128 + 128], lambda c: ua[0][:, c, cs], 4, ua[1], *bf[j])
                    b = proj(P(6 + j), lambda c: OBT[:, c, tt * 128:tt * 128 + 128], lambda c: ub[0][:, c, cs], 4, ub[1], *bf[j])
                    t1 = dve.do(lambda e, tt=tt, cs=cs, j=j: e.tensor_tensor(SGA[:, tt, cs], SGA[:, tt, cs], P(4 + j), ALU.mult),
                                a, act.last())
                    t2 = dve.do(lambda e, tt=tt, cs=cs, j=j: e.tensor_tensor(SGB[:, tt, cs], SGB[:, tt, cs], P(6 + j), ALU.mult), b)
                    bf[j] = [t1, t2]
                    t = dve.do(lambda e, tt=tt, cs=cs: e.tensor_tensor(XS[:, tt, cs], SGA[:, tt, cs], SGB[:, tt, cs], ALU.add), t1, t2)
            done(ua[2], a)
            done(ub[2], b)
            bar()
            turn_all(XS, NT, 8, None, 0, True)
            bar()
            add_residual(NT, [w8(w_out2, 0), w8(w_out2, 1)], 8)
            bar()

        def cross():
            wk.reset()
            w2.reset()
            MT = w2(2048, "p (c t) -> p c t", c=8)
            MM = w2(2048, "p (t d) -> p t d", t=2)
            t = load(act, MM, mem.rearrange("(t p) d -> p t d", p=128), dve.last(), pe.last(), pool.last())
            act.wait(t)
            dve.wait(t)
            norm_turn(MM, MT, sm["g_mem"])
            norm_turn(H, NT, sm["g_cross"])
            qT = wk(1024, "p (m t) -> p m t", m=4)
            kT = wk(1024, "p (m t) -> p m t", m=4)
            V = wk(1024, "p (t n) -> p t n", t=2)
            OT = wk(1024, "p (m t) -> p m t", m=4)
            mx = wk(8)
            den = wk(8)
            proj_turned(w8(w_cq, 0), NT, qT, [0, 1])
            proj_turned(w8(w_ckv, 0), MT, kT, [2, 3])
            proj_tokens(w8(w_ckv, 1), MT, [4, 5], copy_out(V))
            bar()
            S = w2(2048, "p (t h n) -> p t h n", t=2, h=4)
            PT = w2(2048, "p (m h n) -> p m h n", m=2, h=4)
            sc = float(128 ** -0.5)
            for tt in range(2):
                for h in range(4):
                    t = pe.do(mm(P(2 * tt + h // 2)[:, (h % 2) * 256:(h % 2) * 256 + 256], qT[:, h, tt * 128:tt * 128 + 128],
                                 kT[:, h, :], True, True))
            t = dve.do(lambda e: e.tensor_reduce(mx, P(0, 4).rearrange("p (a n) -> p a n", n=256), AX, ALU.max), t)
            t = dve.do(lambda e: e.tensor_scalar(mx, mx, -sc, None, ALU.mult), t)
            for a in range(8):
                k = act.do(lambda e, a=a: e.activation(S[:, a // 4, a % 4, :], P(a // 2)[:, (a % 2) * 256:(a % 2) * 256 + 256],
                                                       ACT.Exp, bias=mx[:, a:a + 1], scale=sc, accum_out=den[:, a:a + 1]), t)
            t = dve.do(lambda e: e.reciprocal(den, den), k)
            for a in range(8):
                s = S[:, a // 4, a % 4, :]
                t1 = dve.do(lambda e, a=a, s=s: e.tensor_scalar(s, s, den[:, a:a + 1], None, ALU.mult), t)
            for m in range(2):
                for pair in range(2):
                    o = P(4 + 2 * m + pair).rearrange("p (h t) -> p h t", h=2)
                    for h in range(2):
                        for tt in range(2):
                            t = pe.do(tr(o[:, h, tt * 128:tt * 128 + 128], S[:, tt, 2 * pair + h, m * 128:m * 128 + 128]), t1)
                    k = act.do(lambda e, m=m, pair=pair, o=o: e.activation(PT[:, m, 2 * pair:2 * pair + 2, :], o, ACT.Copy), t)
            for h in range(4):
                o = P(h // 2)[:, (h % 2) * 256:(h % 2) * 256 + 256]
                pe.raw(mm(o, V[:, 0, h * 128:h * 128 + 128], PT[:, 0, h, :], True, False), k)
                t = pe.do(mm(o, V[:, 1, h * 128:h * 128 + 128], PT[:, 1, h, :], False, True))
                if h % 2:
                    act.do(lambda e, h=h: e.activation(OT[:, h - 1:h + 1, :], P(h // 2).rearrange("p (h t) -> p h t", h=2),
                                                       ACT.Copy), t)
            bar()
            u = unit(w_co.rearrange("(c p) n -> p c n", c=4), "p (c n) -> p c n", c=4)
            for j in range(2):
                for tt in range(2):
                    cs = slice(j * 512, j * 512 + 512)
                    t = proj(P(2 + 2 * j + tt), lambda c: OT[:, c, tt * 128:tt * 128 + 128], lambda c: u[0][:, c, cs], 4, u[1])
                    dve.do(lambda e, j=j, tt=tt, cs=cs: e.tensor_tensor(H[:, tt, cs], P(2 + 2 * j + tt), H[:, tt, cs], ALU.add), t)
            done(u[2], t)
            bar()

        def peer():
            wk.reset()
            w2.reset()
            norm_turn(H, NT, sm["g_peer"])
            b1 = Bump(Wk, 0, 8192)
            wk(8192)
            I1T, I2T, GTT = wk(256), wk(256), wk(256)
            SK = b1(2048, "p (a n) -> p a n", a=16)
            QP = b1(1024, "p (a t) -> p a t", a=4)
            TS = b1(512, "p (a k) -> p a k", a=32)
            TF = b1(512, "p (a k) -> p a k", a=32)
            TIi = b1(512, "p (a k) -> p a k", a=32).bitcast(U32)
            BS = b1(256, "p (a k) -> p a k", a=16)
            BJ = b1(256, "p (a k) -> p a k", a=16).bitcast(U32)
            BA = b1(256, "p (a k) -> p a k", a=16).bitcast(U32)
            BF = b1(512, "p (c a k) -> p c a k", c=2, a=16)
            BG = b1(256, "p (a k) -> p a k", a=16)
            II = b1(512, "p (c t n) -> p c t n", c=2, t=2)
            gs = b1(32, "p (k a) -> p k a", k=2)
            S = w2(4096, "p (a n) -> p a n", a=32)
            CA = w2(4096, "p (a n) -> p a n", a=16)
            XHt, XLt = rounded("XH", "XSs", 0, 2048), rounded("XL", "NTs", 0, 2048)
            XH, XL = (v[:, :].rearrange("p (c t) -> p c t", c=8) for v in (XHt, XLt))
            t_xh = act.do(lambda e: e.activation(XHt[:, :], NTs[:, :], ACT.Copy))
            t_sk = load(act, SK, subk.rearrange("p (a n) -> p a n", a=16), dve.last(), pe.last(), pool.last())

            def top16(src, vals, idx, rows):
                for k in (0, 8):
                    for a in rows:
                        t = dve.do(lambda e, a=a, k=k: e.max(vals[:, a, k:k + 8], src[:, a, :]))
                    dve.wait(t)
                    for a in rows:
                        t = dve.do(lambda e, a=a, k=k: e.max_index(idx[:, a, k:k + 8], vals[:, a, k:k + 8], src[:, a, :]))
                    dve.wait(t)
                    if k == 0:
                        for a in rows:
                            t = dve.do(lambda e, a=a: e.match_replace(src[:, a, :], vals[:, a, 0:8], src[:, a, :], -3e38))
                        dve.wait(t)

            def chain(f, q=dve):
                nonlocal t
                t = q.do(f, t)

            qp_free = [[] for _ in range(4)]
            by_tt = lambda v: v.rearrange("p (t h) k -> p t h k", t=2)
            tsv, tfv = (v.rearrange("p (t h c) k -> p t h c k", t=2, c=2) for v in (TS, TF))
            for ui in range(4):
                w, tw, slot = w8(w_pq, ui)
                for m in range(4):
                    hc = ui * 4 + m
                    b = hc % 4
                    o = P(b)[:, 0:256]
                    t = proj(o, lambda c: w[:, c, m * 128:(m + 1) * 128], lambda c: NT[:, c, :], 8, tw, *bank_free[b])
                    k = act.do(lambda e, m=m, o=o: e.activation(QP[:, m, :], o, ACT.Copy), t, *qp_free[m])
                    bank_free[b] = [k]
                    t_nt = t
                    b = 4 + hc % 4
                    for tt in range(2):
                        t2 = pe.do(mm(P(b)[:, tt * 128:tt * 128 + 128], QP[:, m, tt * 128:tt * 128 + 128], SK[:, hc, :], True, True),
                                   k, t_sk, *bank_free[b])
                    qp_free[m] = [t2]
                    v = S.rearrange("p (t a) n -> p t a n", t=2)[:, :, hc, :]
                    k = act.do(lambda e, v=v, b=b: e.activation(v, P(b)[:, 0:256].rearrange("p (t n) -> p t n", t=2), ACT.Copy), t2)
                    bank_free[b] = [k]
                done(slot, t_nt)
                dve.wait(k)
                top16(S, TS, TIi, [tt * 16 + 4 * ui + m for tt in range(2) for m in range(4)])
                hs = slice(2 * ui, 2 * ui + 2)
                rows = [tt * 8 + h for tt in range(2) for h in (2 * ui, 2 * ui + 1)]
                for tt in range(2):
                    r = slice(tt * 16 + 4 * ui, tt * 16 + 4 * ui + 4)
                    dve.do(lambda e, r=r: e.tensor_copy(TF[:, r, :], TIi[:, r, :]))
                    v = CA[:, tt * 8 + 2 * ui:tt * 8 + 2 * ui + 2, :].rearrange("p h (a b) -> p h a b", a=16)
                    t = dve.do(lambda e, v=v, tt=tt, hs=hs: e.tensor_tensor(
                        v, bc(tsv[:, tt, hs, 0, :].unsqueeze(3), [128, 2, 16, 16]),
                        bc(tsv[:, tt, hs, 1, :].unsqueeze(2), [128, 2, 16, 16]), ALU.add))
                dve.wait(t)
                top16(CA, BS, BJ, rows)
                bj, ba = by_tt(BJ)[:, :, hs, :], by_tt(BA)[:, :, hs, :]
                for c, (n, op) in enumerate(((4, ALU.logical_shift_right), (15, ALU.bitwise_and))):
                    bf = by_tt(BF[:, c])[:, :, hs, :]
                    chain(lambda e, ba=ba, bj=bj, n=n, op=op: e.tensor_scalar(ba, bj, n, None, op))
                    chain(lambda e, bf=bf, ba=ba: e.tensor_copy(bf, ba))
                for c in range(2):
                    for f in range(3):
                        for tt in range(2):
                            q = CA[:, tt * 8 + 2 * ui:tt * 8 + 2 * ui + 2, :].rearrange("p h (k a) -> p h k a", k=16)
                            if f == 0:
                                bf = BF[:, c, tt * 8 + 2 * ui:tt * 8 + 2 * ui + 2, :]
                                k = dve.do(lambda e, q=q, bf=bf: e.tensor_tensor(
                                    q, bc(bf.unsqueeze(3), [128, 2, 16, 16]),
                                    bc(co["iota"][:, 0:16].unsqueeze(1).unsqueeze(1), [128, 2, 16, 16]), ALU.is_equal), t)
                            elif f == 1:
                                k = dve.do(lambda e, q=q, tt=tt, c=c, hs=hs: e.tensor_tensor(
                                    q, q, bc(tfv[:, tt, hs, c, :].unsqueeze(2), [128, 2, 16, 16]), ALU.mult), t)
                            else:
                                ii = II[:, c, tt, 32 * ui:32 * ui + 32].rearrange("p (h k) -> p h k", h=2)
                                k = dve.do(lambda e, q=q, ii=ii: e.tensor_reduce(ii, q, AX, ALU.add), t)
                        t = k
            t_xl = pool.do(lambda e: e.tensor_tensor(XLt[:, :], NTs[:, :], XHt[:, :].bitcast(F32), ALU.subtract), t_nt, t_xh)
            chain(lambda e: e.tensor_tensor(BG, BS, bc(BS[:, :, 0:1], [128, 16, 16]), ALU.subtract))
            chain(lambda e: e.activation(BG, BG, ACT.Exp), act)
            chain(lambda e: e.tensor_reduce(gs[:, 0, :], BG, AX, ALU.add))
            chain(lambda e: e.reciprocal(gs[:, 1, :], gs[:, 0, :]))
            chain(lambda e: e.tensor_tensor(BG, BG, bc(gs[:, 1, :].unsqueeze(2), [128, 16, 16]), ALU.mult))
            bg = BG.rearrange("p (t h) k -> p t (h k)", t=2)
            for n, (src, dst) in enumerate(((II[:, 0], I1T), (II[:, 1], I2T), (bg, GTT))):
                for tt in range(2):
                    t1 = pe.do(tr(P(n)[:, tt * 128:tt * 128 + 128], src[:, tt, :]), t)
                act.do(lambda e, n=n, dst=dst: e.activation(dst, P(n)[:, 0:256], ACT.Copy), t1)
            bar()

            UR = Wk[:, 0:3072].rearrange("p (b n) -> p b n", b=3)
            VR = Wk[:, 3072:6144].rearrange("p (b n) -> p b n", b=3)
            ULt, VLt = rounded("UL", "Wk", 0, 3072), rounded("VL", "Wk", 3072, 3072)
            UHt, VHt = rounded("UH", "Wk", 6144, 2048), rounded("VH", "CO", 0, 2048)
            WHt, WLt = rounded("WH", "RW", 0, 512), rounded("WL", "RW", 512, 512)
            UL, VL = (v[:, :].rearrange("p (b n) -> p b n", b=3) for v in (ULt, VLt))
            UH, VH = (v[:, :].rearrange("p (b n) -> p b n", b=2) for v in (UHt, VHt))
            WH, WL = (v[:, :].rearrange("p (b n) -> p b n", b=2) for v in (WHt, WLt))
            GE = Wk[:, 8192:8704].rearrange("p (b n) -> p b n", b=2)
            us, vs = [sem(f"us{i}") for i in range(3)], [sem(f"vs{i}") for i in range(3)]
            s1, s2 = {}, {}

            def fetch(i):
                s = i % 3
                sp.raw(lambda e: e.dma_start(UR[:, s], peer_u[i]).then_inc(us[s], 16), s1.get(i - 3))
                sp.raw(lambda e: e.dma_start(VR[:, s], peer_v[:, i, :]).then_inc(vs[s], 16), s2.get(i - 3))

            sp.wait(*(q.last() for q in qs))
            for i in range(3):
                fetch(i)

            C = AR[:, :].rearrange("p (t n) -> p t n", t=256)
            OA = Wk[:, 6144:7168].rearrange("p (b k n) -> p b k n", b=2, k=4)
            OB = Wk[:, 7168:8192].rearrange("p (b k n) -> p b k n", b=2, k=4)
            io = co["iota"]
            oh_free, pf = [None, None], [None] * 4
            for g in range(64):
                b = g % 2
                for k in range(4):
                    tok = g * 4 + k
                    ta = dve.do(lambda e, b=b, k=k, tok=tok: e.tensor_scalar(OA[:, b, k, :], io, I1T[:, tok:tok + 1],
                                                                            GTT[:, tok:tok + 1], ALU.is_equal, ALU.mult), oh_free[b])
                for k in range(4):
                    tok = g * 4 + k
                    q = pool if k == 3 else dve
                    tb = q.do(lambda e, b=b, k=k, tok=tok: e.tensor_scalar(OB[:, b, k, :], io, I2T[:, tok:tok + 1], None,
                                                                          ALU.is_equal), oh_free[b])
                pb = 4 + g % 4
                for k in range(4):
                    t = pe.do(mm(P(pb)[:, k * 128:k * 128 + 128], OA[:, b, k, :], OB[:, b, k, :], True, True), dve.last(), tb,
                              pf[g % 4])
                oh_free[b] = t
                pf[g % 4] = act.do(lambda e, g=g, pb=pb: e.activation(C[:, 4 * g:4 * g + 4, :],
                                                                     P(pb).rearrange("p (k n) -> p k n", k=4), ACT.Copy), t)
            t_c = act.last()
            act.wait(pe.last(), dve.last(), pool.last())
            dve.wait(t_c, pe.last(), pool.last())

            def split(raw, high, low, arrived, high_free):
                a = act.do(lambda e: e.activation(high, raw, ACT.Copy), arrived, high_free)
                return dve.do(lambda e: e.tensor_tensor(low, raw, high.bitcast(F32), ALU.subtract), a, arrived)

            def three(o, lh, ll, rh, rl, first, last, inc):
                pe.raw(mm(o, lh, rh, first, False))
                pe.raw(mm(o, lh, rl, False, False))
                f = mm(o, ll, rh, False, last)
                return pe.do(f) if inc else pe.raw(f)

            u_tok, v_tok, w_tok, sf = {}, {}, {}, {}

            def split_u(i):
                u_tok[i] = split(UR[:, i % 3], UH[:, i % 2], UL[:, i % 3], (us[i % 3], 16 * (i // 3 + 1)), s1.get(i - 2))

            def stage1(i):
                o = P(4 + i % 4)[:, 0:256]
                pe.wait(u_tok[i], t_xl, sf.get(i - 4), *pf)
                for c in range(8):
                    cs = slice(c * 128, c * 128 + 128)
                    s1[i] = three(o, UH[:, i % 2, cs], UL[:, i % 3, cs], XH[:, c, :], XL[:, c, :], c == 0, c == 7, c == 7)
                v_tok[i] = split(VR[:, i % 3], VH[:, i % 2], VL[:, i % 3], (vs[i % 3], 16 * (i // 3 + 1)), s2.get(i - 2))
                b = i % 2
                g = GE[:, b, :]
                sf[i] = act.do(lambda e: e.activation(g, o, ACT.Gelu), s1[i], w_tok.get(i - 2))
                t = dve.do(lambda e: e.tensor_tensor(g, g, C[:, :, i], ALU.mult), sf[i])
                t = act.do(lambda e: e.activation(WH[:, b, :], g, ACT.Copy), t, s2.get(i - 2))
                w_tok[i] = dve.do(lambda e: e.tensor_tensor(WL[:, b, :], g, WH[:, b, :].bitcast(F32), ALU.subtract), t)

            def stage2(i):
                b = i % 2
                pe.wait(w_tok[i], v_tok[i])
                for tt in range(2):
                    ts_ = slice(tt * 128, tt * 128 + 128)
                    for j in range(2):
                        js = slice(j * 512, j * 512 + 512)
                        s2[i] = three(P(2 * tt + j), WH[:, b, ts_], WL[:, b, ts_], VH[:, b, js], VL[:, i % 3, js], i == 0, i == 127,
                                      tt == 1 and j == 1)
                if i + 3 < 128:
                    fetch(i + 3)

            split_u(0)
            for i in range(128):
                if i < 127:
                    split_u(i + 1)
                stage1(i)
                if i:
                    stage2(i - 1)
            stage2(127)
            t_f = load(act, UR[:, 0], fin2, s1[127], s2[127])
            bar()
            for tt in range(2):
                for j in range(2):
                    h = H[:, tt, j * 512:(j + 1) * 512]
                    dve.do(lambda e, h=h, b=2 * tt + j: e.tensor_tensor(h, P(b), h, ALU.add))
            bar()
            dve.wait(t_f)
            last_norm(UR[:, 0], XS)

        for n, f in enumerate((mixers, experts, mixers2, cross, peer)):
            f()
            if stage == n + 1 and stage < 5:
                finish(H)
                break
        else:
            finish(None)
        emit()


def constants():
    import numpy as np
    p = np.arange(128)
    a = p[:, None]
    b = p[None, :]
    d = {}
    d["ident"] = (a == b)
    d["tri"] = (a <= b)
    d["neg"] = np.where(a < b, 0.0, -1e30)
    d["m01"] = (a < b)
    d["negu"] = -1.0 * (a >= b)
    d["neg1"] = -np.ones((128, 128))
    d["one"] = np.ones((128, 128))
    k2 = np.arange(256)[None, :]
    d["dist"] = np.concatenate([np.where(b <= a, b - a, -1e30), np.where(k2 <= a + 128, k2 - a - 128.0, -1e30)], 1)
    slope = 2.0 ** -np.arange(1.0, 9.0)
    cpos = np.arange(8) * 32 + 31
    q = np.stack([p, p + 128], 1)
    dc = q[:, :, None] - cpos
    d["cmpb"] = np.where(dc[:, :, None, :] >= 0, -slope[None, None, :, None] * dc[:, :, None, :], -1e30)
    d["cmpv"] = dc >= 0
    hc = np.arange(64)[:, None]
    bd = np.zeros((128, 512))
    bd[:64] = (hc // 8) == (np.arange(512)[None, :] // 64)
    d["bd"] = bd
    es = np.zeros((128, 64))
    es[:8] = (hc.T % 8) == np.arange(8)[:, None]
    d["esel"] = es
    d["iota"] = np.broadcast_to(b, (128, 128))
    return np.concatenate([np.asarray(d[k], np.float32).reshape(128, -1) for k in NC_CONST], 1)


def layout(i):
    import numpy as np
    f = {k: np.asarray(v) for k, v in i.items()}

    def pc(v):
        return v.reshape(128, -1)

    def tile(v):
        return np.broadcast_to(v.reshape(1, -1), (128, v.size))

    small = dict(g_attn=pc(f["attn_norm_g"][0]),
                 g_mix=pc(np.concatenate([f["sb_out_norm_g"][0], f["sg_out_norm_g"][0]])),
                 g_ffn=pc(f["ffn_norm_g"][0]), g_nmix=pc(f["norm_mix_2"][0]), g_sub=pc(f["diff_subln_2"][0]),
                 g_cross=pc(f["norm_cross_2"][0]), g_mem=pc(f["norm_mem_2"][0]), g_peer=pc(f["norm_ffn_2"][0]),
                 bsp=f["b_spatial"][0].T, pos=np.concatenate([f["nsa_cmp_pos_2"][0].T] * 2, 0),
                 lam=tile(f["diff_lambda_2"][0]),
                 rb=tile(np.concatenate([f["b_router_group"][0], f["b_router_expert"][0].reshape(-1)])))
    rows = dict(sg=tile(f["sg_norm_g"][0]), fin1=tile(f["final_norm_g"]))

    def units(w):
        return np.ascontiguousarray(w.reshape(128, 8, -1, 512).transpose(2, 0, 1, 3)).reshape(-1, 128, 4096)

    w2 = f["w_in_2"][0]
    qa, ka, va, qb, kv, gb, ga, gbb = np.split(w2, np.cumsum([512, 512, 512, 512, 768, 24, 1024]), axis=1)
    qb = qb.reshape(1024, 2, 4, 64).transpose(0, 2, 1, 3).reshape(1024, 512)
    kv = kv.reshape(1024, 6, 2, 64)
    kva = np.concatenate([kv[:, 0, 0], kv[:, 1, 0], kv[:, 0, 1], kv[:, 1, 1], kv[:, 2, 0], kv[:, 2, 1],
                          kv[:, 4, 0], kv[:, 4, 1]], 1)
    kvb = np.concatenate([kv[:, 3, 0], kv[:, 3, 1], kv[:, 5, 0], kv[:, 5, 1], gb, np.zeros((1024, 232), w2.dtype)], 1)
    w_in2 = units(np.concatenate([qa, ka, va, qb, kva, kvb, ga, gbb], 1))
    wr = np.concatenate([f["w_router_group"][0], f["w_router_expert"][0].transpose(1, 0, 2).reshape(1024, 32)], 1)
    c1 = np.concatenate([f["nsa_ck_w1_2"][0].reshape(32, 64, 256), f["nsa_cv_w1_2"][0].reshape(32, 64, 256)], 1)
    c1 = c1.reshape(2, 16, 128, 256).transpose(0, 2, 1, 3).reshape(2, 128, 4096)
    c2 = np.stack([f["nsa_ck_w2_2"][0].reshape(2, 128, 64), f["nsa_cv_w2_2"][0].reshape(2, 128, 64)], 0)
    a = dict(
        x=f["x"][0], fin2=tile(f["norm_final_2"]), const=constants(), small=np.concatenate([small[k] for k in NC_SMALL], 1),
        rows=np.concatenate([rows[k] for k in NC_ROWS], 1),
        w_in=units(f["w_in"][0]), w_sp=f["w_spatial"][0].transpose(2, 0, 1).reshape(128, 1024), w_out=units(f["w_out"][0]),
        w_r=wr.reshape(128, 288), w_gate=f["w_gate"].reshape(32, 1024, 512), w_up=f["w_up"].reshape(32, 1024, 512),
        w_down=f["w_down"].reshape(32, 512, 1024), mem=f["mem_2"][0], w_in2=w_in2, ck1=c1,
        ck2=c2.transpose(2, 0, 1, 3).reshape(128, 256), w_a=f["w_branch_a_2"][0], w_b=f["w_branch_b_2"][0],
        w_out2=units(f["w_out_2"][0]), w_cq=units(f["w_cross_q_2"][0]), w_ckv=units(f["w_cross_kv_2"][0]),
        w_co=f["w_cross_o_2"][0], w_pq=units(f["peer_wq_2"][0]),
        subk=f["peer_subkeys_2"][0].transpose(3, 0, 1, 2).reshape(128, 2048),
        peer_u=f["peer_u_2"][0].reshape(128, 128, 128, 8).transpose(1, 2, 3, 0).reshape(128, 128, 1024),
        peer_v=f["peer_v_2"][0].reshape(128, 128, 1024),
    )
    return {k: np.ascontiguousarray(v) for k, v in a.items()}


STAGE = 5


def kernel(**inputs):
    import numpy as np
    import concourse.bacc as bacc
    from concourse.bass_utils import run_bass_kernel_spmd

    nc = bacc.Bacc("TRN2", target_bir_lowering=False, num_devices=1)
    arrays, args = {}, {}
    for name, a in layout(inputs).items():
        arrays[f"in_{name}"] = a
        args[name] = nc.dram_tensor(f"in_{name}", a.shape, mybir.dt.from_np(a.dtype), kind="ExternalInput").ap()
    args["out"] = nc.dram_tensor("out_0", (256, D), F32, kind="ExternalOutput").ap()
    program(nc, STAGE, **args)
    r = run_bass_kernel_spmd(nc, [arrays], core_ids=[0])
    return np.asarray(r.results[0]["out_0"]).reshape(1, 256, D)
```

```python
from contextlib import ExitStack

import concourse.bass as bass
from concourse import mybir

F32 = mybir.dt.float32
F32R = mybir.dt.float32r
U32 = mybir.dt.uint32
ALU = mybir.AluOpType
ACT = mybir.ActivationFunctionType
AX = mybir.AxisListType.X

EPS = 1e-6
SLOTS = 64
D = 1024
NC_CONST = dict(ident=128, tri=128, neg=128, m01=128, negu=128, neg1=128, one=128, dist=384, cmpb=128, cmpv=16,
                bd=512, esel=64, iota=128, sel=16, pst=16, plen=16)
NC_SMALL = dict(g_attn=8, g_mix=8, g_ffn=8, g_nmix=8, g_sub=1, g_cross=8, g_mem=8, g_peer=8, bsp=8, pos=32,
                lam=256, rb=36)
NC_ROWS = dict(sg=512, fin1=1024)


class Queue:

    def __init__(self, sem):
        self.sem, self.n, self.items, self.seen = sem, 0, [], {}

    def wait(self, *tokens):
        for t in tokens:
            if t is None:
                continue
            sem, v = t
            if self.seen.get(id(sem), 0) < v:
                self.seen[id(sem)] = v
                self.items.append(lambda e, sem=sem, v=v: e.wait_ge(sem, v))

    def raw(self, f, *tokens):
        self.wait(*tokens)
        self.items.append(f)

    def do(self, f, *tokens):
        self.wait(*tokens)
        self.n += 1
        self.items.append(lambda e: f(e).then_inc(self.sem, 1))
        return (self.sem, self.n)

    def last(self):
        return (self.sem, self.n) if self.n else None

    def branch(self, sem, flag):
        q = Queue(sem)
        q.seen = dict(self.seen)
        self.items.append((flag, q.items))
        return q


def replay(e, items):
    for f in items:
        if isinstance(f, tuple):
            v = e.value_load(f[0], min_val=0, max_val=1)
            with e.If(v > 0):
                replay(e, f[1])
        else:
            f(e)


def program(nc, x, const, small, rows, w_in, w_sp, w_out, w_r, w_gate, w_up, w_down, mem, w_in2, ck1, ck2,
            w_a, w_b, w_out2, w_cq, w_ckv, w_co, w_pq, subk, peer_u, peer_v, fin2, out):
    ctx = ExitStack()
    with ctx:
        place = {}

        def sb(name, shape, dt=F32):
            t = ctx.enter_context(nc.sbuf_tensor(name, shape, dt))
            place[name] = nc.sbuf_base - 4 * shape[1]
            return t

        def rounded(name, over, at, n):
            return nc.alloc_sbuf_tensor_at(name, [128, n], F32R, offset=place[over] + 4 * at)

        def sem(name):
            return ctx.enter_context(nc.semaphore(name))

        NR, NS = 6, 7
        AR = sb("AR", [128, 8 * 4096])
        Wk = sb("Wk", [128, 9200])
        Hs = sb("Hs", [128, 2 * D])
        XSs = sb("XSs", [128, 2 * D])
        NTs = sb("NTs", [128, 8 * 256])
        CO = sb("CO", [128, sum(NC_CONST.values())])
        SM = sb("SM", [128, sum(NC_SMALL.values())])
        RW = sb("RW", [128, sum(NC_ROWS.values())])
        ST = sb("ST", [128, 64])
        PSt = ctx.enter_context(nc.psum_tensor("PS", [128, 8 * 512], F32))

        def parts(t, widths):
            at, d = 0, {}
            for k, n in widths.items():
                d[k] = t[:, at:at + n]
                at += n
            return d

        co, sm, rw = parts(CO, NC_CONST), parts(SM, NC_SMALL), parts(RW, NC_ROWS)
        ident = co["ident"]
        H = Hs[:, :].rearrange("p (t d) -> p t d", t=2)
        XS = XSs[:, :].rearrange("p (t d) -> p t d", t=2)
        NT = NTs[:, :].rearrange("p (c t) -> p c t", c=8)

        def P(b, n=1):
            return PSt[:, b * 512:(b + n) * 512]

        pe, act, dve, pool = (Queue(sem(f"s_{n}")) for n in ("pe", "act", "dve", "pool"))
        sp = Queue(sem("s_sp"))
        qs = (pe, act, dve, pool)

        def bar():
            for a in qs:
                for b in qs:
                    a.wait(b.last())

        nload = [0]

        def load(q, dst, src, *tokens):
            nload[0] += 1
            s = sem(f"ld{nload[0]}")
            q.raw(lambda e: e.dma_start(dst, src).then_inc(s, 16), *tokens)
            return (s, 16)

        ring_sem = [sem(f"ring{i}") for i in range(NS)]
        ring_free, ring_uses = [[] for _ in range(NS)], [0] * NS
        ring_next, slots, arrived = [0], [4], []

        def unit(src, shape_str, **kw):
            s = ring_next[0] % slots[0]
            ring_next[0] = s + 1
            ring_uses[s] += 1
            npart = src.shape[0]
            cols = 1
            for z in src.shape[1:]:
                cols *= z
            dst = AR[0:npart, s * 4096:s * 4096 + cols] if s < NR else Wk[0:npart, 4800:4800 + cols]
            to = dst.rearrange("p (a n) -> p a n", a=src.shape[1]) if len(src.shape) == 3 else dst
            sp.wait(*(arrived[-2:-1] if slots[0] == 4 else arrived[-3:-2]))
            arrived.append((ring_sem[s], 16 * ring_uses[s]))
            sp.raw(lambda e: e.dma_start(to, src).then_inc(ring_sem[s], 16), *ring_free[s])
            return dst.rearrange(shape_str, **kw), (ring_sem[s], 16 * ring_uses[s]), s

        def done(slot, *tokens):
            ring_free[slot] = list(tokens)

        class Bump:
            def __init__(self, t, lo, hi):
                self.t, self.lo, self.at, self.hi = t, lo, lo, hi

            def __call__(self, n, s=None, p=128, **kw):
                a = self.t[0:p, self.at:self.at + n]
                self.at += n
                assert self.at <= self.hi, (self.at, self.hi)
                return a.rearrange(s, **kw) if s else a

            def reset(self):
                self.at = self.lo

        wk = Bump(Wk, 0, 9200)
        w2 = Bump(AR, NR * 4096, 8 * 4096)

        def mm(o, l, r, start, stop):
            return lambda e: e.matmul(o, l, r, start=start, stop=stop, skip_group_check=True)

        def tr(o, i, n=128):
            return lambda e: e.transpose(o, i, ident[0:n, 0:n])

        def bc(ap, shape):
            return ap.broadcast_to(shape)

        t_x = load(sp, H, x.rearrange("(t p) d -> p t d", p=128))
        t_id = load(sp, CO[:, 0:128], const[:, 0:128])
        t_sm = load(sp, SM[:, :], small)
        act.wait(t_x)
        dve.wait(t_x)

        WR = Wk[:, 8900:9188].rearrange("p (c n) -> p c n", c=8)
        later = {}

        def load_rest():
            later["co"] = load(sp, CO[:, 128:], const[:, 128:])
            later["rw"] = load(sp, RW[:, :], rows)
            later["wr"] = load(sp, WR, w_r.rearrange("p (c n) -> p c n", c=8))

        def rstd(ss, n, width, *tokens):
            a = dve.do(lambda e: e.tensor_scalar(ss, ss, 1.0 / width, EPS, ALU.mult, ALU.add), *tokens)
            b = act.do(lambda e: e.activation(ss, ss, ACT.Sqrt), a)
            return dve.do(lambda e: e.reciprocal(ss, ss), b)

        def square_sum(src, junk, ss, *tokens):
            return act.do(lambda e: e.activation(junk, src, ACT.Square, accum_out=ss), *tokens)

        def rms(src):
            a = square_sum(src[:, 0, :], XS[:, 0, :], ST[:, 0:1])
            b = dve.do(lambda e: e.tensor_tensor_reduce(XS[:, 1, :], src[:, 1, :], src[:, 1, :], 1.0, 0.0, ALU.mult, ALU.add,
                                                        ST[:, 1:2]))
            return rstd(ST[:, 0:2], 2, D, a, b)

        def turn_all(src, dst, nchunk, gain, first_bank, strided, *tokens):
            toks = []
            for pair in range(nchunk // 2):
                bank = P(first_bank + pair).rearrange("p (c t) -> p c t", c=2)
                for k in range(2):
                    c = 2 * pair + k
                    for tt in range(2):
                        s = src[:, tt, c::nchunk] if strided else src[:, tt, c * 128:(c + 1) * 128]
                        t = pe.do(tr(bank[:, k, tt * 128:(tt + 1) * 128], s), *tokens)
                if gain is None:
                    o = dst[:, 2 * pair:2 * pair + 2, :]
                    if pair % 2:
                        toks.append(act.do(lambda e, o=o, bank=bank: e.activation(o, bank, ACT.Copy), t))
                    else:
                        toks.append(dve.do(lambda e, o=o, bank=bank: e.tensor_copy(o, bank), t))
                else:
                    for k in range(2):
                        c = 2 * pair + k
                        toks.append(dve.do(lambda e, c=c, k=k, bank=bank: e.tensor_scalar(
                            dst[:, c, :], bank[:, k, :], gain(c), None, ALU.mult), t))
            return toks

        def norm_turn(src, dst, gain):
            r = rms(src)
            for tt in range(2):
                t = dve.do(lambda e, tt=tt: e.tensor_scalar(XS[:, tt, :], src[:, tt, :], ST[:, tt:tt + 1], None, ALU.mult), r)
            turn_all(XS, dst, 8, lambda c: gain[:, c:c + 1], 0, True, t)
            bar()

        def proj(o, lhs, rhs, n, *tokens, q=pe):
            q.wait(*tokens)
            for c in range(n):
                f = mm(o, lhs(c), rhs(c), c == 0, c == n - 1)
                if c < n - 1:
                    q.raw(f)
                else:
                    return q.do(f)

        bank_free = [[] for _ in range(8)]

        x_tok = {}

        def three(o, lh, ll, rh, rl, first, last, inc):
            pe.raw(mm(o, lh, rh, first, False))
            pe.raw(mm(o, lh, rl, False, False))
            f = mm(o, ll, rh, False, last)
            return pe.do(f) if inc else pe.raw(f)

        HI = [rounded(f"HI{i}", "AR", (4 + i) * 4096, 4096) for i in range(2)]
        LO = [rounded(f"LO{i}", "AR", i * 4096, 4096) for i in range(4)]
        hi_n = [0]
        XHt, XLt = rounded("XH", "XSs", 0, 2048), rounded("XL", "NTs", 0, 2048)
        X2 = tuple(v[:, :].rearrange("p (c t) -> p c t", c=8) for v in (XHt, XLt))

        def split_unit(src, rest=dve):
            w, tw, slot = unit(src, "p (a n) -> p a n", a=4)
            h = hi_n[0] % 2
            hi_n[0] += 1
            hi, lo = HI[h][:, :], LO[slot][:, :]
            toks = []
            for k in range(4):
                cs = slice(1024 * k, 1024 * k + 1024)
                a = act.do(lambda e, k=k, cs=cs: e.activation(hi[:, cs], w[:, k, :], ACT.Copy), tw, *ring_free[4 + h])
                toks.append(rest.do(lambda e, k=k, cs=cs: e.tensor_tensor(lo[:, cs], w[:, k, :], hi[:, cs].bitcast(F32), ALU.subtract),
                                   a, tw))
            return (hi.rearrange("p (c n) -> p c n", c=8), lo.rearrange("p (c n) -> p c n", c=8), toks, slot, 4 + h)

        def release(u, t):
            done(u[3], t)
            done(u[4], t)

        def proj_turned(u, X, dst, banks, scale=None):
            wh, wl, tw, _, _ = u
            for m in range(4):
                b = banks[m % len(banks)]
                o = P(b)[:, 0:256]
                ms = slice(m * 128, m * 128 + 128)
                pe.wait(*bank_free[b])
                for c in range(8):
                    pe.wait(tw[c // 2], x_tok[id(X), c])
                    t = three(o, wh[:, c, ms], wl[:, c, ms], X[0][:, c, :], X[1][:, c, :], c == 0, c == 7, c == 7)
                bank_free[b] = [act.do(lambda e, m=m, o=o: e.activation(dst[:, m, :], o, ACT.Copy, scale=scale or 1.0), t)]
            release(u, t)

        def proj_tokens(u, X, banks, evac, ncol=512):
            wh, wl, tw, _, _ = u
            for tt in range(2):
                b = banks[tt]
                o = P(b)[:, 0:ncol]
                xs = slice(tt * 128, tt * 128 + 128)
                pe.wait(*bank_free[b])
                for c in range(8):
                    pe.wait(tw[c // 2], x_tok[id(X), c])
                    t = three(o, X[0][:, c, xs], X[1][:, c, xs], wh[:, c, 0:ncol], wl[:, c, 0:ncol], c == 0, c == 7, c == 7)
                bank_free[b] = [evac(tt, o, t)]
            release(u, t)

        def run(jobs, *us):
            us = list(us) or [split_unit(jobs[0][0])]
            for i, (_, f) in enumerate(jobs):
                if len(us) < min(i + 2, len(jobs)):
                    us.append(split_unit(jobs[i + 1][0]))
                f(us[i])

        def add_residual(X, units):
            for j, u in enumerate(units):
                def evac(tt, o, t, j=j):
                    h = H[:, tt, j * 512:(j + 1) * 512]
                    return dve.do(lambda e: e.tensor_tensor(h, o, h, ALU.add), t)
                proj_tokens(u, X, [4 + 2 * j, 5 + 2 * j], evac)

        def turn_split(src, X, gain, *tokens):
            for c in range(8):
                for tt in range(2):
                    o = P(c // 2)[:, (c % 2) * 256 + tt * 128:(c % 2) * 256 + tt * 128 + 128]
                    t = pe.do(tr(o, src[:, tt, c::8]), *tokens, *bank_free[c // 2])
            for b in range(4):
                bank = P(b).rearrange("p (c t) -> p c t", c=2)
                for k in range(2):
                    c = 2 * b + k
                    g = 1.0 if gain is None else gain[:, c:c + 1]
                    a = act.do(lambda e, c=c, k=k, g=g, bank=bank: e.activation(X[0][:, c, :], bank[:, k, :], ACT.Copy, scale=g), t)
                for k in range(2):
                    c = 2 * b + k
                    g = 1.0 if gain is None else gain[:, c:c + 1]
                    d = dve.do(lambda e, c=c, k=k, g=g, bank=bank: e.scalar_tensor_tensor(
                        X[1][:, c, :], bank[:, k, :], g, X[0][:, c, :].bitcast(F32), ALU.mult, ALU.subtract), a)
                    x_tok[id(X), c] = d
                bank_free[b] = [d]

        def norm_split(src, X, gain):
            bar()
            r = rms(src)
            t0 = act.do(lambda e: e.activation(XS[:, 0, :], src[:, 0, :], ACT.Copy, scale=ST[:, 0:1]), r)
            t1 = dve.do(lambda e: e.tensor_scalar(XS[:, 1, :], src[:, 1, :], ST[:, 1:2], None, ALU.mult), r)
            turn_split(XS, X, gain, t0, t1)

        def copy_out(dst):
            return lambda tt, o, t: act.do(lambda e: e.activation(dst[:, tt, :], o, ACT.Copy), t)

        def finish():
            t = dve.last()
            s = sem("s_out")
            sp.raw(lambda e: e.dma_start(out.rearrange("(t p) d -> p t d", p=128), XS).then_inc(s, 16), t)
            sp.raw(lambda e: e.wait_ge(s, 16))

        def emit():
            with nc.Block() as block:
                for q, reg in ((sp, block.sync), (pe, block.tensor), (act, block.scalar), (dve, block.vector),
                               (pool, block.gpsimd)):
                    @reg
                    def _(e, q=q):
                        replay(e, q.items)

        def w8s(src, i):
            return split_unit(src[i])

        def mixers():
            for q in qs:
                q.wait(t_id, t_sm)
            norm_split(H, X2, sm["g_attn"])
            qT = wk(1024, "p (m t) -> p m t", m=4)
            kT = wk(1024, "p (m t) -> p m t", m=4)
            V1 = wk(1024, "p (t n) -> p t n", t=2)
            WS = wk(1024, "p (h t) -> p h t", h=8)
            MX = wk(2048, "p (t n) -> p t n", t=2)
            U1 = wk(1024, "p (t n) -> p t n", t=2)
            SP = w2(3072)
            T1 = w2(3072)
            VG = w2(1024, "p (t n) -> p t n", t=2)
            def gelu_out(dst):
                return lambda tt, o, t: act.do(lambda e: e.activation(dst[:, tt, :], o, ACT.Gelu_apprx_tanh), t)

            blocks = [(0, 0), (0, 1), (1, 1)]
            sptok, ztok = [], []

            def scores():
                pe.wait(*(t for b in range(6) for t in bank_free[b]))
                for b, (kt, qt) in enumerate(blocks):
                    for h in range(8):
                        r = slice(64 * (h % 2), 64 * (h % 2) + 64)
                        o = P(2 * b + h % 2)[:, (h // 2) * 128:(h // 2) * 128 + 128]
                        t = pe.do(mm(o, kT[r, h // 2, kt * 128:kt * 128 + 128], qT[r, h // 2, qt * 128:qt * 128 + 128],
                                     h < 2, False))
                    ztok.append(t)

            def softplus():
                for k in range(3):
                    for b in range(3):
                        z, l = P(2 * b, 2), T1[:, b * 1024:(b + 1) * 1024]
                        if k == 0:
                            t = act.do(lambda e, l=l, z=z: e.activation(l, z, ACT.Abs), ztok[b])
                        elif k == 1:
                            t = act.do(lambda e, l=l: e.activation(l, l, ACT.Exp, scale=-1.0), t)
                        else:
                            sptok.append(act.do(lambda e, l=l: e.activation(l, l, ACT.Ln, bias=1.0), t))
                for b, (kt, qt) in enumerate(blocks):
                    z, l, s = P(2 * b, 2), T1[:, b * 1024:(b + 1) * 1024], SP[:, b * 1024:(b + 1) * 1024]
                    t = dve.do(lambda e, s=s, z=z, l=l: e.scalar_tensor_tensor(s, z, 0.0, l, ALU.max, ALU.add), sptok[b])
                    if kt == qt:
                        v = s.rearrange("p (h t) -> p h t", h=8)
                        m = bc(co["m01"].unsqueeze(1), [128, 8, 128])
                        t = dve.do(lambda e, v=v, m=m: e.tensor_tensor(v, v, m, ALU.mult), t, later["co"])
                    sptok[b] = t

            def split(i):
                return split_unit(w_in[i])

            u = [split(0)]
            load_rest()
            t_ws = load(sp, WS, w_sp.rearrange("p (h t) -> p h t", h=8))
            u.append(split(1))
            proj_turned(u[0], X2, qT, [0, 1], 0.125)
            u.append(split(2))
            proj_turned(u[1], X2, kT, [2, 3])
            u.append(split(4))
            for q in qs:
                q.wait(later["co"], later["rw"])
            scores()
            softplus()
            proj_tokens(u[2], X2, [6, 7], copy_out(V1))
            u.append(split(3))
            proj_tokens(u[3], X2, [6, 7], gelu_out(VG))
            t = act.last()
            ts = [square_sum(VG[:, tt, :], MX[:, tt, 512:1024], ST[:, 4 + tt:5 + tt], t) for tt in range(2)]
            tw = pool.do(lambda e: e.tensor_tensor(WS, WS, bc(co["tri"].unsqueeze(1), [128, 8, 128]), ALU.mult), t_ws)
            uo = [w8s(w_out, 0)]
            proj_tokens(u[4], X2, [6, 7], gelu_out(U1))
            r = rstd(ST[:, 4:6], 2, 512, *ts)
            tv = [dve.do(lambda e, tt=tt: e.scalar_tensor_tensor(VG[:, tt, :], VG[:, tt, :], ST[:, 4 + tt:5 + tt], rw["sg"],
                                                                 ALU.mult, ALU.mult), r) for tt in range(2)]
            atok = []
            for b in range(3):
                for j in range(2):
                    o = P(2 * b + j)
                    s = SP[:, b * 1024 + j * 512:b * 1024 + (j + 1) * 512]
                    t = pe.do(mm(o, co["negu"], s, False, b != 1), *sptok)
                    if b == 1:
                        s = SP[:, 2048 + j * 512:2048 + (j + 1) * 512]
                        t = pe.do(mm(o, co["neg1"], s, False, True))
                z = P(2 * b, 2)
                l = T1[:, b * 1024:(b + 1) * 1024]
                if b != 1:
                    v = l.rearrange("p (h t) -> p h t", h=8)
                    zv = z.rearrange("p (h t) -> p h t", h=8)
                    m = bc(co["neg"].unsqueeze(1), [128, 8, 128])
                    t = dve.do(lambda e, v=v, zv=zv, m=m: e.tensor_tensor(v, zv, m, ALU.min), t)
                    z = l
                atok.append(act.do(lambda e, l=l, z=z: e.activation(l, z, ACT.Exp), t))
            A = T1.rearrange("p (b h t) -> p b h t", b=3, h=8)
            for h in range(8):
                o = P(6 + h // 4)[:, (h % 4) * 128:(h % 4) * 128 + 128].rearrange("p (c d) -> p c d", c=2)
                t = pe.do(mm(o, WS[:, h, :], VG[:, :, h * 64:h * 64 + 64], True, True), tw, *tv, *bank_free[6], *bank_free[7])
            for c in range(2):
                o = P(6, 2).rearrange("p (h c d) -> p h c d", h=8, c=2)[:, :, c, :]
                v = MX[:, c, 512:1024].rearrange("p (h d) -> p h d", h=8)
                u = U1[:, c, :].rearrange("p (h d) -> p h d", h=8)
                bb = bc(sm["bsp"].unsqueeze(2), [128, 8, 64])
                t1 = dve.do(lambda e, o=o, v=v, bb=bb: e.tensor_tensor(v, o, bb, ALU.add), t)
                t1 = dve.do(lambda e, v=v, u=u: e.tensor_tensor(v, v, u, ALU.mult), t1)
            for h in range(8):
                i = h % 2 * 4 + h // 2
                cs = slice(h * 64, h * 64 + 64)
                pe.raw(mm(P(0)[:, cs], A[:, 0, i, :], V1[:, 0, cs], True, True), *atok)
                pe.raw(mm(P(1)[:, cs], A[:, 1, i, :], V1[:, 0, cs], True, False))
                t_pv = pe.do(mm(P(1)[:, cs], A[:, 2, i, :], V1[:, 1, cs], False, True))
            uo.append(w8s(w_out, 1))
            ts = []
            for tt in range(2):
                ts.append(square_sum(P(tt), SP[:, 1024 * tt:1024 * tt + 512], ST[:, 8 + tt:9 + tt], t_pv))
                ts.append(square_sum(MX[:, tt, 512:1024], SP[:, 1024 * tt + 512:1024 * tt + 1024], ST[:, 10 + tt:11 + tt], t1))
            r = rstd(ST[:, 8:12], 4, 512, *ts)
            for tt in range(2):
                dve.do(lambda e, tt=tt: e.tensor_scalar(MX[:, tt, 0:512], P(tt), ST[:, 8 + tt:9 + tt], None, ALU.mult), r)
                t = dve.do(lambda e, tt=tt: e.tensor_scalar(MX[:, tt, 512:1024], MX[:, tt, 512:1024], ST[:, 10 + tt:11 + tt],
                                                            None, ALU.mult), r)
            bar()
            turn_split(MX, X2, sm["g_mix"])
            add_residual(X2, uo)
            bar()

        halves, ahead = [], []

        def experts():
            wk.reset()
            wk.hi = 4800
            w2.reset()
            slots[0] = 7
            ring_next[0] = 2
            done(6, *(q.last() for q in qs))
            XGH = rounded("XGH", "AR", NR * 4096 + 6144, 2048)
            halves.append(tuple(v[:, :].rearrange("p (t d) -> p t d", t=2) for v in (XGH, XHt)))
            norm_turn(H, NT, sm["g_ffn"])
            t = act.do(lambda e: e.activation(XGH[:, :], XSs[:, :], ACT.Copy))
            t_xs = pool.do(lambda e: e.tensor_tensor(XHt[:, :], XSs[:, :], XGH[:, :].bitcast(F32), ALU.subtract), t)
            LG = wk(72, "p (t n) -> p t n", t=2)
            G8 = wk(16, "p (t n) -> p t n", t=2)
            E8 = wk(16, "p (t n) -> p t n", t=2)
            M8 = wk(32, "p (a t n) -> p a t n", a=2, t=2)
            X8 = ctx.enter_context(nc.sbuf_tensor("X8", [128, 2, 2, 8], U32))
            XF = wk(32, "p (a t n) -> p a t n", a=2, t=2)
            OG = wk(8, "p (t n) -> p t n", t=2)
            OE = wk(32, "p (a t n) -> p a t n", a=2, t=2)
            EX = wk(64, "p (t n) -> p t n", t=2)
            CB = wk(64, "p (t n) -> p t n", t=2)
            SL = wk(64, "p (t n) -> p t n", t=2)
            FL = ctx.enter_context(nc.sbuf_tensor("FL", [128, 1], mybir.dt.int32))
            sc = wk(16, "p (k t) -> p k t", t=2)
            io = co["iota"]
            t_lg = [proj(P(tt)[:, 0:36], lambda c: NT[:, c, tt * 128:tt * 128 + 128], lambda c: WR[:, c, :], 8, later["wr"]) for tt in range(2)]

            def route(tt):
                t = dve.do(lambda e, tt=tt: e.tensor_tensor(LG[:, tt, :], P(tt)[:, 0:36], sm["rb"], ALU.add), t_lg[tt])

                def chain(f, q=dve):
                    nonlocal t
                    t = q.do(f, t)

                chain(lambda e, tt=tt: e.memset(G8[:, tt, :], -3e38))
                yield
                chain(lambda e, tt=tt: e.tensor_copy(G8[:, tt, 0:4], LG[:, tt, 0:4]))
                yield
                chain(lambda e, tt=tt: e.max(M8[:, 0, tt, :], G8[:, tt, :]))
                yield
                chain(lambda e, tt=tt: e.max_index(X8[:, 0, tt, :], M8[:, 0, tt, :], G8[:, tt, :]))
                yield
                chain(lambda e, tt=tt: e.tensor_copy(XF[:, 0, tt, :], X8[:, 0, tt, :]))
                yield
                chain(lambda e, tt=tt: e.tensor_scalar(OG[:, tt, :], io[:, 0:4], XF[:, 0, tt, 0:1], None, ALU.is_equal))
                yield
                chain(lambda e, tt=tt: e.tensor_scalar(sc[:, 0, tt:tt + 1], M8[:, 0, tt, 0:1], -1.0, None, ALU.mult))
                yield
                chain(lambda e, tt=tt: e.activation(G8[:, tt, 0:4], LG[:, tt, 0:4], ACT.Exp, bias=sc[:, 0, tt:tt + 1],
                                                    accum_out=sc[:, 1, tt:tt + 1]), act)
                yield
                chain(lambda e, tt=tt: e.reciprocal(sc[:, 2, tt:tt + 1], sc[:, 1, tt:tt + 1]))
                yield
                ev = EX[:, tt, :].rearrange("p (g n) -> p g n", g=4)
                chain(lambda e, tt=tt, ev=ev: e.tensor_tensor(ev, LG[:, tt, 4:36].rearrange("p (g n) -> p g n", g=4),
                                                              bc(OG[:, tt, :].unsqueeze(2), [128, 4, 8]), ALU.mult))
                yield
                chain(lambda e, tt=tt, ev=ev: e.tensor_reduce(E8[:, tt, :], ev.rearrange("p g n -> p n g"), AX, ALU.add))
                yield
                chain(lambda e, tt=tt: e.max(M8[:, 1, tt, :], E8[:, tt, :]))
                yield
                chain(lambda e, tt=tt: e.max_index(X8[:, 1, tt, :], M8[:, 1, tt, :], E8[:, tt, :]))
                yield
                chain(lambda e, tt=tt: e.tensor_copy(XF[:, 1, tt, :], X8[:, 1, tt, :]))
                yield
                chain(lambda e, tt=tt: e.tensor_scalar(sc[:, 3, tt:tt + 1], M8[:, 1, tt, 0:1], -1.0, None, ALU.mult))
                yield
                chain(lambda e, tt=tt: e.activation(M8[:, 0, tt, 0:2], M8[:, 1, tt, 0:2], ACT.Exp, bias=sc[:, 3, tt:tt + 1],
                                                    accum_out=sc[:, 4, tt:tt + 1]), act)
                yield
                chain(lambda e, tt=tt: e.reciprocal(sc[:, 5, tt:tt + 1], sc[:, 4, tt:tt + 1]))
                yield
                chain(lambda e, tt=tt: e.tensor_scalar(M8[:, 0, tt, 0:2], M8[:, 0, tt, 0:2], sc[:, 5, tt:tt + 1],
                                                       sc[:, 2, tt:tt + 1], ALU.mult, ALU.mult))
                yield
                for k in range(2):
                    chain(lambda e, tt=tt, k=k: e.tensor_scalar(OE[:, k, tt, :], io[:, 0:8], XF[:, 1, tt, k:k + 1], None,
                                                                ALU.is_equal))
                    yield
                chain(lambda e, tt=tt: e.tensor_tensor(EX[:, tt, 0:8], OE[:, 0, tt, :], OE[:, 1, tt, :], ALU.add))
                yield
                chain(lambda e, tt=tt: e.tensor_tensor(SL[:, tt, :].rearrange("p (g n) -> p g n", g=4),
                                                       bc(EX[:, tt, 0:8].unsqueeze(1), [128, 4, 8]),
                                                       bc(OG[:, tt, :].unsqueeze(2), [128, 4, 8]), ALU.mult))
                yield
                for k in range(2):
                    chain(lambda e, tt=tt, k=k: e.tensor_scalar(OE[:, k, tt, :], OE[:, k, tt, :], M8[:, 0, tt, k:k + 1], None,
                                                                ALU.mult))
                    yield
                chain(lambda e, tt=tt: e.tensor_tensor(EX[:, tt, 0:8], OE[:, 0, tt, :], OE[:, 1, tt, :], ALU.add))
                yield
                chain(lambda e, tt=tt: e.tensor_tensor(CB[:, tt, :].rearrange("p (g n) -> p g n", g=4),
                                                       bc(EX[:, tt, 0:8].unsqueeze(1), [128, 4, 8]),
                                                       bc(OG[:, tt, :].unsqueeze(2), [128, 4, 8]), ALU.mult))
                yield
            for _ in zip(route(0), route(1)):
                pass
            bar()
            pe.raw(mm(P(0)[:, 0:32], co["m01"], SL[:, 0, :], True, True))
            pe.raw(mm(P(0)[:, 32:64], co["one"], SL[:, 0, :], True, False))
            pe.raw(mm(P(0)[:, 32:64], co["m01"], SL[:, 1, :], False, True))
            pe.raw(mm(P(0)[:, 64:96], co["one"], SL[:, 0, :], True, False))
            t = pe.do(mm(P(0)[:, 64:96], co["one"], SL[:, 1, :], False, True))
            RK = wk(64, "p (t n) -> p t n", t=2)
            CR = wk(64, "p (t n) -> p t n", t=2)
            rkf, crf = (v.rearrange("p t n -> p (t n)") for v in (RK, CR))
            slf, cbf = (v.rearrange("p t n -> p (t n)") for v in (SL, CB))
            t = dve.do(lambda e: e.scalar_tensor_tensor(rkf, slf, -1000.0, P(0)[:, 0:64], ALU.mult, ALU.add), t)
            t = dve.do(lambda e: e.tensor_scalar(rkf, rkf, 1000.0, None, ALU.add), t)
            t_rk = t

            def overflow():
                t = dve.do(lambda e: e.tensor_scalar(crf, rkf, float(SLOTS), None, ALU.is_ge), t_rk)
                t = dve.do(lambda e: e.tensor_tensor(crf, crf, cbf, ALU.mult), t)
                t = dve.do(lambda e: e.tensor_reduce(sc[:, 6, 0:1], P(0)[:, 64:96], AX, ALU.max), t)
                return dve.do(lambda e: e.tensor_scalar(FL[:, :], sc[:, 6, 0:1], float(SLOTS), None, ALU.is_gt), t)
            t_flag = moe_slots(CB, RK, t_rk, t_xs, overflow)
            slots[0], ring_next[0], hi_n[0] = 4, 0, 0
            ahead.extend(w8s(w_in2, i) for i in range(2))
            bar()
            for tt in range(2):
                for j in range(2):
                    h = H[:, tt, j * 512:(j + 1) * 512]
                    dve.do(lambda e, h=h, b=2 * tt + j: e.tensor_tensor(h, P(b), h, ALU.add))
            bar()
            wk.reset()
            w2.reset()
            wk(1200)
            moe_rest(CR, FL[0:1, 0:1], t_flag)
            last_norm(rw["fin1"], H)
            bar()

        def moe_slots(CB, RK, t_rk, t_xs, overflow):
            XG = w2(4096, "p (b c n) -> p b c n", b=2, c=8)
            PG = rounded("PG", "Wk", wk.at, 1024)[:, :].rearrange("p (b t n) -> p b t n", b=2, t=2)
            wk(1024)
            PC = wk(1024, "p (b t n) -> p b t n", b=2, t=2)
            HP = wk(1024, "p (b n) -> p b n", b=2)
            SG = w2(512, "p (b n) -> p b n", b=2)
            HM = w2(512, "p (b n) -> p b n", b=2)
            YS = w2(1024, "p (b n) -> p b n", b=2)
            slot = bc(co["iota"][:, 0:64].unsqueeze(1), [128, 4, 64])
            pg_tok, pc_tok, xg_tok = {}, {}, {}
            pg_free, pc_free, xg_free = [None, None], [None, None], [None, None]
            y_first = [None]
            g_free, hp_free, ys_free, step_free = [None, None], [None, None], [None, None], [[], []]

            def prep(g):
                b = g % 2
                for tt in range(2):
                    pg = PG[:, b, tt, :].rearrange("p (e s) -> p e s", e=4)
                    pc = PC[:, b, tt, :].rearrange("p (e s) -> p e s", e=4)
                    rk = bc(RK[:, tt, 4 * g:4 * g + 4].unsqueeze(2), [128, 4, 64])
                    cb = bc(CB[:, tt, 4 * g:4 * g + 4].unsqueeze(2), [128, 4, 64])
                    t = dve.do(lambda e, pg=pg, rk=rk: e.tensor_tensor(pg, slot, rk, ALU.is_equal), t_rk, pg_free[b])
                    t2 = dve.do(lambda e, pg=pg, pc=pc, cb=cb: e.tensor_tensor(pc, pg.bitcast(F32), cb, ALU.mult), t, pc_free[b])
                pg_tok[g], pc_tok[g] = t, t2
                xg_tok[g] = []

            def gather(g, s):
                b = g % 2
                o = P(7 if g else 4 + s).rearrange("p (c n) -> p c n", c=2)
                for k in range(2):
                    for n in range(4):
                        tt = n // 2
                        t = pe.do(mm(o[:, k, :], halves[0][n % 2][:, tt, 2 * s + k::8], PG[:, b, tt, :], n == 0, n == 3),
                                  pg_tok[g], t_xs, *(step_free[0] if g else []))
                pg_free[b] = t
                ks = []
                for k in range(2):
                    c = 2 * s + k
                    ks.append(dve.do(lambda e, k=k, c=c: e.tensor_scalar(XG[:, b, c, :], o[:, k, :], sm["g_ffn"][:, c:c + 1],
                                                                         None, ALU.mult), t, xg_free[b]))
                step_free[0] = ks
                xg_tok[g] += ks
                if g == 0:
                    g_free[0] = g_free[1] = y_first[0] = ks[1]

            ys_tok, pct = {}, {}

            def scatter(ex):
                b = ex % 2
                for tt in range(2):
                    for j in range(2):
                        r = slice(64 * j, 64 * j + 64)
                        t = pe.do(mm(P(2 * tt + j), HP[r, b, 256 + tt * 128:384 + tt * 128], YS[r, b, :], ex == 0, ex == 31),
                                  ys_tok[ex])
                ys_free[b] = hp_free[b] = t

            prep(0)
            for s in range(4):
                gather(0, s)
            y_free = y_first[0]
            t_flag = overflow()
            pe.wait(t_flag)
            for ex in range(32):
                g, k4, b = ex // 4, ex % 4, ex % 2
                if k4 == 0 and g < 7:
                    prep(g + 1)
                wg, tg, s1 = unit(w_gate[ex].rearrange("(p c) n -> p (c n)", c=8), "p (c n) -> p c n", c=8)
                wu, tu, s2 = unit(w_up[ex].rearrange("(p c) n -> p (c n)", c=8), "p (c n) -> p c n", c=8)
                wd, td, s3 = unit(w_down[ex].rearrange("(h p c) n -> p h (c n)", h=2, c=2), "p (h c n) -> p h c n", h=2, c=2)
                G = P(4 + b)
                x = XG[:, g % 2, :, k4 * 64:k4 * 64 + 64]
                for w, tw, z in ((wg, tg, 0), (wu, tu, 256)):
                    for c in range(8):
                        for j in range(2):
                            t = pe.do(mm(G[64 * j:64 * j + 64, z:z + 256], x[:, c, :], w[:, c, 256 * j:256 * j + 256], c == 0, c == 7),
                                      tw, g_free[b], *xg_tok[g])
                    done(s1 if z == 0 else s2, t)
                if k4 == 3:
                    xg_free[g % 2] = t
                s = act.do(lambda e, b=b, G=G: e.activation(SG[:, b, :], G[:, 0:256], ACT.Silu), t)
                h = dve.do(lambda e, b=b, G=G: e.tensor_tensor(HM[:, b, :], SG[:, b, :], G[:, 256:512], ALU.mult), s)
                if ex:
                    scatter(ex - 1)
                for c in range(2):
                    t = pe.do(tr(G[:, c * 128:c * 128 + 128], HM[:, b, c::2]), h)
                for tt in range(2):
                    pc = PC[:, g % 2, tt, k4 * 64:k4 * 64 + 64]
                    for j in range(2):
                        t = pe.do(mm(G[64 * j:64 * j + 64, 256 + tt * 128:384 + tt * 128], pc, ident, True, True), pc_tok[g])
                if k4 == 3:
                    pc_free[g % 2] = t
                k = act.do(lambda e, b=b, G=G: e.activation(HP[:, b, :], G, ACT.Copy), t, hp_free[b])
                g_free[b] = k
                if g < 7:
                    gather(g + 1, k4)
                ht = HP[:, b, 0:256].rearrange("p (c h s) -> p h c s", c=2, h=2)
                for c in range(4):
                    for j in range(2):
                        t = pe.do(mm(P(6)[64 * j:64 * j + 64, :], ht[:, c // 2, c % 2, :], wd[:, c // 2, c % 2, 512 * j:512 * j + 512],
                                     c == 0, c == 3), k, td, y_free)
                done(s3, t)
                ys_tok[ex] = y_free = dve.do(lambda e, b=b: e.tensor_copy(YS[:, b, :], P(6)), t, ys_free[b])
            scatter(31)
            return t_flag

        def moe_rest(CR, flag, t_flag):
            for q in (pe, act, dve, sp):
                q.wait(t_flag)
            fp, fa, fd, fs = (q.branch(sem(f"f_{n}"), flag) for n, q in (("pe", pe), ("act", act), ("dve", dve), ("sp", sp)))
            fs.wait(*(q.last() for q in qs), *(t for f in ring_free for t in f))
            SG = w2(1024, "p (t n) -> p t n", t=2)
            HM = w2(1024, "p (t n) -> p t n", t=2)
            HT = w2(1024, "p (t c n) -> p t c n", t=2, c=4)
            places = [AR[:, 2 * 4096:3 * 4096], AR[:, 3 * 4096:4 * 4096], Wk[:, 4800:8896]]
            sems = [sem(f"f_ld{i}") for i in range(3)]
            slot_free = [None] * 3
            free = {b: None for b in range(4, 8)}

            def weights(n, src, c):
                s = n % 3
                dst = places[s]
                fs.raw(lambda e: e.dma_start(dst, src.rearrange("(p c) n -> p (c n)", c=c)).then_inc(sems[s], 16), slot_free[s])
                return dst.rearrange("p (c n) -> p c n", c=c), (sems[s], 16 * (n // 3 + 1)), s

            for ex in range(32):
                g, tg, sg_ = weights(3 * ex, w_gate[ex], 8)
                u, tu, su_ = weights(3 * ex + 1, w_up[ex], 8)
                d, td, sd_ = weights(3 * ex + 2, w_down[ex], 4)
                hm = []
                for tt in range(2):
                    x8 = lambda c: NT[:, c, tt * 128:tt * 128 + 128]
                    a = proj(P(4 + 2 * tt), x8, lambda c: g[:, c, :], 8, tg, free[4 + 2 * tt], q=fp)
                    b = proj(P(5 + 2 * tt), x8, lambda c: u[:, c, :], 8, tu, free[5 + 2 * tt], q=fp)
                    s = fa.do(lambda e, tt=tt: e.activation(SG[:, tt, :], P(4 + 2 * tt), ACT.Silu), a)
                    h = fd.do(lambda e, tt=tt, ex=ex: e.scalar_tensor_tensor(
                        HM[:, tt, :], SG[:, tt, :], CR[:, tt, ex:ex + 1], P(5 + 2 * tt), ALU.mult, ALU.mult), s, b)
                    hm.append(h)
                    free[5 + 2 * tt] = h
                slot_free[sg_], slot_free[su_] = a, b
                for tt in range(2):
                    for c in range(4):
                        t = fp.do(tr(P(4 + 2 * tt)[:, c * 128:(c + 1) * 128], HM[:, tt, c::4]), hm[tt])
                    k = fa.do(lambda e, tt=tt: e.activation(HT[:, tt, :, :], P(4 + 2 * tt).rearrange("p (c n) -> p c n", c=4),
                                                            ACT.Copy), t)
                    free[4 + 2 * tt] = k
                    for j in range(2):
                        for c in range(4):
                            t = fp.do(mm(P(2 * tt + j), HT[:, tt, c, :], d[:, c, j * 512:(j + 1) * 512],
                                         ex == 0 and c == 0, ex == 31 and c == 3), k, td)
                slot_free[sd_] = t
            for tt in range(2):
                for j in range(2):
                    h = H[:, tt, j * 512:(j + 1) * 512]
                    fd.do(lambda e, h=h, b=2 * tt + j: e.tensor_tensor(h, P(b), h, ALU.add), t)
            for q in (fp, fa, fd, fs):
                q.wait(fp.last(), fa.last(), fd.last())

        def last_norm(gain, dst):
            r = rms(H)
            for tt in range(2):
                dve.do(lambda e, tt=tt: e.scalar_tensor_tensor(dst[:, tt, :], H[:, tt, :], ST[:, tt:tt + 1], gain,
                                                               ALU.mult, ALU.mult), r)

        def mixers2():
            wk.reset()
            w2.reset()
            wk.hi = 9200
            norm_split(H, X2, sm["g_nmix"])
            qT = wk(1024, "p (m t) -> p m t", m=4)
            kT = wk(1024, "p (m t) -> p m t", m=4)
            qB = wk(1024, "p (m t) -> p m t", m=4)
            kV = wk(1024, "p (m t) -> p m t", m=4)
            VA = wk(1024, "p (t n) -> p t n", t=2)
            OAT, OBT = qT, qB
            S = wk(4 * 384, "p (i n) -> p i n", i=4)
            PT = wk(4 * 384, "p (i n) -> p i n", i=4)
            VB = wk(560, "p (t n) -> p t n", t=2)
            lm = wk(8)
            mx = wk(64, "p (i t) -> p i t", t=2)
            den = wk(64, "p (i t) -> p i t", t=2)
            OA = w2(1024, "p (t n) -> p t n", t=2)
            GT = w2(48, "p (t n) -> p t n", t=2)
            KP = w2(1024, "p (n l) -> p n l", l=32)
            HE = w2(512, "p (b n) -> p b n", b=2)
            HID = w2(64, "p (b h n) -> p b h n", b=2, h=2)
            CK2 = w2(256, "p (b h n) -> p b h n", b=2, h=2)
            KCT = w2(8)
            VC = w2(128, p=8)
            BDV = w2(512, p=64)
            SC = w2(128, "p (t h c) -> p t h c", t=2, h=8)
            CS = w2(64, "p (k t h) -> p k t h", k=4, t=2)
            PCT = w2(256, p=64)
            t_c2 = load(act, CK2, ck2.rearrange("p (b h n) -> p b h n", b=2, h=2))
            lam = sm["lam"]
            for i in range(2):
                a = lam[:, 128 * i:128 * i + 64]
                b = lam[:, 128 * i + 64:128 * i + 128]
                t = dve.do(lambda e, i=i, a=a, b=b: e.tensor_tensor_reduce(S[:, i, 0:64], a, b, 1.0, 0.0, ALU.mult, ALU.add,
                                                                           lm[:, i:i + 1]))
            t = act.do(lambda e: e.activation(lm[:, 2:4], lm[:, 0:2], ACT.Exp), t)
            t_lam = dve.do(lambda e: e.tensor_scalar(lm[:, 4:5], lm[:, 3:4], lm[:, 2:3], -0.2, ALU.subtract, ALU.add), t)

            run([(w_in2[0], lambda u: proj_turned(u, X2, qT, [0, 1], 0.125)),
                 (w_in2[1], lambda u: proj_turned(u, X2, kT, [2, 3])),
                 (w_in2[2], lambda u: proj_tokens(u, X2, [4, 5], copy_out(VA))),
                 (w_in2[3], lambda u: proj_turned(u, X2, qB, [0, 1], 0.125)),
                 (w_in2[4], lambda u: proj_turned(u, X2, kV, [2, 3])),
                 (w_in2[5], lambda u: proj_tokens(u, X2, [6, 7], copy_out(VB), ncol=280))], *ahead)
            bar()
            act.do(lambda e: e.activation(GT, VB[:, :, 256:280], ACT.Sigmoid))

            s_free = [[] for _ in range(4)]
            pt_free = [[] for _ in range(4)]
            soft, turned = {}, {}
            tiles = ((0, slice(0, 128)), (1, slice(128, 384)))

            def scores(n):
                if n < 8:
                    r, lq, rk, m, mk = slice(64 * (n % 2), 64 * (n % 2) + 64), qT, kT, n // 2, n // 2
                    slope = float(2.0 ** (-2.0 * (n // 2 + 1)))
                else:
                    j, h = (n - 8) // 8, n % 8
                    r, lq, rk, m, mk = slice(64 * (h // 4), 64 * (h // 4) + 64), qB, kV, h % 4, 2 + j
                    slope = float(2.0 ** -(h + 1.0))
                b = n % 2
                free = bank_free[b]
                pe.raw(mm(P(b)[:, 0:128], lq[r, m, 0:128], rk[r, mk, 0:128], True, True), *free)
                t = pe.do(mm(P(b)[:, 128:384], lq[r, m, 128:256], rk[r, mk, 0:256], True, True))
                yield
                s = S[:, n % 4, :]
                t = dve.do(lambda e: e.scalar_tensor_tensor(s, co["dist"], slope, P(b)[:, 0:384], ALU.mult, ALU.add),
                           t, *s_free[n % 4])
                bank_free[b] = [t]
                ms = [dve.do(lambda e, tt=tt, cs=cs: e.tensor_reduce(mx[:, n, tt:tt + 1], s[:, cs], AX, ALU.max, negate=True), t)
                      for tt, cs in tiles]
                for (tt, cs), m in zip(tiles, ms):
                    soft[n] = act.do(lambda e, tt=tt, cs=cs: e.activation(
                        s[:, cs], s[:, cs], ACT.Exp, bias=mx[:, n, tt:tt + 1], accum_out=den[:, n, tt:tt + 1]), m)

            def weights(n):
                if n < 8:
                    t = dve.do(lambda e: e.reciprocal(den[:, n:n + 2, :], den[:, n:n + 2, :]), soft[n], soft[n + 1])
                    t = dve.do(lambda e: e.tensor_scalar(den[:, n + 1, :], den[:, n + 1, :], lm[:, 4:5], None, ALU.mult), t, t_lam)
                    bs = [dve.do(lambda e, tt=tt, cs=cs: e.tensor_scalar(
                        S[:, (n + 1) % 4, cs], S[:, (n + 1) % 4, cs], den[:, n + 1, tt:tt + 1], None, ALU.mult), t) for tt, cs in tiles]
                    for (tt, cs), b in zip(tiles, bs):
                        a = dve.do(lambda e, tt=tt, cs=cs: e.scalar_tensor_tensor(
                            S[:, n % 4, cs], S[:, n % 4, cs], den[:, n, tt:tt + 1], S[:, (n + 1) % 4, cs], ALU.mult, ALU.add), b)
                    s_free[(n + 1) % 4] = [a]
                else:
                    j, h = (n - 8) // 8, n % 8
                    t = dve.do(lambda e: e.reciprocal(den[:, n, :], den[:, n, :]), soft[n])
                    t = dve.do(lambda e: e.tensor_tensor(den[:, n, :], den[:, n, :], GT[:, :, h * 3 + 1 + j], ALU.mult), t, t_gt)
                    for tt, cs in tiles:
                        a = dve.do(lambda e, tt=tt, cs=cs: e.tensor_scalar(S[:, n % 4, cs], S[:, n % 4, cs], den[:, n, tt:tt + 1],
                                                                           None, ALU.mult), t)
                yield
                b = 2 + (n // 2 if n < 8 else n) % 2
                for k in range(3):
                    t = pe.do(tr(P(b)[:, k * 128:(k + 1) * 128], S[:, n % 4, k * 128:(k + 1) * 128]), a, *bank_free[b])
                s_free[n % 4] = [t]
                turned[n] = act.do(lambda e: e.activation(PT[:, n % 4, :], P(b)[:, 0:384], ACT.Copy), t, *pt_free[n % 4])
                bank_free[b] = [turned[n]]

            def values(n):
                p = PT[:, n % 4, :]
                if n < 8:
                    cs = slice(n // 2 * 128, n // 2 * 128 + 128)
                    pe.raw(mm(P(4)[:, cs], p[:, 0:128], VA[:, 0, cs], True, True), turned[n])
                    pe.raw(mm(P(5)[:, cs], p[:, 128:256], VA[:, 0, cs], True, False))
                    t = pe.do(mm(P(5)[:, cs], p[:, 256:384], VA[:, 1, cs], False, True))
                else:
                    j, h = (n - 8) // 8, n % 8
                    g = h // 4
                    o = P(6 + g)[(h % 2) * 64:(h % 2) * 64 + 64, (h // 2 % 2) * 256:(h // 2 % 2) * 256 + 256]
                    vs = slice(128 * j + 64 * g, 128 * j + 64 * g + 64)
                    pe.raw(mm(o, VB[:, 0, vs], p[:, 0:256], False, False), turned[n])
                    t = pe.do(mm(o[:, 128:256], VB[:, 1, vs], p[:, 256:384], False, n == 23))
                pt_free[n % 4] = [t]

            t_gt = act.last()
            ua = unit(ck1[0], "p (l n) -> p l n", l=16)
            ub = unit(ck1[1], "p (l n) -> p l n", l=16)

            def compressed():
                tz = pool.do(lambda e: e.memset(KP[:, 16:32, :], 0.0))
                tk = dve.do(lambda e: e.tensor_tensor(KP[:, 0:16, :], kV[:, 0:2, :].rearrange("p g (c l) -> p (g c) l", l=32),
                                                      bc(sm["pos"].unsqueeze(1), [128, 16, 32]), ALU.add))
                yield
                for l in range(32):
                    w, q = (ua, ub)[l // 16], slice(32 * (l % 4), 32 * (l % 4) + 32)
                    for b in range(2):
                        r = slice(64 * b, 64 * b + 64)
                        t = pe.do(mm(P(6 + b)[q, 0:256], KP[r, :, l], w[0][r, l % 16, :], l < 4, l >= 28), w[1], tk, tz)
                    if l % 16 == 15:
                        yield
                done(ua[2], t)
                done(ub[2], t)
                t2 = act.do(lambda e: e.activation(HE[:, 0, :], P(6)[:, 0:256], ACT.Copy), t)
                t3 = dve.do(lambda e: e.tensor_copy(HE[:, 1, :], P(7)[:, 0:256]), t)
                yield
                for b in range(2):
                    for ht in range(2):
                        t = pe.do(mm(P(6)[:, b * 32 + ht * 16:b * 32 + ht * 16 + 16], HE[:, b, ht * 128:ht * 128 + 128], co["sel"],
                                     True, True), t2, t3)
                t2 = act.do(lambda e: e.activation(HID, P(6)[:, 0:64].rearrange("p (b h n) -> p b h n", b=2, h=2), ACT.Gelu), t)
                yield
                for g in range(2):
                    r = slice(64 * g, 64 * g + 64)
                    for ht in range(2):
                        pe.raw(mm(P(6)[r, 0:8], CK2[:, 0, ht, :], HID[:, 0, ht, g * 8:g * 8 + 8], ht == 0, ht == 1), t2, t_c2)
                    for ht in range(2):
                        t = pe.do(mm(P(7)[0:8, g * 64:g * 64 + 64], HID[:, 1, ht, g * 8:g * 8 + 8], CK2[:, 1, ht, :],
                                     ht == 0, ht == 1))
                yield
                t1 = act.do(lambda e: e.activation(KCT, P(6)[:, 0:8], ACT.Copy), t)
                t2 = act.do(lambda e: e.activation(VC, P(7)[0:8, 0:128], ACT.Copy), t)
                yield
                vcb = bc(VC.rearrange("p (g d) -> p g d", g=2).unsqueeze(2), [8, 2, 4, 64])
                t = pe.do(mm(P(6)[0:64, :].rearrange("p (g r d) -> p g r d", g=2, r=4), co["esel"][0:8, :], vcb, True, True), t1, t2)
                yield
                t_bd = dve.do(lambda e: e.tensor_tensor(BDV, P(6)[0:64, :], co["bd"][0:64, :], ALU.mult), t)
                yield
                for tt in range(2):
                    for h in range(8):
                        r = slice(64 * (h // 4), 64 * (h // 4) + 64)
                        t = pe.do(mm(P(6 + h // 4)[:, tt * 32 + h % 4 * 8:tt * 32 + h % 4 * 8 + 8],
                                     qB[r, h % 4, tt * 128:tt * 128 + 128], KCT[r, :], True, True), t1, t_bd)
                yield
                scf = SC.rearrange("p t h c -> p (t h) c")

                def chain(f, q=dve):
                    nonlocal t
                    t = q.do(f, t)
                for g in range(2):
                    chain(lambda e, g=g: e.tensor_tensor(
                        SC[:, :, 4 * g:4 * g + 4, :].rearrange("p t h c -> p t (h c)"),
                        P(6 + g)[:, 0:64].rearrange("p (t a) -> p t a", t=2),
                        co["cmpb"].rearrange("p (t a) -> p t a", t=2)[:, :, 32 * g:32 * g + 32], ALU.add))
                csf = [CS[:, k, :, :].rearrange("p t h -> p (t h)") for k in range(4)]
                chain(lambda e: e.tensor_reduce(csf[0], scf, AX, ALU.max))
                chain(lambda e: e.tensor_tensor(scf, scf, bc(csf[0].unsqueeze(2), [128, 16, 8]), ALU.subtract))
                yield
                chain(lambda e: e.activation(scf, scf, ACT.Exp), act)
                yield
                chain(lambda e: e.tensor_reduce(csf[1], scf, AX, ALU.add))
                chain(lambda e: e.reciprocal(csf[2], csf[1]))
                g3 = GT.rearrange("p t (h j) -> p (t h) j", j=3)
                dve.wait(t_gt)
                chain(lambda e: e.tensor_tensor(csf[3], csf[2], g3[:, :, 0], ALU.mult))
                yield
                for tt in range(2):
                    chain(lambda e, tt=tt: e.tensor_tensor(SC[:, tt, :, :], SC[:, tt, :, :],
                                                           bc(co["cmpv"][:, tt * 8:tt * 8 + 8].unsqueeze(1), [128, 8, 8]), ALU.mult))
                chain(lambda e: e.tensor_tensor(scf, scf, bc(csf[3].unsqueeze(2), [128, 16, 8]), ALU.mult))
                yield
                for tt in range(2):
                    t3 = pe.do(tr(P(6)[0:64, tt * 128:tt * 128 + 128], SC[:, tt, :, :].rearrange("p h c -> p (h c)")), t)
                yield
                t3 = act.do(lambda e: e.activation(PCT, P(6)[0:64, 0:256], ACT.Copy), t3)
                yield
                for m in range(4):
                    pe.do(mm(P(6 + m // 2)[:, (m % 2) * 256:(m % 2) * 256 + 256], BDV[:, m * 128:m * 128 + 128], PCT,
                             m % 2 == 0, False), t3, t_bd)

            def differential():
                t, ts = pe.last(), []
                for tt in range(2):
                    for h in range(4):
                        ts.append(square_sum(P(4 + tt)[:, h * 128:h * 128 + 128], OA[:, tt, h * 128:h * 128 + 128],
                                             ST[:, 16 + 4 * tt + h:17 + 4 * tt + h], t))
                    yield
                r = rstd(ST[:, 16:24], 8, 128, *ts)
                yield
                for tt in range(2):
                    v = OA[:, tt, :].rearrange("p (h d) -> p h d", h=4)
                    a = dve.do(lambda e, tt=tt, v=v: e.tensor_tensor(
                        v, P(4 + tt).rearrange("p (h d) -> p h d", h=4),
                        bc(ST[:, 16 + 4 * tt:20 + 4 * tt].unsqueeze(2), [128, 4, 128]), ALU.mult), r)
                yield
                for c in range(4):
                    for tt in range(2):
                        o = P(4 + c // 2)[:, (c % 2) * 256 + tt * 128:(c % 2) * 256 + tt * 128 + 128]
                        t = pe.do(tr(o, OA[:, tt, c * 128:c * 128 + 128]), a)
                yield
                for c in range(4):
                    dve.do(lambda e, c=c: e.tensor_scalar(OAT[:, c, :], P(4 + c // 2)[:, (c % 2) * 256:(c % 2) * 256 + 256],
                                                          sm["g_sub"], 0.8, ALU.mult, ALU.mult), t)

            def ready(k):
                return (k - 1 if k % 2 else None) if 0 <= k < 8 else k if 8 <= k < 24 else None

            pieces = compressed()
            for n in range(27):
                if n == 26:
                    u_gate = split_unit(w_in2[6])
                if n == 11:
                    for _ in pieces:
                        pass
                    pieces = differential()
                a = scores(n) if n < 24 else iter(())
                b = weights(ready(n - 2)) if ready(n - 2) is not None else iter(())
                for part in (a, b, a, b):
                    next(part, None)
                next(pieces, None)
                if ready(n - 3) is not None:
                    values(ready(n - 3))
                if n < 11:
                    next(pieces, None)
            t = pe.last()
            for m in range(4):
                act.do(lambda e, m=m: e.activation(OBT[:, m, :], P(6 + m // 2)[:, (m % 2) * 256:(m % 2) * 256 + 256], ACT.Copy), t)
            t_o = (act.last(), dve.last())
            SGA = w2(2048, "p (t n) -> p t n", t=2)
            SGB = w2(2048, "p (t n) -> p t n", t=2)
            def gate(j):
                dst = (SGA, SGB)[j // 2]

                def evac(tt, o, t):
                    return act.do(lambda e: e.activation(dst[:, tt, (j % 2) * 512:(j % 2) * 512 + 512], o, ACT.Sigmoid), t)
                return w_in2[6 + j], lambda u: proj_tokens(u, X2, [2 * (j % 2), 2 * (j % 2) + 1], evac)
            run([gate(j) for j in range(4)], u_gate)
            pe.wait(*t_o)
            ua = unit(w_a.rearrange("(c p) n -> p c n", c=4), "p (c n) -> p c n", c=4)
            ub = unit(w_b.rearrange("(c p) n -> p c n", c=4), "p (c n) -> p c n", c=4)
            uo = [w8s(w_out2, j) for j in range(2)]
            bf = [[], []]
            for tt in range(2):
                for j in range(2):
                    cs = slice(j * 512, j * 512 + 512)
                    a = proj(P(4 + j), lambda c: OAT[:, c, tt * 128:tt * 128 + 128], lambda c: ua[0][:, c, cs], 4, ua[1], *bf[j])
                    b = proj(P(6 + j), lambda c: OBT[:, c, tt * 128:tt * 128 + 128], lambda c: ub[0][:, c, cs], 4, ub[1], *bf[j])
                    t1 = dve.do(lambda e, tt=tt, cs=cs, j=j: e.tensor_tensor(SGA[:, tt, cs], SGA[:, tt, cs], P(4 + j), ALU.mult),
                                a, act.last())
                    t2 = dve.do(lambda e, tt=tt, cs=cs, j=j: e.tensor_tensor(SGB[:, tt, cs], SGB[:, tt, cs], P(6 + j), ALU.mult), b)
                    bf[j] = [t1, t2]
                    t = dve.do(lambda e, tt=tt, cs=cs: e.tensor_tensor(XS[:, tt, cs], SGA[:, tt, cs], SGB[:, tt, cs], ALU.add), t1, t2)
            done(ua[2], a)
            done(ub[2], b)
            bar()
            cross_memory(uo)

        cross_in, ahead_q = [], []

        def cross_memory(uo):
            wk.reset()
            w2.reset()
            w2(4096)
            MM = w2(2048, "p (t d) -> p t d", t=2)
            MX2 = tuple(rounded(n, "AR", at, 2048)[:, :].rearrange("p (c t) -> p c t", c=8)
                        for n, at in (("MH", 6 * 4096), ("ML", 6 * 4096 + 2048)))
            junk = w2(2048, "p (t d) -> p t d", t=2)
            qT = wk(1024, "p (m t) -> p m t", m=4)
            kT = wk(1024, "p (m t) -> p m t", m=4)
            V = wk(1024, "p (t n) -> p t n", t=2)
            cross_in.extend((qT, kT, V))
            t_mm = load(act, MM, mem.rearrange("(t p) d -> p t d", p=128))
            turn_split(XS, X2, None)
            a = act.do(lambda e: e.activation(junk[:, 0, :], MM[:, 0, :], ACT.Square, accum_out=ST[:, 24:25]), t_mm)
            b = dve.do(lambda e: e.tensor_tensor_reduce(junk[:, 1, :], MM[:, 1, :], MM[:, 1, :], 1.0, 0.0, ALU.mult, ALU.add,
                                                        ST[:, 25:26]), t_mm)
            r = rstd(ST[:, 24:26], 2, D, a, b)
            for tt in range(2):
                t = dve.do(lambda e, tt=tt: e.tensor_scalar(MM[:, tt, :], MM[:, tt, :], ST[:, 24 + tt:25 + tt], None, ALU.mult), r)

            def residual(j):
                def evac(tt, o, t):
                    h = H[:, tt, j * 512:(j + 1) * 512]
                    return dve.do(lambda e: e.tensor_tensor(h, o, h, ALU.add), t)
                proj_tokens(uo[j], X2, [4 + 2 * j, 5 + 2 * j], evac)

            residual(0)
            turn_split(MM, MX2, sm["g_mem"], t)
            uk = w8s(w_ckv, 0)
            residual(1)
            act.wait(dve.last())
            dve.wait(dve.last())
            r = rms(H)
            for tt in range(2):
                t = dve.do(lambda e, tt=tt: e.tensor_scalar(XS[:, tt, :], H[:, tt, :], ST[:, tt:tt + 1], None, ALU.mult), r)
            uv = w8s(w_ckv, 1)
            proj_turned(uk, MX2, kT, [4, 5])
            uq = w8s(w_cq, 0)
            turn_split(XS, X2, sm["g_cross"], t)
            proj_tokens(uv, MX2, [6, 7], copy_out(V))
            proj_turned(uq, X2, qT, [4, 5])
            bar()

        def cross():
            qT, kT, V = cross_in
            w2.reset()
            OT = wk(1024, "p (m t) -> p m t", m=4)
            mx = wk(8)
            den = wk(8)
            S = w2(2048, "p (t h n) -> p t h n", t=2, h=4)
            PT = w2(2048, "p (m h n) -> p m h n", m=2, h=4)
            sc = float(128 ** -0.5)
            for tt in range(2):
                for h in range(4):
                    t = pe.do(mm(P(2 * tt + h // 2)[:, (h % 2) * 256:(h % 2) * 256 + 256], qT[:, h, tt * 128:tt * 128 + 128],
                                 kT[:, h, :], True, True))
            t = dve.do(lambda e: e.tensor_reduce(mx, P(0, 4).rearrange("p (a n) -> p a n", n=256), AX, ALU.max), t)
            t = dve.do(lambda e: e.tensor_scalar(mx, mx, -sc, None, ALU.mult), t)
            for a in range(8):
                k = act.do(lambda e, a=a: e.activation(S[:, a // 4, a % 4, :], P(a // 2)[:, (a % 2) * 256:(a % 2) * 256 + 256],
                                                       ACT.Exp, bias=mx[:, a:a + 1], scale=sc, accum_out=den[:, a:a + 1]), t)
            t = dve.do(lambda e: e.reciprocal(den, den), k)
            for a in range(8):
                s = S[:, a // 4, a % 4, :]
                t1 = dve.do(lambda e, a=a, s=s: e.tensor_scalar(s, s, den[:, a:a + 1], None, ALU.mult), t)
            for m in range(2):
                for pair in range(2):
                    o = P(4 + 2 * m + pair).rearrange("p (h t) -> p h t", h=2)
                    for h in range(2):
                        for tt in range(2):
                            t = pe.do(tr(o[:, h, tt * 128:tt * 128 + 128], S[:, tt, 2 * pair + h, m * 128:m * 128 + 128]), t1)
                    k = act.do(lambda e, m=m, pair=pair, o=o: e.activation(PT[:, m, 2 * pair:2 * pair + 2, :], o, ACT.Copy), t)
            for h in range(4):
                o = P(h // 2)[:, (h % 2) * 256:(h % 2) * 256 + 256]
                pe.raw(mm(o, V[:, 0, h * 128:h * 128 + 128], PT[:, 0, h, :], True, False), k)
                t = pe.do(mm(o, V[:, 1, h * 128:h * 128 + 128], PT[:, 1, h, :], False, True))
                if h % 2:
                    act.do(lambda e, h=h: e.activation(OT[:, h - 1:h + 1, :], P(h // 2).rearrange("p (h t) -> p h t", h=2),
                                                       ACT.Copy), t)
            bar()
            u = unit(w_co.rearrange("(c p) n -> p c n", c=4), "p (c n) -> p c n", c=4)
            ahead_q.extend(split_unit(w_pq[i]) for i in range(2))
            for j in range(2):
                for tt in range(2):
                    cs = slice(j * 512, j * 512 + 512)
                    t = proj(P(2 + 2 * j + tt), lambda c: OT[:, c, tt * 128:tt * 128 + 128], lambda c: u[0][:, c, cs], 4, u[1])
                    dve.do(lambda e, j=j, tt=tt, cs=cs: e.tensor_tensor(H[:, tt, cs], P(2 + 2 * j + tt), H[:, tt, cs], ALU.add), t)
            done(u[2], t)
            bar()

        def peer():
            wk.reset()
            w2.reset()
            norm_split(H, X2, sm["g_peer"])
            b1 = Bump(Wk, 0, 8192)
            wk(8192)
            I1T, I2T, GTT = wk(256), wk(256), wk(256)
            SK = b1(2048, "p (a n) -> p a n", a=16)
            QP = b1(1024, "p (a t) -> p a t", a=4)
            TS = b1(512, "p (a k) -> p a k", a=32)
            TF = b1(512, "p (a k) -> p a k", a=32)
            TIi = b1(512, "p (a k) -> p a k", a=32).bitcast(U32)
            BS = b1(256, "p (a k) -> p a k", a=16)
            BJ = b1(256, "p (a k) -> p a k", a=16).bitcast(U32)
            BF = b1(512, "p (c a k) -> p c a k", c=2, a=16)
            DF = b1(256, "p (a k) -> p a k", a=16)
            BG = b1(256, "p (a k) -> p a k", a=16)
            II = b1(512, "p (c t n) -> p c t n", c=2, t=2)
            gs = b1(32, "p (k a) -> p k a", k=2)
            S = w2(4096, "p (a n) -> p a n", a=32)
            CA = w2(50 * 16, "p (a n) -> p a n", a=16)
            GA, GB, GC = (w2(1024, "p (t n j) -> p t n j", t=2, j=16) for _ in range(3))
            XH, XL = X2
            t_sk = load(act, SK, subk.rearrange("p (a n) -> p a n", a=16), dve.last(), pe.last(), pool.last())

            def top16(src, vals, idx, rows):
                for k in (0, 8):
                    for a in rows:
                        t = dve.do(lambda e, a=a, k=k: e.max(vals[:, a, k:k + 8], src[:, a, :]))
                    dve.wait(t)
                    for a in rows:
                        t = dve.do(lambda e, a=a, k=k: e.max_index(idx[:, a, k:k + 8], vals[:, a, k:k + 8], src[:, a, :]))
                    dve.wait(t)
                    if k == 0:
                        for a in rows:
                            t = dve.do(lambda e, a=a: e.match_replace(src[:, a, :], vals[:, a, 0:8], src[:, a, :], -3e38))
                        dve.wait(t)

            def chain(f, q=dve):
                nonlocal t
                t = q.do(f, t)

            qp_free = [[] for _ in range(4)]
            by_tt = lambda v: v.rearrange("p (t h) k -> p t h k", t=2)
            tsv, tfv = (v.rearrange("p (t h c) k -> p t h c k", t=2, c=2) for v in (TS, TF))
            a_tok, b_tok = {}, {}

            def rows_of(v, tt, ui):
                return v[:, tt * 8 + 2 * ui:tt * 8 + 2 * ui + 2, :]

            def four(v):
                return v.rearrange("p (h k) j -> p h k j", h=2)

            def place_a(ui, q):
                hs = slice(2 * ui, 2 * ui + 2)
                t = dve.do(lambda e: e.tensor_copy(by_tt(BF[:, 0])[:, :, hs, :], by_tt(BJ)[:, :, hs, :]), dve.last())
                for tt in range(2):
                    p = rows_of(BF[:, 0], tt, ui).rearrange("p h k -> p (h k)")
                    t1 = dve.do(lambda e, tt=tt, p=p: e.tensor_tensor(GA[:, tt], bc(p.unsqueeze(2), [128, 32, 16]),
                                                                   bc(co["pst"].unsqueeze(1), [128, 32, 16]), ALU.is_ge), t)
                for tt in range(2):
                    d = rows_of(DF, tt, ui)
                    t2 = q.do(lambda e, tt=tt, d=d: e.tensor_tensor(four(GB[:, tt]), four(GA[:, tt]),
                                                                   bc(d.unsqueeze(2), [128, 2, 16, 16]), ALU.mult), t1)
                for tt in range(2):
                    t2 = q.do(lambda e, tt=tt: e.tensor_tensor(GA[:, tt], GA[:, tt], bc(co["plen"].unsqueeze(1), [128, 32, 16]),
                                                               ALU.mult), t2)
                a_tok[ui] = t2

            def place_b(ui, q):
                ks, hs = slice(32 * ui, 32 * ui + 32), slice(2 * ui, 2 * ui + 2)
                pq, bq = (BF[:, c].rearrange("p (t a) k -> p t (a k)", t=2)[:, :, ks] for c in range(2))
                dve.do(lambda e: e.tensor_reduce(II[:, 0, :, ks], GB, AX, ALU.add), a_tok[ui])
                t = dve.do(lambda e: e.tensor_reduce(bq, GA, AX, ALU.add))
                t = dve.do(lambda e: e.tensor_tensor(bq, pq, bq, ALU.subtract), t)
                for tt in range(2):
                    t1 = dve.do(lambda e, tt=tt: e.tensor_tensor(GC[:, tt], bc(bq[:, tt].unsqueeze(2), [128, 32, 16]),
                                                               bc(co["iota"][:, 0:16].unsqueeze(1), [128, 32, 16]), ALU.is_equal), t)
                for tt in range(2):
                    t1 = q.do(lambda e, tt=tt: e.tensor_tensor(four(GC[:, tt]), four(GC[:, tt]),
                                                               bc(tfv[:, tt, hs, 1, :].unsqueeze(2), [128, 2, 16, 16]), ALU.mult), t1)
                b_tok[ui] = t1

            def place_c(ui):
                ks = slice(32 * ui, 32 * ui + 32)
                return dve.do(lambda e: e.tensor_reduce(II[:, 1, :, ks], GC, AX, ALU.add), b_tok[ui])

            def key_scores(hc, k):
                m, b = hc % 4, 4 + hc % 4
                for tt in range(2):
                    t2 = pe.do(mm(P(b)[:, tt * 128:tt * 128 + 128], QP[:, m, tt * 128:tt * 128 + 128], SK[:, hc, :], True, True),
                               k, t_sk, *bank_free[b])
                qp_free[m] = [t2]
                v = S.rearrange("p (t a) n -> p t a n", t=2)[:, :, hc, :]
                s_tok[hc] = act.do(lambda e: e.activation(v, P(b)[:, 0:256].rearrange("p (t n) -> p t n", t=2), ACT.Copy), t2)
                bank_free[b] = [s_tok[hc]]

            s_tok, q_tok = {}, {}
            wq = ahead_q
            for ui in range(4):
                if len(wq) < min(ui + 2, 4):
                    wq.append(split_unit(w_pq[ui + 1], pool))
                wh, wl, tw, _, _ = wq[ui]
                for m in range(4):
                    hc = ui * 4 + m
                    b = hc % 4
                    o = P(b)[:, 0:256]
                    ms = slice(m * 128, m * 128 + 128)
                    pe.wait(*bank_free[b])
                    for c in range(8):
                        pe.wait(tw[c // 2], x_tok[id(X2), c])
                        t = three(o, wh[:, c, ms], wl[:, c, ms], XH[:, c, :], XL[:, c, :], c == 0, c == 7, c == 7)
                    q_tok[hc] = act.do(lambda e, m=m, o=o: e.activation(QP[:, m, :], o, ACT.Copy), t, *qp_free[m])
                    bank_free[b] = [q_tok[hc]]
                    if m:
                        key_scores(hc - 1, q_tok[hc - 1])
                release(wq[ui], t)
                key_scores(hc, q_tok[hc])
                for half in range(2):
                    dve.wait(s_tok[4 * ui + 2 * half + 1])
                    top16(S, TS, TIi, [tt * 16 + 4 * ui + m for tt in range(2) for m in (2 * half, 2 * half + 1)])
                hs = slice(2 * ui, 2 * ui + 2)
                at = 0
                cav, dfv = by_tt(CA)[:, :, hs, :], by_tt(DF)[:, :, hs, :]
                for a0, a1 in ((0, 1), (1, 2), (2, 3), (3, 4), (4, 5), (5, 8), (8, 16)):
                    nb = 16 // (a0 + 1)
                    for tt in range(2):
                        v = cav[:, tt, :, at:at + (a1 - a0) * nb].rearrange("p h (a b) -> p h a b", b=nb)
                        shape = [128, 2, a1 - a0, nb]
                        t = dve.do(lambda e, v=v, tt=tt, hs=hs, a0=a0, a1=a1, nb=nb, shape=shape: e.tensor_tensor(
                            v, bc(tsv[:, tt, hs, 0, a0:a1].unsqueeze(3), shape),
                            bc(tsv[:, tt, hs, 1, 0:nb].unsqueeze(2), shape), ALU.add))
                    at += (a1 - a0) * nb
                for tt in range(2):
                    r = slice(tt * 16 + 4 * ui, tt * 16 + 4 * ui + 4)
                    t1 = dve.do(lambda e, r=r: e.tensor_copy(TF[:, r, :], TIi[:, r, :]))
                dve.do(lambda e, hs=hs, dfv=dfv: e.tensor_tensor(dfv[:, :, :, 1:16], tfv[:, :, hs, 0, 1:16], tfv[:, :, hs, 0, 0:15],
                                                                 ALU.subtract), t1)
                dve.do(lambda e, hs=hs, dfv=dfv: e.tensor_copy(dfv[:, :, :, 0:1], tfv[:, :, hs, 0, 0:1]), t1)
                dve.wait(t)
                if ui:
                    place_b(ui - 1, pool)
                top16(CA, BS, BJ, [tt * 8 + h for tt in range(2) for h in (2 * ui, 2 * ui + 1)])
                if ui:
                    place_c(ui - 1)
                place_a(ui, dve if ui == 3 else pool)
            place_b(3, dve)
            t = place_c(3)
            chain(lambda e: e.tensor_tensor(BG, BS, bc(BS[:, :, 0:1], [128, 16, 16]), ALU.subtract))
            chain(lambda e: e.activation(BG, BG, ACT.Exp), act)
            chain(lambda e: e.tensor_reduce(gs[:, 0, :], BG, AX, ALU.add))
            chain(lambda e: e.reciprocal(gs[:, 1, :], gs[:, 0, :]))
            chain(lambda e: e.tensor_tensor(BG, BG, bc(gs[:, 1, :].unsqueeze(2), [128, 16, 16]), ALU.mult))
            bg = BG.rearrange("p (t h) k -> p t (h k)", t=2)
            for n, (src, dst) in enumerate(((II[:, 0], I1T), (II[:, 1], I2T), (bg, GTT))):
                for tt in range(2):
                    t1 = pe.do(tr(P(n)[:, tt * 128:tt * 128 + 128], src[:, tt, :]), t)
                act.do(lambda e, n=n, dst=dst: e.activation(dst, P(n)[:, 0:256], ACT.Copy), t1)
            bar()

            UR = Wk[:, 0:3072].rearrange("p (b n) -> p b n", b=3)
            VR = Wk[:, 3072:6144].rearrange("p (b n) -> p b n", b=3)
            ULt, VLt = rounded("UL", "Wk", 0, 3072), rounded("VL", "Wk", 3072, 3072)
            UHt, VHt = rounded("UH", "Wk", 6144, 2048), rounded("VH", "CO", 0, 2048)
            WHt, WLt = rounded("WH", "RW", 0, 512), rounded("WL", "RW", 512, 512)
            UL, VL = (v[:, :].rearrange("p (b n) -> p b n", b=3) for v in (ULt, VLt))
            UH, VH = (v[:, :].rearrange("p (b n) -> p b n", b=2) for v in (UHt, VHt))
            WH, WL = (v[:, :].rearrange("p (b n) -> p b n", b=2) for v in (WHt, WLt))
            GE = Wk[:, 8192:8704].rearrange("p (b n) -> p b n", b=2)
            us, vs = [sem(f"us{i}") for i in range(3)], [sem(f"vs{i}") for i in range(3)]
            s1, s2 = {}, {}

            def fetch(i):
                s = i % 3
                sp.raw(lambda e: e.dma_start(UR[:, s], peer_u[i]).then_inc(us[s], 16), s1.get(i - 3))
                sp.raw(lambda e: e.dma_start(VR[:, s], peer_v[:, i, :]).then_inc(vs[s], 16), s2.get(i - 3))

            sp.wait(*(q.last() for q in qs))
            for i in range(3):
                fetch(i)

            C = AR[:, :].rearrange("p (t n) -> p t n", t=256)
            OA, OB = ([v.rearrange("p (k n) -> p k n", k=4) for v in vs_] for vs_ in (
                (Wk[:, 6144:6656], Wk[:, 6656:7168], RW[:, 512:1024]), (Wk[:, 7168:7680], Wk[:, 7680:8192], RW[:, 1024:1536])))
            io = co["iota"]
            NI, NG = RW[:, 0:256], RW[:, 256:512]
            act.do(lambda e: e.activation(NI, I1T, ACT.Copy, scale=-1.0))
            act.wait(act.do(lambda e: e.activation(NG, GTT, ACT.Copy, scale=-1.0)))
            oh_free, pf, full = [None] * 3, [None] * 4, []

            def to_c(behind):
                while len(full) > behind:
                    g, pb, t = full.pop(0)
                    pf[g % 4] = act.do(lambda e, g=g, pb=pb: e.activation(C[:, 4 * g:4 * g + 4, :], P(pb).rearrange("p (k n) -> p k n", k=4),
                                                              ACT.Copy), t)
            for g in range(64):
                b = g % 3
                made = [dve.do(lambda e, b=b, g=g: e.tensor_tensor(OB[b], bc(io.unsqueeze(1), [128, 4, 128]),
                                                                   bc(I2T[:, 4 * g:4 * g + 4].unsqueeze(2), [128, 4, 128]), ALU.is_equal),
                               oh_free[b])]
                for k in range(4):
                    tok = g * 4 + k
                    o, i1, gt = OA[b][:, k, :], I1T[:, tok:tok + 1], GTT[:, tok:tok + 1]
                    q = (dve, dve, pool, act if g % 4 else pool)[k]
                    if k == 3 and q is pool:
                        to_c(1)
                    if q is act:
                        t = act.do(lambda e, o=o, tok=tok: e.activation(o, io, ACT.Abs, bias=NI[:, tok:tok + 1]), oh_free[b])
                        to_c(1)
                        t = act.do(lambda e, o=o, tok=tok, gt=gt: e.activation(o, o, ACT.Relu, bias=gt, scale=NG[:, tok:tok + 1]), t)
                    else:
                        t = q.do(lambda e, o=o, i1=i1, gt=gt: e.tensor_scalar(o, io, i1, gt, ALU.is_equal, ALU.mult), oh_free[b])
                    made.append(t)
                pb = 4 + g % 4
                for k in range(4):
                    t = pe.do(mm(P(pb)[:, k * 128:k * 128 + 128], OA[b][:, k, :], OB[b][:, k, :], True, True), *made, pf[g % 4])
                oh_free[b] = t
                full.append((g, pb, t))
            to_c(0)
            t_c = act.last()
            act.wait(pe.last(), dve.last(), pool.last())
            dve.wait(t_c, pe.last(), pool.last())

            def split(raw, high, low, arrived, high_free):
                a = act.do(lambda e: e.activation(high, raw, ACT.Copy), arrived, high_free)
                return dve.do(lambda e: e.tensor_tensor(low, raw, high.bitcast(F32), ALU.subtract), a, arrived)

            u_tok, v_tok, w_tok, sf = {}, {}, {}, {}

            def split_u(i):
                u_tok[i] = split(UR[:, i % 3], UH[:, i % 2], UL[:, i % 3], (us[i % 3], 16 * (i // 3 + 1)), s1.get(i - 2))

            def stage1(i):
                o = P(4 + i % 4)[:, 0:256]
                pe.wait(u_tok[i], sf.get(i - 4), *pf)
                for c in range(8):
                    cs = slice(c * 128, c * 128 + 128)
                    s1[i] = three(o, UH[:, i % 2, cs], UL[:, i % 3, cs], XH[:, c, :], XL[:, c, :], c == 0, c == 7, c == 7)
                v_tok[i] = split(VR[:, i % 3], VH[:, i % 2], VL[:, i % 3], (vs[i % 3], 16 * (i // 3 + 1)), s2.get(i - 2))
                b = i % 2
                g = GE[:, b, :]
                sf[i] = act.do(lambda e: e.activation(g, o, ACT.Gelu), s1[i], w_tok.get(i - 2))
                t = dve.do(lambda e: e.tensor_tensor(g, g, C[:, :, i], ALU.mult), sf[i])
                t = act.do(lambda e: e.activation(WH[:, b, :], g, ACT.Copy), t, s2.get(i - 2))
                w_tok[i] = dve.do(lambda e: e.tensor_tensor(WL[:, b, :], g, WH[:, b, :].bitcast(F32), ALU.subtract), t)

            def stage2(i):
                b = i % 2
                pe.wait(w_tok[i], v_tok[i])
                for tt in range(2):
                    ts_ = slice(tt * 128, tt * 128 + 128)
                    for j in range(2):
                        js = slice(j * 512, j * 512 + 512)
                        s2[i] = three(P(2 * tt + j), WH[:, b, ts_], WL[:, b, ts_], VH[:, b, js], VL[:, i % 3, js], i == 0, i == 127,
                                      tt == 1 and j == 1)
                if i + 3 < 128:
                    fetch(i + 3)

            split_u(0)
            for i in range(128):
                if i < 127:
                    split_u(i + 1)
                stage1(i)
                if i:
                    stage2(i - 1)
            stage2(127)
            t_f = load(act, UR[:, 0], fin2, s1[127], s2[127])
            bar()
            for tt in range(2):
                for j in range(2):
                    h = H[:, tt, j * 512:(j + 1) * 512]
                    dve.do(lambda e, h=h, b=2 * tt + j: e.tensor_tensor(h, P(b), h, ALU.add))
            bar()
            dve.wait(t_f)
            last_norm(UR[:, 0], XS)

        for phase in (mixers, experts, mixers2, cross, peer):
            phase()
        finish()
        emit()


def constants():
    import numpy as np
    p = np.arange(128)
    a = p[:, None]
    b = p[None, :]
    d = {}
    d["ident"] = (a == b)
    d["tri"] = (a <= b)
    d["neg"] = np.where(a < b, 0.0, -1e30)
    d["m01"] = (a < b)
    d["negu"] = -1.0 * (a >= b)
    d["neg1"] = -np.ones((128, 128))
    d["one"] = np.ones((128, 128))
    k2 = np.arange(256)[None, :]
    d["dist"] = np.concatenate([np.where(b <= a, b - a, -1e30), np.where(k2 <= a + 128, k2 - a - 128.0, -1e30)], 1)
    slope = 2.0 ** -np.arange(1.0, 9.0)
    cpos = np.arange(8) * 32 + 31
    q = np.stack([p, p + 128], 1)
    dc = q[:, :, None] - cpos
    d["cmpb"] = np.where(dc[:, :, None, :] >= 0, -slope[None, None, :, None] * dc[:, :, None, :], -1e30)
    d["cmpv"] = dc >= 0
    hc = np.arange(64)[:, None]
    bd = np.zeros((128, 512))
    bd[:64] = (hc // 8) == (np.arange(512)[None, :] // 64)
    d["bd"] = bd
    es = np.zeros((128, 64))
    es[:8] = (hc.T % 8) == np.arange(8)[:, None]
    d["esel"] = es
    count = np.array([16 // (j + 1) for j in range(16)])
    first = np.cumsum(count) - count
    d["pst"] = np.broadcast_to(first[None, :], (128, 16))
    d["plen"] = np.broadcast_to(np.diff(first, prepend=0)[None, :], (128, 16))
    d["sel"] = (a % 32) == np.arange(16)[None, :]
    d["iota"] = np.broadcast_to(b, (128, 128))
    return np.concatenate([np.asarray(d[k], np.float32).reshape(128, -1) for k in NC_CONST], 1)


def layout(i):
    import numpy as np
    f = {k: np.asarray(v) for k, v in i.items()}

    def pc(v):
        return v.reshape(128, -1)

    def tile(v):
        return np.broadcast_to(v.reshape(1, -1), (128, v.size))

    small = dict(g_attn=pc(f["attn_norm_g"][0]),
                 g_mix=pc(np.concatenate([f["sb_out_norm_g"][0], f["sg_out_norm_g"][0]])),
                 g_ffn=pc(f["ffn_norm_g"][0]), g_nmix=pc(f["norm_mix_2"][0]), g_sub=pc(f["diff_subln_2"][0]),
                 g_cross=pc(f["norm_cross_2"][0]), g_mem=pc(f["norm_mem_2"][0]), g_peer=pc(f["norm_ffn_2"][0]),
                 bsp=f["b_spatial"][0].T, pos=np.concatenate([f["nsa_cmp_pos_2"][0].T] * 2, 0),
                 lam=tile(f["diff_lambda_2"][0]),
                 rb=tile(np.concatenate([f["b_router_group"][0], f["b_router_expert"][0].reshape(-1)])))
    rows = dict(sg=tile(f["sg_norm_g"][0]), fin1=tile(f["final_norm_g"]))

    def units(w):
        return np.ascontiguousarray(w.reshape(128, 8, -1, 512).transpose(2, 0, 1, 3)).reshape(-1, 128, 4096)

    w2 = f["w_in_2"][0]
    qa, ka, va, qb, kv, gb, ga, gbb = np.split(w2, np.cumsum([512, 512, 512, 512, 768, 24, 1024]), axis=1)
    qb = qb.reshape(1024, 2, 4, 64).transpose(0, 2, 1, 3).reshape(1024, 512)
    kv = kv.reshape(1024, 6, 2, 64)
    kva = np.concatenate([kv[:, 0, 0], kv[:, 1, 0], kv[:, 0, 1], kv[:, 1, 1], kv[:, 2, 0], kv[:, 2, 1],
                          kv[:, 4, 0], kv[:, 4, 1]], 1)
    kvb = np.concatenate([kv[:, 3, 0], kv[:, 3, 1], kv[:, 5, 0], kv[:, 5, 1], gb, np.zeros((1024, 232), w2.dtype)], 1)
    w_in2 = units(np.concatenate([qa, ka, va, qb, kva, kvb, ga, gbb], 1))
    wr = np.concatenate([f["w_router_group"][0], f["w_router_expert"][0].transpose(1, 0, 2).reshape(1024, 32)], 1)
    c1 = np.concatenate([f["nsa_ck_w1_2"][0].reshape(32, 64, 256), f["nsa_cv_w1_2"][0].reshape(32, 64, 256)], 1)
    c1 = c1.reshape(2, 16, 128, 256).transpose(0, 2, 1, 3).reshape(2, 128, 4096)
    c2 = np.stack([f["nsa_ck_w2_2"][0].reshape(2, 128, 64), f["nsa_cv_w2_2"][0].reshape(2, 128, 64)], 0)
    a = dict(
        x=f["x"][0], fin2=tile(f["norm_final_2"]), const=constants(), small=np.concatenate([small[k] for k in NC_SMALL], 1),
        rows=np.concatenate([rows[k] for k in NC_ROWS], 1),
        w_in=units(f["w_in"][0]), w_sp=f["w_spatial"][0].transpose(2, 0, 1).reshape(128, 1024), w_out=units(f["w_out"][0]),
        w_r=wr.reshape(128, 288), w_gate=f["w_gate"].reshape(32, 1024, 512), w_up=f["w_up"].reshape(32, 1024, 512),
        w_down=f["w_down"].reshape(32, 512, 1024), mem=f["mem_2"][0], w_in2=w_in2, ck1=c1,
        ck2=c2.transpose(2, 0, 1, 3).reshape(128, 256), w_a=f["w_branch_a_2"][0], w_b=f["w_branch_b_2"][0],
        w_out2=units(f["w_out_2"][0]), w_cq=units(f["w_cross_q_2"][0]), w_ckv=units(f["w_cross_kv_2"][0]),
        w_co=f["w_cross_o_2"][0], w_pq=units(f["peer_wq_2"][0]),
        subk=f["peer_subkeys_2"][0].transpose(3, 0, 1, 2).reshape(128, 2048),
        peer_u=f["peer_u_2"][0].reshape(128, 128, 128, 8).transpose(1, 2, 3, 0).reshape(128, 128, 1024),
        peer_v=f["peer_v_2"][0].reshape(128, 128, 1024),
    )
    return {k: np.ascontiguousarray(v) for k, v in a.items()}


def kernel(**inputs):
    import numpy as np
    import concourse.bacc as bacc
    from concourse.bass_utils import run_bass_kernel_spmd

    nc = bacc.Bacc("TRN2", target_bir_lowering=False, num_devices=1)
    arrays, args = {}, {}
    for name, a in layout(inputs).items():
        arrays[f"in_{name}"] = a
        args[name] = nc.dram_tensor(f"in_{name}", a.shape, mybir.dt.from_np(a.dtype), kind="ExternalInput").ap()
    args["out"] = nc.dram_tensor("out_0", (256, D), F32, kind="ExternalOutput").ap()
    program(nc, **args)
    r = run_bass_kernel_spmd(nc, [arrays], core_ids=[0])
    return np.asarray(r.results[0]["out_0"]).reshape(1, 256, D)
```
